# Optimizing a Trainium2 kernel written in Bass

```python
import jax, jax.numpy as jnp
from jax import lax
import numpy as np

D_MODEL = 1024
BATCH = 1
SEQ = 256
DEPTH = 1

CHUNK = 64
EPS = 1e-6
GLA_HEADS = 4
GLA_DK = D_MODEL // 2
GLA_DV = D_MODEL
GLA_HK = GLA_DK // GLA_HEADS
GLA_HV = GLA_DV // GLA_HEADS
GLA_GATE_RANK = 16
GLA_GATE_NORMALIZER = 16.0
SSM_EXPAND = 2
SSM_DINNER = SSM_EXPAND * D_MODEL
SSM_HEADDIM = 64
SSM_HEADS = SSM_DINNER // SSM_HEADDIM
SSM_GROUPS = 8
SSM_HPG = SSM_HEADS // SSM_GROUPS
SSM_DSTATE = 128
SSM_CONV = 4
SSM_CONV_DIM = SSM_DINNER + 2 * SSM_GROUPS * SSM_DSTATE
MOE_GROUPS = 4
MOE_EPG = 8
MOE_EXPERTS = MOE_GROUPS * MOE_EPG
MOE_TOPK = 2
MOE_DFF = 256
N_BRANCH = 2
N_MOD = 6
IN_SIZES = (GLA_DK, GLA_DK, GLA_DV, GLA_DV, GLA_GATE_RANK, SSM_DINNER, SSM_CONV_DIM, SSM_HEADS, N_BRANCH * D_MODEL)
D_IN = GLA_DK + GLA_DK + GLA_DV + GLA_DV + GLA_GATE_RANK + SSM_DINNER + SSM_CONV_DIM + SSM_HEADS + N_BRANCH * D_MODEL

kernel_name = 'hybrid_gla_ssd_hmoe_adaln'

def split_cols(t, sizes):
    out, start = [], 0
    for s in sizes:
        out.append(t[..., start:start + s])
        start += s
    return out

def rms_norm(x, g):
    xf = x.astype(jnp.float32)
    y = xf * lax.rsqrt(jnp.mean(xf * xf, axis=-1, keepdims=True) + EPS)
    return y.astype(x.dtype) * g

def causal_depthwise_conv(u, w, b):
    out = lax.conv_general_dilated(u, w[:, None, :].astype(u.dtype), window_strides=(1,),
                                   padding=[(SSM_CONV - 1, 0)],
                                   dimension_numbers=('NWC', 'WIO', 'NWC'),
                                   feature_group_count=u.shape[-1])
    return out + b

def chunk_recurrence(decay, update):
    def step(s, inp):
        a, u = inp
        return a * s + u, s
    s0 = jnp.zeros_like(update[0])
    _, prev = lax.scan(step, s0, (decay, update))
    return prev

def gla_mixer(q, k, v, g, gk_low, w_gk2, b_gk, norm_g):
    bsz, s = q.shape[0], q.shape[1]
    nc = s // CHUNK
    gk = jax.nn.log_sigmoid((gk_low @ w_gk2 + b_gk).astype(jnp.float32)) / GLA_GATE_NORMALIZER
    q = q.reshape(bsz, nc, CHUNK, GLA_HEADS, GLA_HK) * (GLA_HK ** -0.5)
    k = k.reshape(bsz, nc, CHUNK, GLA_HEADS, GLA_HK)
    v = v.reshape(bsz, nc, CHUNK, GLA_HEADS, GLA_HV)
    gk = gk.reshape(bsz, nc, CHUNK, GLA_HEADS, GLA_HK)
    g_cum = jnp.cumsum(gk, axis=2)
    g_end = g_cum[:, :, -1]
    k_dec = k * jnp.exp(g_end[:, :, None] - g_cum)
    update = jnp.einsum('bclhk,bclhv->cbhkv', k_dec, v)
    decay = jnp.exp(g_end).transpose(1, 0, 2, 3)[..., None]
    prev = chunk_recurrence(decay, update)
    state = decay * prev + update
    o = jnp.einsum('bclhk,cbhkv->bclhv', q, state)
    o = rms_norm(o, norm_g)
    return o.reshape(bsz, s, GLA_DV) * jax.nn.silu(g)

def ssd_mixer(z, xbc, dt_raw, conv_w, conv_b, dt_bias, a_log, d_skip, norm_g):
    bsz, s = z.shape[0], z.shape[1]
    nc = s // CHUNK
    xbc = jax.nn.silu(causal_depthwise_conv(xbc, conv_w, conv_b))
    xs, b_m, c_m = split_cols(xbc, (SSM_DINNER, SSM_GROUPS * SSM_DSTATE, SSM_GROUPS * SSM_DSTATE))
    dt = jax.nn.softplus(dt_raw.astype(jnp.float32) + dt_bias)
    a = -jnp.exp(a_log.astype(jnp.float32))
    d_a = (dt * a).reshape(bsz, nc, CHUNK, SSM_GROUPS, SSM_HPG)
    dt = dt.reshape(bsz, nc, CHUNK, SSM_GROUPS, SSM_HPG)
    xh = xs.reshape(bsz, nc, CHUNK, SSM_GROUPS, SSM_HPG, SSM_HEADDIM)
    b_m = b_m.reshape(bsz, nc, CHUNK, SSM_GROUPS, SSM_DSTATE)
    c_m = c_m.reshape(bsz, nc, CHUNK, SSM_GROUPS, SSM_DSTATE)
    a_cum = jnp.cumsum(d_a, axis=2)
    xdt = xh * dt[..., None]
    seg = a_cum[:, :, :, None] - a_cum[:, :, None, :]
    l_mask = jnp.exp(-jnp.abs(seg))
    cb = jnp.einsum('bctgn,bcsgn->bctsg', c_m, b_m)
    y_diag = jnp.einsum('bctsg,bctsgr,bcsgrp->bctgrp', cb, l_mask, xdt)
    dec_end = jnp.exp(a_cum[:, :, -1:] - a_cum)
    update = jnp.einsum('bclgn,bclgr,bclgrp->cbgrpn', b_m, dec_end, xdt)
    chunk_decay = jnp.exp(a_cum[:, :, -1]).transpose(1, 0, 2, 3)[..., None, None]
    prev = chunk_recurrence(chunk_decay, update)
    y_off = jnp.einsum('bctgn,cbgrpn,bctgr->bctgrp', c_m, prev, jnp.exp(a_cum))
    y = y_diag + y_off + xh * d_skip.reshape(SSM_GROUPS, SSM_HPG)[..., None]
    y = y.reshape(bsz, s, SSM_DINNER) * jax.nn.silu(z)
    gsz = SSM_DINNER // SSM_GROUPS
    y = rms_norm(y.reshape(bsz, s, SSM_GROUPS, gsz), norm_g.reshape(SSM_GROUPS, gsz))
    return y.reshape(bsz, s, SSM_DINNER)

def hier_moe(h, w_rg, b_rg, w_re, b_re, w1, w3, w2):
    bsz, s, d = h.shape
    t = bsz * s
    hf = h.reshape(t, d)
    group_prob = jax.nn.softmax((hf @ w_rg + b_rg).astype(jnp.float32), axis=-1)
    g_w, g_idx = lax.top_k(group_prob, 1)
    expert_logits = (hf @ w_re + b_re).astype(jnp.float32).reshape(t, MOE_GROUPS, MOE_EPG)
    sel_logits = jnp.einsum('tg,tge->te', jax.nn.one_hot(g_idx[:, 0], MOE_GROUPS, dtype=jnp.float32), expert_logits)
    e_prob = jax.nn.softmax(sel_logits, axis=-1)
    e_w, e_idx = lax.top_k(e_prob, MOE_TOPK)
    e_w = e_w / jnp.sum(e_w, axis=-1, keepdims=True)
    weights = g_w * e_w
    global_idx = g_idx * MOE_EPG + e_idx
    combine = jnp.sum(jax.nn.one_hot(global_idx, MOE_EXPERTS, dtype=jnp.float32) * weights[..., None], axis=1)
    combine = combine.reshape(t, MOE_GROUPS, MOE_EPG).astype(h.dtype)
    out = jnp.zeros((t, d), dtype=h.dtype)
    for gi in range(MOE_GROUPS):
        hid = jax.nn.silu(jnp.einsum('td,edf->tef', hf, w1[gi])) * jnp.einsum('td,edf->tef', hf, w3[gi])
        out = out + jnp.einsum('tef,efd->td', hid * combine[:, gi, :, None], w2[gi])
    return out.reshape(bsz, s, d)

def setup_inputs(seed: int = 0) -> dict:
    key = jax.random.key(seed)
    ks = jax.random.split(key, 32)
    f32 = jnp.float32
    nrm = lambda k, shape, scale: jax.random.normal(k, shape, f32) * scale
    dt0 = jnp.exp(jax.random.uniform(ks[10], (DEPTH, SSM_HEADS), f32, np.log(1e-3), np.log(1e-1)))
    return {
        'x': nrm(ks[0], (BATCH, SEQ, D_MODEL), 1.0),
        'c': nrm(ks[1], (BATCH, D_MODEL), 1.0),
        'ada_w': nrm(ks[2], (DEPTH, D_MODEL, N_MOD * D_MODEL), D_MODEL ** -0.5),
        'ada_b': nrm(ks[3], (DEPTH, N_MOD * D_MODEL), 0.02),
        'norm1_g': 1.0 + nrm(ks[4], (DEPTH, D_MODEL), 0.02),
        'w_in': nrm(ks[5], (DEPTH, D_MODEL, D_IN), D_MODEL ** -0.5),
        'gla_w_gk2': nrm(ks[6], (DEPTH, GLA_GATE_RANK, GLA_DK), GLA_GATE_RANK ** -0.5),
        'gla_b_gk': nrm(ks[7], (DEPTH, GLA_DK), 0.1),
        'gla_norm_g': 1.0 + nrm(ks[8], (DEPTH, GLA_HV), 0.02),
        'conv_w': nrm(ks[9], (DEPTH, SSM_CONV, SSM_CONV_DIM), SSM_CONV ** -0.5),
        'conv_b': nrm(ks[11], (DEPTH, SSM_CONV_DIM), 0.02),
        'dt_bias': dt0 + jnp.log(-jnp.expm1(-dt0)),
        'a_log': jnp.log(jax.random.uniform(ks[12], (DEPTH, SSM_HEADS), f32, 1.0, 16.0)),
        'd_skip': 1.0 + nrm(ks[13], (DEPTH, SSM_HEADS), 0.02),
        'ssm_norm_g': 1.0 + nrm(ks[14], (DEPTH, SSM_DINNER), 0.02),
        'w_oa': nrm(ks[15], (DEPTH, GLA_DV, D_MODEL), GLA_DV ** -0.5),
        'w_ob': nrm(ks[16], (DEPTH, SSM_DINNER, D_MODEL), SSM_DINNER ** -0.5),
        'w_out': nrm(ks[17], (DEPTH, D_MODEL, D_MODEL), D_MODEL ** -0.5),
        'norm2_g': 1.0 + nrm(ks[18], (DEPTH, D_MODEL), 0.02),
        'router_group_w': nrm(ks[19], (DEPTH, D_MODEL, MOE_GROUPS), D_MODEL ** -0.5),
        'router_group_b': nrm(ks[20], (DEPTH, MOE_GROUPS), 0.01),
        'router_expert_w': nrm(ks[21], (DEPTH, D_MODEL, MOE_EXPERTS), D_MODEL ** -0.5),
        'router_expert_b': nrm(ks[22], (DEPTH, MOE_EXPERTS), 0.01),
        'expert_w1': nrm(ks[23], (DEPTH, MOE_GROUPS, MOE_EPG, D_MODEL, MOE_DFF), D_MODEL ** -0.5),
        'expert_w3': nrm(ks[24], (DEPTH, MOE_GROUPS, MOE_EPG, D_MODEL, MOE_DFF), D_MODEL ** -0.5),
        'expert_w2': nrm(ks[25], (DEPTH, MOE_GROUPS, MOE_EPG, MOE_DFF, D_MODEL), MOE_DFF ** -0.5),
        'final_norm_g': 1.0 + nrm(ks[26], (D_MODEL,), 0.02),
    }

def reference(x, c, ada_w, ada_b, norm1_g, w_in, gla_w_gk2, gla_b_gk, gla_norm_g, conv_w, conv_b,
              dt_bias, a_log, d_skip, ssm_norm_g, w_oa, w_ob, w_out, norm2_g, router_group_w,
              router_group_b, router_expert_w, router_expert_b, expert_w1, expert_w3, expert_w2,
              final_norm_g):
    c_act = jax.nn.silu(c)
    for l in range(DEPTH):
        mod = c_act @ ada_w[l] + ada_b[l]
        sh1, sc1, gt1, sh2, sc2, gt2 = [m[:, None, :] for m in jnp.split(mod, N_MOD, axis=-1)]
        h = rms_norm(x, norm1_g[l]) * (1.0 + sc1) + sh1
        proj = h @ w_in[l]
        q, k, v, g_out, gk_low, z, xbc, dt_raw, gates = split_cols(proj, IN_SIZES)
        o_a = gla_mixer(q, k, v, g_out, gk_low, gla_w_gk2[l], gla_b_gk[l], gla_norm_g[l])
        o_b = ssd_mixer(z, xbc, dt_raw, conv_w[l], conv_b[l], dt_bias[l], a_log[l], d_skip[l], ssm_norm_g[l])
        gate_a, gate_b = jnp.split(jax.nn.sigmoid(gates), N_BRANCH, axis=-1)
        merged = gate_a * (o_a @ w_oa[l]) + gate_b * (o_b @ w_ob[l])
        x = x + gt1 * (merged @ w_out[l])
        h = rms_norm(x, norm2_g[l]) * (1.0 + sc2) + sh2
        x = x + gt2 * hier_moe(h, router_group_w[l], router_group_b[l], router_expert_w[l],
                               router_expert_b[l], expert_w1[l], expert_w3[l], expert_w2[l])
    return rms_norm(x, final_norm_g)


_drawn_inputs = setup_inputs


def setup_inputs(seed=0):
    import zlib

    import numpy as np

    out = dict(_drawn_inputs(seed))
    spreads = {}
    factors = {'gla_norm_g': 14.199,
     'conv_b': 3.217,
     'd_skip': 24.699,
     'ssm_norm_g': 11.533,
     'router_group_b': 23.032,
     'router_expert_b': 22.048,
     'final_norm_g': 7.64,
     'norm2_g': 2.838}
    for name, (base, spread) in spreads.items():
        noise = np.random.default_rng([zlib.crc32(name.encode()), seed]).standard_normal(out[name].shape)
        drawn = base * np.exp(spread * noise) if base else spread * noise
        out[name] = __import__('jax').numpy.asarray(drawn.astype(out[name].dtype))
    for name, factor in factors.items():
        out[name] = (out[name] * factor).astype(out[name].dtype)
    return out
```

```python
from contextlib import ExitStack

import concourse.bass as bass
from concourse import mybir

F32, I32 = mybir.dt.float32, mybir.dt.int32
ALU = mybir.AluOpType
ACT = mybir.ActivationFunctionType
AX_X = mybir.AxisListType.X

P = 128
T = 256
TT = T // P
D = 1024
KD = D // P
CH = 64
NC = T // CH
EPS = 1e-6
GH, HK, HV, RANK = 4, 128, 256, 16
SH, SP_, SG, NS = 32, 64, 8, 128
DI = SH * SP_
CONV_CH, TAPS = DI + 2 * SG * NS, 4
E, EG, FF = 32, 8, 256
SLOTS, CW = 4, 512
W2S = 4

OFF = {}
_at = 0
for _n, _w in (("q", 512), ("k", 512), ("v", 1024), ("g", 1024), ("gk", RANK), ("z", DI), ("xbc", CONV_CH),
               ("dt", SH), ("gate", 2 * D)):
    OFF[_n] = _at
    _at += _w

COL, _at = {"conv_w": 0}, 128
for _n, _w in (("conv_b", 32), ("ssm_g", 16), ("norm1", 8), ("norm2", 8), ("ada_b", 48), ("c", 8), ("gla_g", 2)):
    COL[_n] = _at
    _at += _w
NCOL = _at

CHUNKS = ([("ada", i) for i in range(4)] + [("xbc", i) for i in range(8)] + [("k", 0), ("q", 0), ("v", 0), ("v", 1)]
          + [("g", i) for i in range(2)] + [("z", i) for i in range(4)] + [("gate", i) for i in range(4)]
          + [("ada", i) for i in range(4, 12)] + [("oa", i) for i in range(2)] + [("ob", i) for i in range(4)]
          + [("out", i) for i in range(2)])
CHUNK_AT = {c: i for i, c in enumerate(CHUNKS)}
UNITS = [c for c in CHUNKS if c[0] not in ("ada", "ob", "oa", "out")] + [("oa", 0), ("oa", 1), ("ob", 0), ("ob", 1),
                                                                        ("out", 0), ("out", 1)]
MIX = ["cols", "modA"] + [("xT", i) for i in range(4)] + ["small"]
for _i in range(1, 7):
    MIX += [("tr", _i - 1, 0), ("tr", _i - 1, 1)]
MIX += ["acum", ("gklin", 0), ("gklin", 1), ("gsuf", 0), ("gsuf", 1), "gdec"]
MIX += [("arow", 0, j) for j in range(4)] + [("arow", 1, j) for j in range(4)] + [("cb", 0), ("cb", 1)]
MIX += [("gU", c, hp) for c in range(NC) for hp in range(2)] + [("gO", t, hp) for t in range(TT) for hp in range(2)]
for _j in range(4):
    MIX += [("U", _j, c) for c in range(3)] + [("off", _j, 0), ("off", _j, 1), ("diag", _j, 0), ("diag", _j, 1)]
MIX += [("oaT", i) for i in range(4)] + [("obT", i) for i in range(8)]
MIX += ["modB"] + [("gtb", w, h) for w in range(2) for h in range(2)]
MIX += [("x2T", i) for i in range(4)] + ["router"]
MIX_AT = {n: i for i, n in enumerate(MIX)}


def trunk(nc, x, c, ada_w, ada_b, norm1_g, w_in, gla_w_gk2, gla_b_gk, gla_norm_g, conv_w, conv_b, dt_bias, a_log,
          d_skip, ssm_norm_g, w_oa, w_ob, w_out, norm2_g, router_group_w, router_group_b, router_expert_w,
          router_expert_b, expert_w1, expert_w3, expert_w2, final_norm_g, out):
    with ExitStack() as ctx:
        def sb(name, *dims):
            return ctx.enter_context(nc.sbuf_tensor(name, [P, *dims], F32))

        def sem(name):
            return ctx.enter_context(nc.semaphore(name))

        ring = sb("ring", SLOTS, KD, CW)
        x_sb = sb("x_sb", TT, D)
        hT = sb("hT", KD, T)
        r_k = sb("r_k", 1024)
        r_q = sb("r_q", 1024)
        r_v = sb("r_v", 2048)
        g_sb = sb("g_sb", TT, D)
        r_z = sb("r_z", 4096)
        r_xs = sb("r_xs", 4096)
        r_bt = sb("r_bt", 2048)
        r_ct = sb("r_ct", 2048)
        r_btm = sb("r_btm", 2048)
        r_lm = sb("r_lm", 4096)
        r_st = sb("r_st", 4096)
        r_pv = sb("r_pv", 3, 512)

        def view(region, pattern, **kw):
            return region[:].rearrange(pattern, **kw)

        k_tm = view(r_k, "p (t d) -> p t d", t=TT)
        qT = view(r_q, "p (h t) -> p h t", h=GH)
        v_tm = view(r_v, "p (t d) -> p t d", t=TT)
        z_tm = view(r_z, "p (t d) -> p t d", t=TT)
        xn = r_z[:, 0:2048].rearrange("p (t d) -> p t d", t=TT)
        xs = view(r_xs, "p (t d) -> p t d", t=TT)
        BT = view(r_bt, "p (g t) -> p g t", g=SG)
        CT = view(r_ct, "p (g t) -> p g t", g=SG)
        Btm = view(r_btm, "p (t d) -> p t d", t=TT)
        u_cv = r_lm[:, 0:1024].rearrange("p (b a t) -> p b a t", b=2, a=2)
        acc_cv = r_lm[:, 1024:2048].rearrange("p (b a t) -> p b a t", b=2, a=2)
        xsT = r_lm[:, 2048:4096].rearrange("p (b a t) -> p b a t", b=2, a=4)
        M = view(r_lm, "p (t h s) -> p t h s", t=TT, h=SH)
        rhsL = r_st[:, 0:2048].rearrange("p (h s) -> p h s", h=SH)
        gla_st = view(r_st, "p (c h v) -> p c h v", c=NC, h=GH)
        gateT = view(r_st, "p (m t) -> p m t", m=2 * KD)
        gk_abs = r_pv[:, 0, :]
        gk_sp = r_pv[:, 1, :]
        gsuf_e = r_pv[:, 2, :]
        xdt = view(r_v, "p (b t d) -> p b t d", b=2, t=TT)
        xdd = view(r_bt, "p (b t d) -> p b t d", b=2, t=TT)
        y_tmp = view(r_k, "p (b d) -> p b d", b=2)
        y_off = view(r_q, "p (b d) -> p b d", b=2)
        oaT = view(r_btm, "p (m t) -> p m t", m=KD)
        obT = view(r_lm, "p (m t) -> p m t", m=2 * KD)
        mT = view(r_bt, "p (m t) -> p m t", m=KD)
        gt1b = view(r_k, "p d -> p d")
        gt2b = view(r_q, "p d -> p d")
        diag = r_pv[:, 0:2, :]
        m_tmp = r_pv[:, 2, :]
        x2n = view(r_v, "p (t d) -> p t d", t=TT)
        w2z = view(r_z, "p (b k d) -> p b k d", b=2, k=2)
        w2x = view(r_xs, "p (b k d) -> p b k d", b=2, k=2)
        w2_slot = [w2z[:, 0], w2z[:, 1], w2x[:, 0], w2x[:, 1]]
        fng = r_ct[:, 0:1024]
        hid_s, hid_p, hid_w = r_lm[:, 0:512], r_lm[:, 512:1024], r_lm[:, 1024:1024 + T]
        moe_dg = r_lm[:, 1536:2048].rearrange("p (b t q) -> p b t q", b=2, t=TT) if False else r_lm[:, 3072:3584].rearrange(
            "p (b t q) -> p b t q", b=2, t=TT)
        hid = r_lm[:, 2048:3072].rearrange("p (b f t) -> p b f t", b=2, f=2)

        stackA, stackB = r_z[:, 2048:2176], r_z[:, 2176:2304]
        wsm = r_z[:, 2304:2304 + KD * (RANK + SH)].rearrange("p (k n) -> p k n", k=KD)
        gkT, wgk2 = r_z[0:RANK + 1, 2688:2688 + T], r_z[0:RANK + 1, 2944:2944 + 512]
        gk_ls = g_sb[:, 1]
        gk_ls = gk_ls.rearrange("p (t d) -> p t d", t=TT)
        late = {}
        at = 0
        for name, dims in (("wr", (KD, 36)), ("rb", (36,)), ("lg", (TT, 36)), ("rt", (24, TT, 8)), ("rt4", (TT, 4, EG)),
                           ("comb", (TT, E))):
            size = 1
            for d in dims:
                size *= d
            late[name] = r_btm[:, at:at + size]
            if len(dims) > 1:
                letters = "abc"[:len(dims)]
                late[name] = late[name].rearrange("p (" + " ".join(letters) + ") -> p " + " ".join(letters),
                                                  **dict(zip(letters, dims)))
            at += size
        wr, rb, lg, rt, rt4, comb = (late[k] for k in ("wr", "rb", "lg", "rt", "rt4", "comb"))
        sq = sb("sq", 256)
        newton = sb("newton", 3, 16)
        sq_d = r_ct[:, 1024:2048]
        ident = sb("ident", P)
        same = sb("same", P)
        upto = sb("upto", P)
        after = sb("after", P)
        upto1 = sb("upto1", CH)
        inch = sb("inch", 2, P)
        ones = sb("ones", P)
        w_down = sb("w_down", 8)
        cols = sb("cols", NCOL)
        rows = sb("rows", 3, SH)
        cact = sb("cact", KD)
        mod = sb("mod", 48)
        st = sb("st", 16)
        dtb = sb("dtb", 5, TT, SH)
        dt, dA, acum, eacum, dend = (dtb[:, i] for i in range(5))
        dt_abs = sb("dt_abs", TT, SH)
        cdec = sb("cdec", NC, SH)
        gdec = sb("gdec", GH, NC)
        gss = sb("gss", 2, TT, GH)
        sss = sb("sss", 2, TT, SG)

        ps = [ctx.enter_context(nc.psum_tensor(f"ps{i}", [P, 512], F32)) for i in range(8)]

        slot_full = [sem(f"slot_full{i}") for i in range(SLOTS)]
        slot_free = [sem(f"slot_free{i}") for i in range(SLOTS)]
        bank_full = [sem(f"bank_full{i}") for i in range(8)]
        bank_free = [sem(f"bank_free{i}") for i in range(8)]
        w2_full = [sem(f"w2_full{i}") for i in range(W2S)]
        w2_free = [sem(f"w2_free{i}") for i in range(W2S)]
        s_stack, s_x, s_small, s_rows, s_wr, s_fng = (sem(n) for n in ("s_stack", "s_x", "s_small", "s_rows", "s_wr", "s_fng"))
        s_const = sem("s_const")
        s_pool = sem("s_pool_chain")
        s_dve = sem("s_dve_chain")
        s_act = sem("s_act_chain")
        (x_sq, xn_done, cols_done, cact_done, hT_done, sm_done, a_exp, dt_sp, dA_done, ones_done, conv_step,
         conv_done, silu_done, gk_in, gk_l, gk_done, gsuf_done, kdec_done, gdec_done, ac_done, eac_done,
         rhs_done, seg_unused, L_done, M_done, gO_sq, oa_done, xdt_done, xdd_done, skip_done, y_done, y_sq,
         ob_done, mod_done, diag_done, x2_done, x2_sq, x2n_done, rt_in, rt_e, rt_in2, rt_e2, comb_done,
         combT_done, hs_done, hp_done, hw_done, dg_done, hid_done, y_moe, x3_sq, fin_done, out_done, ada_used, moe_h, ob_used,
         y_evac,) = (sem(n) for n in (
            "x_sq xn_done cols_done cact_done hT_done sm_done a_exp dt_sp dA_done ones_done conv_step "
            "conv_done silu_done gk_in gk_l gk_done gsuf_done kdec_done gdec_done ac_done eac_done rhs_done "
            "seg_unused L_done M_done gO_sq oa_done xdt_done xdd_done skip_done y_done y_sq ob_done mod_done "
            "diag_done x2_done x2_sq x2n_done rt_in rt_e rt_in2 rt_e2 comb_done combT_done hs_done hp_done hw_done dg_done "
            "hid_done y_moe x3_sq fin_done out_done ada_used moe_h ob_used y_evac ").split())

        def mix(name):
            n = MIX_AT[name]
            return ps[4 + n % 4], 4 + n % 4, n // 4

        def mix_wait(eng, name):
            bank, b, turn = mix(name)
            eng.wait_ge(bank_full[b], turn + 1)
            return bank

        def mix_used(name):
            return bank_free[mix(name)[1]]

        def mix_taken(eng, name):
            _, b, turn = mix(name)
            eng.wait_ge(bank_free[b], turn + 1)

        def unit(name, half):
            n = 2 * UNITS.index(name) + half
            return ps[n % 4], n % 4, n // 4

        def unit_wait(eng, name, half):
            bank, b, turn = unit(name, half)
            eng.wait_ge(bank_full[b], turn + 1)
            return bank

        def unit_used(name, half):
            return bank_free[unit(name, half)[1]]

        def unit_taken(eng, name, half):
            _, b, turn = unit(name, half)
            eng.wait_ge(bank_free[b], turn + 1)

        def chunk_used(eng, n):
            kind, i = CHUNKS[n]
            if kind == "ada":
                eng.wait_ge(ada_used, i + 1)
            elif kind == "ob" and i % 2 == 0:
                eng.wait_ge(ob_used, i // 2 + 1)
            else:
                unit_wait(eng, (kind, i // 2 if kind == "ob" else i), 1)

        def col(name, i=0, n=1):
            return cols[:, COL[name] + i:COL[name] + i + n]

        def heads(ap):
            return ap.rearrange("p (h q) -> p h q", q=SP_)

        def over(ap, n):
            return ap.unsqueeze(len(ap.shape)).to_broadcast([*ap.shape, n])

        w_in2, ada2 = w_in[0], ada_w[0]

        def chunk_src(kind, i):
            w, at = {"ada": (ada2, 0), "oa": (w_oa[0], 0), "out": (w_out[0], 0)}.get(kind, (w_in2, OFF.get(kind, 0)))
            if kind == "ob":
                return w_ob[0, (i % 2) * D:(i % 2 + 1) * D, (i // 2) * CW:(i // 2 + 1) * CW].rearrange(
                    "(k p) n -> p k n", p=P)
            return w[:, at + i * CW:at + (i + 1) * CW].rearrange("(k p) n -> p k n", p=P)

        block = ctx.enter_context(nc.Block())

        @block.sync
        def _(sp):
            rowsA = conv_w[0].rearrange("w (t p) -> (w t) p", p=P)
            sp.dma_start(stackA, rowsA).then_inc(s_stack, 16)
            at = 0
            for v, n in ((conv_b, 32), (ssm_norm_g, 16), (norm1_g, 8), (norm2_g, 8), (ada_b, 48), (c, 8), (gla_norm_g, 2)):
                sp.dma_start(stackB[at:at + n, :], v[0].rearrange("(t p) -> t p", p=P)).then_inc(s_stack, 16)
                at += n
            sp.dma_start(x_sb[:], x[0].rearrange("(t p) d -> p t d", p=P)).then_inc(s_x, 16)
            sp.dma_start(wsm[:, :, 0:RANK], w_in2[:, OFF["gk"]:OFF["gk"] + RANK].rearrange("(k p) n -> p k n", p=P)
                         ).then_inc(s_small, 16)
            sp.dma_start(wsm[:, :, RANK:], w_in2[:, OFF["dt"]:OFF["dt"] + SH].rearrange("(k p) n -> p k n", p=P)
                         ).then_inc(s_small, 16)
            sp.dma_start(wgk2[0:RANK, :], gla_w_gk2[0]).then_inc(s_small, 16)
            sp.dma_start(wgk2[RANK:RANK + 1, :], gla_b_gk).then_inc(s_small, 16)
            for i, v in enumerate((dt_bias, a_log, d_skip)):
                sp.dma_start(rows[:, i, :], v[0].partition_broadcast(P)).then_inc(s_rows, 16)
            for i, (kind, n) in enumerate(CHUNKS):
                s = i % SLOTS
                if i >= SLOTS:
                    chunk_used(sp, i - SLOTS)
                sp.dma_start(ring[:, s], chunk_src(kind, n)).then_inc(slot_full[s], 16)
                if (kind, n) == ("out", 1):
                    for h in range(2):
                        unit_taken(sp, ("oa", 1), h)
                    sp.dma_start(wr[:, :, 0:4], router_group_w[0].rearrange("(k p) n -> p k n", p=P)).then_inc(s_wr, 16)
                    sp.dma_start(wr[:, :, 4:36], router_expert_w[0].rearrange("(k p) n -> p k n", p=P)).then_inc(s_wr, 16)
                    sp.dma_start(rb[:, 0:4], router_group_b[0].partition_broadcast(P)).then_inc(s_wr, 16)
                    sp.dma_start(rb[:, 4:36], router_expert_b[0].partition_broadcast(P)).then_inc(s_wr, 16)
            base = len(CHUNKS)
            w1v = expert_w1[0].rearrange("g e (k p) f -> (g e) p k f", p=P)
            w3v = expert_w3[0].rearrange("g e (k p) f -> (g e) p k f", p=P)
            w2v = expert_w2[0].rearrange("g e (k p) d -> (g e) p k d", p=P)
            for i in range(8):
                mix_taken(sp, ("obT", i))

            def expert(e, u):
                s = (base + u) % SLOTS
                sp.dma_start(ring[:, s, :, 0:FF], w1v[e]).then_inc(slot_full[s], 16)
                sp.dma_start(ring[:, s, :, FF:2 * FF], w3v[e]).then_inc(slot_full[s], 16)
                sp.dma_start(w2_slot[u], w2v[e]).then_inc(w2_full[u], 16)

            for u in range(4):
                chunk_used(sp, base - SLOTS + u)
                expert(u, u)
            with sp.Fori(1, E // 4) as i:
                for u in range(4):
                    sp.wait_ge(slot_free[(base + u) % SLOTS], i)
                    sp.wait_ge(w2_free[u], i)
                    expert(i * 4 + u, u)
            for t in range(TT):
                sp.wait_ge(fin_done, t + 1)
                sp.dma_start(out[0, t * P:(t + 1) * P, :], x_sb[:, t]).then_inc(out_done, 16)
            sp.wait_ge(out_done, 16 * TT)

        @block.gpsimd
        def _(pool):
            n = [0]

            def link(ins):
                n[0] += 1
                ins.then_inc(s_pool, 1)
                pool.wait_ge(s_pool, n[0])

            nc.gpsimd.memset(ones[:], 1.0)
            nc.gpsimd.memset(ident[:], 0.0)
            nc.gpsimd.memset(inch[:], 1.0)
            link(nc.gpsimd.memset(same[:], 1.0))
            link(nc.gpsimd.affine_select(out=ident[:], in_=ident[:], compare_op=ALU.not_equal, fill=1.0, base=0,
                                         pattern=[[-1, P]], channel_multiplier=1))
            for m, w in ((same[:].rearrange("p (j t) -> p j t", j=2), CH), (inch[:], P)):
                link(nc.gpsimd.affine_select(out=m, in_=m, compare_op=ALU.is_ge, fill=0.0, base=0,
                                             pattern=[[-CH, 2], [0, w]], channel_multiplier=1))
                link(nc.gpsimd.affine_select(out=m, in_=m, compare_op=ALU.is_ge, fill=0.0, base=CH - 1,
                                             pattern=[[CH, 2], [0, w]], channel_multiplier=-1))
            link(nc.gpsimd.affine_select(out=upto[:], in_=same[:], compare_op=ALU.is_ge, fill=0.0, base=0,
                                         pattern=[[1, P]], channel_multiplier=-1))
            link(nc.gpsimd.affine_select(out=after[:], in_=same[:], compare_op=ALU.is_ge, fill=0.0, base=-1,
                                         pattern=[[-1, P]], channel_multiplier=1))
            link(nc.gpsimd.iota(w_down[:], pattern=[[-1, 8]], base=8, channel_multiplier=0,
                                allow_small_or_imprecise_dtypes=True))
            nc.gpsimd.tensor_tensor(upto1[:], upto[:, 0:CH], upto[:, CH:P], ALU.add).then_inc(s_const, 1)
            pool.wait_ge(eac_done, 1)
            pool.wait_ge(s_rows, 48)
            for i in range(4):
                for t in range(TT):
                    mix_taken(pool, ("tr", i, t))
            for j in range(4):
                b = j % 2
                if j == 0:
                    for name in [("gU", NC - 1, 0), ("gU", NC - 1, 1), ("cb", 0), ("cb", 1)]:
                        mix_wait(pool, name)
                if j >= 2:
                    for t in range(TT):
                        mix_wait(pool, ("diag", j - 2, t))
                    mix_wait(pool, ("U", j - 2, 2))
                src = xs[:, :, j * 512:(j + 1) * 512]
                for t in range(TT):
                    h = slice(8 * j, 8 * j + 8)
                    link(nc.gpsimd.tensor_tensor(heads(xdt[:, b, t]), heads(src[:, t]), over(dt[:, t, h], SP_), ALU.mult))
                    nc.gpsimd.tensor_tensor(heads(xdd[:, b, t]), heads(xdt[:, b, t]), over(dend[:, t, h], SP_),
                                            ALU.mult).then_inc(xdd_done, 1)
                    nc.gpsimd.tensor_tensor(heads(src[:, t]), heads(src[:, t]), over(rows[:, 2, h], SP_),
                                            ALU.mult).then_inc(skip_done, 1)
            mix_wait(pool, ("off", 3, 1))
            pool.dma_start(fng, final_norm_g.partition_broadcast(P)).then_inc(s_fng, 16)

        @block.scalar
        def _(act):
            n = [0]

            def link(ins):
                n[0] += 1
                ins.then_inc(s_act, 1)
                act.wait_ge(s_act, n[0])

            act.wait_ge(s_x, 16)
            for t in range(TT):
                ins = nc.scalar.activation(hT[:].rearrange("p k t -> p (k t)")[:, t * D:(t + 1) * D], x_sb[:, t], ACT.Square,
                                           accum_out=st[:, t:t + 1])
                ins.then_inc(x_sq, 1)
            mix_taken(act, "cols")
            nc.scalar.activation(cact[:], col("c", 0, 8), ACT.Silu).then_inc(cact_done, 1)
            act.wait_ge(s_rows, 48)
            nc.scalar.activation(rows[:, 1, :], rows[:, 1, :], ACT.Exp).then_inc(a_exp, 1)
            act.wait_ge(sm_done, 1)
            link(nc.scalar.activation(dt_abs[:], dt_abs[:], ACT.Exp, scale=-1.0))
            nc.scalar.activation(dt_abs[:], dt_abs[:], ACT.Ln, bias=1.0).then_inc(dt_sp, 1)

            def silu_out(g):
                i, a = g // 2, 2 * (g % 2)
                if i < 4:
                    return xsT[:, i % 2, a:a + 2]
                return (BT if i < 6 else CT)[:, 4 * (i % 2) + a:4 * (i % 2) + a + 2]

            def conv_silu(g):
                act.wait_ge(conv_done, g + 1)
                if 4 <= g < 8:
                    mix_wait(act, ("tr", g // 2 - 2, 1))
                nc.scalar.activation(silu_out(g), acc_cv[:, g % 2], ACT.Silu).then_inc(silu_done, 1)

            for i in range(8):
                for half in range(2):
                    g = 2 * i + half
                    bank = unit_wait(act, ("xbc", i), half)
                    if g >= 2:
                        act.wait_ge(conv_done, g - 1)
                    nc.scalar.copy(u_cv[:, g % 2].rearrange("p a t -> p (a t)"), bank[:]).then_inc(
                        unit_used(("xbc", i), half), 1)
                    if g:
                        conv_silu(g - 1)
                if 1 <= i <= 6:
                    for t in range(TT):
                        bank = mix_wait(act, ("tr", i - 1, t))
                        dst = xs[:, t, (i - 1) * 512:i * 512] if i <= 4 else Btm[:, t, (i - 5) * 512:(i - 4) * 512]
                        nc.scalar.copy(dst, bank[:]).then_inc(mix_used(("tr", i - 1, t)), 1)
            conv_silu(15)

            for t in range(TT):
                bank = unit_wait(act, ("k", 0), t)
                nc.scalar.copy(k_tm[:, t], bank[:]).then_inc(unit_used(("k", 0), t), 1)
            for t in range(TT):
                act.wait_ge(gk_in, t + 1)
                link(nc.scalar.activation(gk_abs, gk_abs, ACT.Exp, scale=-1.0))
                nc.scalar.activation(gk_sp, gk_abs, ACT.Ln, bias=1.0).then_inc(gk_l, 1)
            mix_taken(act, "acum")
            nc.scalar.activation(dend, dend, ACT.Exp)
            nc.scalar.activation(eacum, acum, ACT.Exp)
            nc.scalar.activation(cdec[:], cdec[:], ACT.Exp).then_inc(eac_done, 1)
            for t in range(TT):
                bank = mix_wait(act, ("gsuf", t))
                if t:
                    act.wait_ge(kdec_done, t)
                nc.scalar.activation(gsuf_e, bank[:], ACT.Exp, scale=1.0 / 16).then_inc(mix_used(("gsuf", t)), 1)
            bank = mix_wait(act, "gdec")
            nc.scalar.activation(gdec[:].rearrange("p h c -> p (h c)"), bank[:, 0:GH * NC], ACT.Exp,
                                 scale=1.0 / 16).then_inc(mix_used("gdec"), 1)
            for h in range(2):
                bank = unit_wait(act, ("q", 0), h)
                nc.scalar.mul(qT[:, 2 * h:2 * h + 2].rearrange("p h t -> p (h t)"), bank[:], HK ** -0.5).then_inc(
                    unit_used(("q", 0), h), 1)
            for i in range(2):
                for t in range(TT):
                    bank = unit_wait(act, ("v", i), t)
                    nc.scalar.copy(v_tm[:, t, i * CW:(i + 1) * CW], bank[:]).then_inc(unit_used(("v", i), t), 1)
                for j in range(4):
                    mix_taken(act, ("arow", i, j))
                link(nc.scalar.activation(M[:, i], M[:, i], ACT.Abs))
                nc.scalar.activation(M[:, i], M[:, i], ACT.Exp, scale=-1.0).then_inc(L_done, 1)
            for i in range(2):
                for t in range(TT):
                    bank = unit_wait(act, ("g", i), t)
                    nc.scalar.activation(g_sb[:, t, i * CW:(i + 1) * CW], bank[:], ACT.Silu).then_inc(
                        unit_used(("g", i), t), 1)

            def gla_squares():
                for t in range(TT):
                    for hp in range(2):
                        bank = mix_wait(act, ("gO", t, hp))
                        for a in range(2):
                            if t or hp or a:
                                act.wait_ge(gO_sq, 4 * t + 2 * hp + a)
                            nc.scalar.activation(sq[:], bank[:, a * HV:(a + 1) * HV], ACT.Square,
                                                 accum_out=gss[:, 0, t, 2 * hp + a:2 * hp + a + 1]).then_inc(gO_sq, 1)

            def ssd_squares(j):
                for t in range(TT):
                    act.wait_ge(y_done, 2 * j + t + 1)
                    for a in range(2):
                        g, n_sq = 2 * j + a, 4 * j + 2 * t + a
                        if n_sq:
                            act.wait_ge(y_sq, n_sq)
                        else:
                            act.wait_ge(gO_sq, TT * GH)
                        nc.scalar.activation(sq[:], z_tm[:, t, g * 256:(g + 1) * 256], ACT.Square,
                                             accum_out=sss[:, 0, t, g:g + 1]).then_inc(y_sq, 1)

            for i in range(4):
                for t in range(TT):
                    bank = unit_wait(act, ("z", i), t)
                    nc.scalar.activation(z_tm[:, t, i * CW:(i + 1) * CW], bank[:], ACT.Silu).then_inc(
                        unit_used(("z", i), t), 1)
                if i == 0:
                    gla_squares()
                if i >= 2:
                    ssd_squares(i - 2)
            for i in range(4):
                for h in range(2):
                    bank = unit_wait(act, ("gate", i), h)
                    m = 4 * i + 2 * h
                    nc.scalar.activation(gateT[:, m:m + 2].rearrange("p m t -> p (m t)"), bank[:], ACT.Sigmoid).then_inc(
                        unit_used(("gate", i), h), 1)
                if i < 2:
                    ssd_squares(i + 2)
            for i in range(4):
                bank = mix_wait(act, ("oaT", i))
                for a in range(2):
                    m = 2 * i + a
                    ins = nc.scalar.mul(oaT[:, m], bank[:, a * T:(a + 1) * T], col("gla_g", m % 2))
                ins.then_inc(mix_used(("oaT", i)), 1)
            for i in range(8):
                bank = mix_wait(act, ("obT", i))
                for a in range(2):
                    m = 2 * i + a
                    ins = nc.scalar.mul(obT[:, m], bank[:, a * T:(a + 1) * T], col("ssm_g", m))
                ins.then_inc(mix_used(("obT", i)), 1)
            for t in range(TT):
                unit_taken(act, ("out", 1), t)
            for t in range(TT):
                if t:
                    act.wait_ge(x2_sq, t)
                nc.scalar.activation(sq_d, x_sb[:, t], ACT.Square, accum_out=st[:, 2 + t:3 + t]).then_inc(x2_sq, 1)
            act.wait_ge(rt_in, 1)
            nc.scalar.activation(rt[:, 0, :, 0:4], rt[:, 0, :, 0:4], ACT.Exp).then_inc(rt_e, 1)
            act.wait_ge(rt_in2, 1)
            nc.scalar.activation(rt[:, 12, :, 0:1], rt[:, 12, :, 0:1], ACT.Exp).then_inc(rt_e2, 1)
            with act.Fori(0, E // 4) as i:
                for u in range(4):
                    e = i * 4 + u
                    act.wait_ge(moe_h, e + 1)
                    act.wait_ge(hid_done, e + 1)
                    nc.scalar.activation(hid_s, ps[4][:], ACT.Silu).then_inc(hs_done, 1)
            act.wait_ge(y_moe, 1)
            for t in range(TT):
                act.wait_ge(y_evac, t + 1)
                if t:
                    act.wait_ge(x3_sq, t)
                nc.scalar.activation(sq_d, x_sb[:, t], ACT.Square, accum_out=st[:, 4 + t:5 + t]).then_inc(x3_sq, 1)

        @block.vector
        def _(dve):
            n = [0]

            def link(ins):
                n[0] += 1
                ins.then_inc(s_dve, 1)
                dve.wait_ge(s_dve, n[0])

            def rstd(ap, width):
                n_el = ap.free_size()
                m, y, s = (newton[:, i, 0:n_el] for i in range(3))
                if len(ap.shape) == 3:
                    m, y, s = (v.rearrange("p (a b) -> p a b", a=ap.shape[1]) for v in (m, y, s))
                link(nc.vector.tensor_scalar(m, ap, 1.0 / width, EPS, ALU.mult, ALU.add))
                link(nc.vector.tensor_scalar(s.bitcast(I32), m.bitcast(I32), 1, None, ALU.logical_shift_right))
                link(nc.vector.tensor_scalar(y.bitcast(I32), s.bitcast(I32), -1.0, float(0x5F3759DF), ALU.mult, ALU.add))
                for step in range(3):
                    link(nc.vector.tensor_tensor(s, y, y, ALU.mult))
                    link(nc.vector.scalar_tensor_tensor(s, s, -0.5, m, ALU.mult, ALU.mult))
                    link(nc.vector.scalar_tensor_tensor(y if step < 2 else ap, s, 1.5, y, ALU.add, ALU.mult))

            nc.vector.memset(gkT, 1.0).then_inc(ones_done, 1)
            nc.vector.memset(st[:, 12:13], 0.0).then_inc(hid_done, 1)
            bank = mix_wait(dve, "cols")
            nc.vector.tensor_copy(cols[:], bank[:, 0:NCOL]).then_inc(mix_used("cols"), 1)
            mix_taken(dve, "cols")
            dve.wait_ge(x_sq, TT)
            rstd(st[:, 0:TT], D)
            for t in range(TT):
                nc.vector.tensor_scalar(xn[:, t], x_sb[:, t], st[:, t:t + 1], None, ALU.mult).then_inc(xn_done, 1)
            bank = mix_wait(dve, "modA")
            link(nc.vector.tensor_tensor(mod[:, 0:16], bank[:, 0:16], col("ada_b", 0, 16), ALU.add))
            ins = nc.vector.scalar_tensor_tensor(mod[:, 8:16], mod[:, 8:16], 1.0, col("norm1", 0, 8), ALU.add, ALU.mult)
            ins.then_inc(mix_used("modA"), 1)
            mix_taken(dve, "modA")
            for i in range(4):
                bank = mix_wait(dve, ("xT", i))
                for a in range(2):
                    k = 2 * i + a
                    ins = nc.vector.tensor_scalar(hT[:, k], bank[:, a * T:(a + 1) * T], mod[:, 8 + k:9 + k],
                                                  mod[:, k:k + 1], ALU.mult, ALU.add)
                ins.then_inc(mix_used(("xT", i)), 1)
            bank = mix_wait(dve, "small")
            dve.wait_ge(ones_done, 1)
            nc.vector.tensor_copy(gkT[0:RANK, :], bank[0:RANK, 0:T])
            dve.wait_ge(s_rows, 48)
            nc.vector.tensor_tensor(dt, bank[:, T:T + TT * SH].rearrange("p (t h) -> p t h", t=TT),
                                    rows[:, 0:1, :].to_broadcast([P, TT, SH]), ALU.add).then_inc(mix_used("small"), 1)
            mix_taken(dve, "small")
            nc.vector.scalar_tensor_tensor(dt_abs[:], dt, -1.0, dt, ALU.mult, ALU.max).then_inc(sm_done, 1)
            dve.wait_ge(dt_sp, 1)
            link(nc.vector.scalar_tensor_tensor(dt, dt, 0.0, dt_abs[:], ALU.max, ALU.add))
            dve.wait_ge(a_exp, 1)
            nc.vector.scalar_tensor_tensor(dA, dt, -1.0, rows[:, 1:2, :].to_broadcast([P, TT, SH]), ALU.mult,
                                           ALU.mult).then_inc(dA_done, 1)
            step = 0
            for g in range(16):
                unit_taken(dve, ("xbc", g // 2), g % 2)
                if g >= 2:
                    dve.wait_ge(silu_done, g - 1)
                u, acc = u_cv[:, g % 2], acc_cv[:, g % 2]
                for tap in range(TAPS):
                    for a in range(2):
                        m = 2 * g + a
                        w = col("conv_w", (TAPS - 1 - tap) * 32 + m)
                        if tap == 0:
                            ins = nc.vector.tensor_scalar(acc[:, a], u[:, a], w, col("conv_b", m), ALU.mult, ALU.add)
                        else:
                            dve.wait_ge(conv_step, step - 1)
                            ins = nc.vector.scalar_tensor_tensor(acc[:, a, tap:], u[:, a, 0:T - tap], w,
                                                                 acc[:, a, tap:], ALU.mult, ALU.add)
                        if tap < TAPS - 1:
                            ins.then_inc(conv_step, 1)
                            step += 1
                        elif a == 0:
                            ins.then_inc(conv_step, 1)
                            step += 1
                        else:
                            ins.then_inc(conv_done, 1)
            bank = mix_wait(dve, "acum")
            nc.vector.tensor_copy(acum, bank[:, 0:64].rearrange("p (t h) -> p t h", t=TT))
            nc.vector.tensor_copy(dend, bank[:, 64:128].rearrange("p (t h) -> p t h", t=TT))
            nc.vector.tensor_copy(cdec[:].rearrange("p c h -> p (c h)"), bank[:, 128:256]).then_inc(mix_used("acum"), 1)
            mix_taken(dve, "acum")
            for t in range(TT):
                bank = mix_wait(dve, ("gklin", t))
                nc.vector.tensor_copy(gk_ls[:, t], bank[:]).then_inc(mix_used(("gklin", t)), 1)
                mix_taken(dve, ("gklin", t))
                nc.vector.scalar_tensor_tensor(gk_abs, gk_ls[:, t], -1.0, gk_ls[:, t], ALU.mult, ALU.max).then_inc(gk_in, 1)
                dve.wait_ge(gk_l, t + 1)
                nc.vector.scalar_tensor_tensor(gk_ls[:, t], gk_ls[:, t], 0.0, gk_sp, ALU.min, ALU.subtract
                                               ).then_inc(gk_done, 1)
            for t in range(TT):
                mix_taken(dve, ("gsuf", t))
                unit_taken(dve, ("k", 0), t)
                nc.vector.tensor_tensor(k_tm[:, t], k_tm[:, t], gsuf_e, ALU.mult).then_inc(kdec_done, 1)
            dve.wait_ge(s_const, 1)
            for t in range(TT):
                if t:
                    for j in range(4):
                        mix_wait(dve, ("arow", t - 1, j))
                nc.vector.tensor_tensor(rhsL, over(dA[:, t], CH), upto1[:].unsqueeze(1).to_broadcast([P, SH, CH]),
                                        ALU.mult).then_inc(rhs_done, 1)
                if t == 0:
                    dve.wait_ge(silu_done, 16)
                    for tt in range(TT):
                        mix_taken(dve, ("tr", 5, tt))
                for j in range(4):
                    bank = mix_wait(dve, ("arow", t, j))
                    ins = nc.vector.tensor_tensor(M[:, t, 8 * j:8 * j + 8], bank[:].rearrange("p (h s) -> p h s", s=CH),
                                                  over(acum[:, t, 8 * j:8 * j + 8], CH), ALU.subtract)
                    ins.then_inc(mix_used(("arow", t, j)), 1)
            for t in range(TT):
                bank = mix_wait(dve, ("cb", t))
                dve.wait_ge(L_done, t + 1)
                Mt = M[:, t].rearrange("p (g r) s -> p g r s", g=SG)
                cb = bank[:].rearrange("p (g s) -> p g s", g=SG).unsqueeze(2).to_broadcast([P, SG, 4, CH])
                nc.vector.tensor_tensor(Mt, Mt, cb, ALU.mult).then_inc(mix_used(("cb", t)), 1)
            mix_taken(dve, "gdec")
            for c_ in range(NC):
                for hp in range(2):
                    bank = mix_wait(dve, ("gU", c_, hp))
                    if c_:
                        mix_taken(dve, ("gU", c_ - 1, hp))
                    for a in range(2):
                        h = 2 * hp + a
                        u = bank[:, a * HV:(a + 1) * HV]
                        if c_ == 0:
                            ins = nc.vector.tensor_copy(gla_st[:, 0, h], u)
                        else:
                            ins = nc.vector.scalar_tensor_tensor(gla_st[:, c_, h], gla_st[:, c_ - 1, h],
                                                                 gdec[:, h, c_:c_ + 1], u, ALU.mult, ALU.add)
                    ins.then_inc(mix_used(("gU", c_, hp)), 1)
            for i in range(2):
                for t in range(TT):
                    unit_taken(dve, ("g", i), t)
            for t in range(TT):
                for hp in range(2):
                    bank = mix_wait(dve, ("gO", t, hp))
                    dve.wait_ge(gO_sq, 4 * t + 2 * hp + 2)
                    rstd(gss[:, 0, t, 2 * hp:2 * hp + 2], HV)
                    for a in range(2):
                        h = 2 * hp + a
                        o = g_sb[:, t, h * HV:(h + 1) * HV]
                        ins = nc.vector.scalar_tensor_tensor(o, bank[:, a * HV:(a + 1) * HV], gss[:, 0, t, h:h + 1], o,
                                                             ALU.mult, ALU.mult)
                    ins.then_inc(mix_used(("gO", t, hp)), 1)
            dve.wait_ge(eac_done, 1)
            for j in range(4):
                hs = slice(8 * j, 8 * j + 8)
                for c_ in range(3):
                    bank = mix_wait(dve, ("U", j, c_))
                    if c_ == 0:
                        ins = nc.vector.tensor_copy(r_pv[:, 0], bank[:])
                    else:
                        link(nc.vector.tensor_tensor(heads(r_pv[:, c_]), heads(r_pv[:, c_ - 1]), over(cdec[:, c_, hs], SP_),
                                                     ALU.mult))
                        ins = nc.vector.tensor_tensor(r_pv[:, c_], r_pv[:, c_], bank[:], ALU.add)
                    ins.then_inc(mix_used(("U", j, c_)), 1)
                    mix_taken(dve, ("U", j, c_))
                dve.wait_ge(skip_done, 2 * j + 2)
                for t in range(TT):
                    lo = CH if t == 0 else 0
                    off = mix_wait(dve, ("off", j, t))
                    nc.vector.tensor_tensor(heads(y_off[lo:, t]), heads(off[lo:, :]), over(eacum[lo:, t, hs], SP_),
                                            ALU.mult).then_inc(mix_used(("off", j, t)), 1)
                for t in range(TT):
                    lo = CH if t == 0 else 0
                    dg = mix_wait(dve, ("diag", j, t))
                    nc.vector.tensor_tensor(y_tmp[:, t], dg[:], xs[:, t, j * 512:(j + 1) * 512], ALU.add).then_inc(
                        mix_used(("diag", j, t)), 1)
                    mix_taken(dve, ("diag", j, t))
                    mix_taken(dve, ("off", j, t))
                    link(nc.vector.tensor_tensor(y_tmp[lo:, t], y_tmp[lo:, t], y_off[lo:, t], ALU.add))
                    unit_taken(dve, ("z", j), t)
                    z = z_tm[:, t, j * 512:(j + 1) * 512]
                    nc.vector.tensor_tensor(z, y_tmp[:, t], z, ALU.mult).then_inc(y_done, 1)
            dve.wait_ge(y_sq, TT * SG)
            rstd(sss[:, 0], 256)
            for t in range(TT):
                for g in range(SG):
                    o = z_tm[:, t, g * 256:(g + 1) * 256]
                    ins = nc.vector.tensor_scalar(o, o, sss[:, 0, t, g:g + 1], None, ALU.mult)
                ins.then_inc(ob_done, 1)
            bank = mix_wait(dve, "modB")
            link(nc.vector.tensor_tensor(mod[:, 16:48], bank[:, 0:32], col("ada_b", 16, 32), ALU.add))
            nc.vector.scalar_tensor_tensor(mod[:, 32:40], mod[:, 32:40], 1.0, col("norm2", 0, 8), ALU.add,
                                           ALU.mult).then_inc(mix_used("modB"), 1)
            mix_taken(dve, "modB")
            for w in range(2):
                for h in range(2):
                    at = (16, 40)[w] + 4 * h
                    nc.vector.tensor_tensor(diag[:, h].rearrange("p (k q) -> p k q", k=4),
                                            ident[:].unsqueeze(1).to_broadcast([P, 4, P]), over(mod[:, at:at + 4], P),
                                            ALU.mult).then_inc(diag_done, 1)
                for h in range(2):
                    bank = mix_wait(dve, ("gtb", w, h))
                    nc.vector.tensor_copy((gt1b, gt2b)[w][:, h * 512:(h + 1) * 512], bank[:]).then_inc(
                        mix_used(("gtb", w, h)), 1)
            for i in range(4):
                for h in range(2):
                    unit_taken(dve, ("gate", i), h)
            for name in ("oa", "ob"):
                for i in range(2):
                    for h in range(2):
                        bank = unit_wait(dve, (name, i), h)
                        m = 4 * i + 2 * h
                        dst = mT[:, m:m + 2].rearrange("p m t -> p (m t)")
                        if name == "oa":
                            ins = nc.vector.tensor_tensor(dst, bank[:], gateT[:, m:m + 2].rearrange("p m t -> p (m t)"),
                                                          ALU.mult)
                        else:
                            link(nc.vector.tensor_tensor(m_tmp, bank[:], gateT[:, KD + m:KD + m + 2].rearrange(
                                "p m t -> p (m t)"), ALU.mult))
                            ins = nc.vector.tensor_tensor(dst, dst, m_tmp, ALU.add)
                        ins.then_inc(unit_used((name, i), h), 1)
                        unit_taken(dve, (name, i), h)
            for i in range(2):
                for t in range(TT):
                    bank = unit_wait(dve, ("out", i), t)
                    xs_ = x_sb[:, t, i * CW:(i + 1) * CW]
                    link(nc.vector.tensor_tensor(m_tmp, bank[:], gt1b[:, i * CW:(i + 1) * CW], ALU.mult))
                    ins = nc.vector.tensor_tensor(xs_, xs_, m_tmp, ALU.add)
                    ins.then_inc(unit_used(("out", i), t), 1)
                    unit_taken(dve, ("out", i), t)
            dve.wait_ge(x2_sq, TT)
            rstd(st[:, 2:4], D)
            for t in range(TT):
                nc.vector.tensor_scalar(x2n[:, t], x_sb[:, t], st[:, 2 + t:3 + t], None, ALU.mult).then_inc(x2n_done, 1)
            for i in range(4):
                bank = mix_wait(dve, ("x2T", i))
                for a in range(2):
                    k = 2 * i + a
                    ins = nc.vector.tensor_scalar(hT[:, k], bank[:, a * T:(a + 1) * T], mod[:, 32 + k:33 + k],
                                                  mod[:, 24 + k:25 + k], ALU.mult, ALU.add)
                ins.then_inc(mix_used(("x2T", i)), 1)
            bank = mix_wait(dve, "router")
            dve.wait_ge(s_wr, 64)
            nc.vector.tensor_tensor(lg, bank[:, 0:TT * 36].rearrange("p (t n) -> p t n", t=TT),
                                    rb.unsqueeze(1).to_broadcast([P, TT, 36]), ALU.add).then_inc(mix_used("router"), 1)
            mix_taken(dve, "router")
            R = [rt[:, i] for i in range(24)]

            def pick(dst, vals, top, w, tmp):
                link(nc.vector.tensor_tensor(tmp[:, :, 0:w], vals, top.to_broadcast([P, TT, w]), ALU.is_equal))
                link(nc.vector.tensor_tensor(tmp[:, :, 0:w], tmp[:, :, 0:w],
                                             w_down[:, 0:w].unsqueeze(1).to_broadcast([P, TT, w]), ALU.mult))
                link(nc.vector.reduce_max(R[23][:, :, 0:1], tmp[:, :, 0:w], AX_X))
                link(nc.vector.tensor_tensor(dst, tmp[:, :, 0:w], R[23][:, :, 0:1].to_broadcast([P, TT, w]), ALU.is_equal))

            link(nc.vector.reduce_max(R[1][:, :, 0:1], lg[:, :, 0:4], AX_X))
            pick(R[2][:, :, 0:4], lg[:, :, 0:4], R[1][:, :, 0:1], 4, R[3])
            nc.vector.tensor_tensor(R[0][:, :, 0:4], lg[:, :, 0:4], R[1][:, :, 0:1].to_broadcast([P, TT, 4]),
                                    ALU.subtract).then_inc(rt_in, 1)
            link(nc.vector.tensor_tensor(rt4, lg[:, :, 4:36].rearrange("p t (g e) -> p t g e", g=4),
                                         over(R[2][:, :, 0:4], EG), ALU.mult))
            link(nc.vector.reduce_sum(R[4], rt4.rearrange("p t g e -> p t e g"), AX_X))
            link(nc.vector.reduce_max(R[5][:, :, 0:1], R[4], AX_X))
            link(nc.vector.tensor_tensor(R[6], R[4], R[5][:, :, 0:1].to_broadcast([P, TT, EG]), ALU.subtract))
            link(nc.vector.memset(R[7][:, :, 0:1], 0.0))
            pick(R[8], R[6], R[7][:, :, 0:1], EG, R[9])
            link(nc.vector.scalar_tensor_tensor(R[10], R[8], -1e30, R[6], ALU.mult, ALU.add))
            link(nc.vector.reduce_max(R[11][:, :, 0:1], R[10], AX_X))
            nc.vector.tensor_copy(R[12][:, :, 0:1], R[11][:, :, 0:1]).then_inc(rt_in2, 1)
            pick(R[13], R[10], R[11][:, :, 0:1], EG, R[14])
            dve.wait_ge(rt_e, 1)
            link(nc.vector.reduce_sum(R[15][:, :, 0:1], R[0][:, :, 0:4], AX_X))
            dve.wait_ge(rt_e2, 1)
            link(nc.vector.tensor_scalar(R[16][:, :, 0:1], R[12][:, :, 0:1], 1.0, None, ALU.add))
            link(nc.vector.tensor_tensor(R[16][:, :, 0:1], R[16][:, :, 0:1], R[15][:, :, 0:1], ALU.mult))
            link(nc.vector.reciprocal(R[17][:, :, 0:1], R[16][:, :, 0:1]))
            link(nc.vector.tensor_tensor(R[18][:, :, 0:1], R[17][:, :, 0:1], R[12][:, :, 0:1], ALU.mult))
            link(nc.vector.tensor_tensor(R[8], R[8], R[17][:, :, 0:1].to_broadcast([P, TT, EG]), ALU.mult))
            link(nc.vector.tensor_tensor(R[13], R[13], R[18][:, :, 0:1].to_broadcast([P, TT, EG]), ALU.mult))
            link(nc.vector.tensor_tensor(R[19], R[8], R[13], ALU.add))
            nc.vector.tensor_tensor(comb.rearrange("p t (g e) -> p t g e", g=4), over(R[2][:, :, 0:4], EG),
                                    R[19].unsqueeze(2).to_broadcast([P, TT, 4, EG]), ALU.mult).then_inc(comb_done, 1)
            dve.wait_ge(comb_done, 1)
            with dve.Fori(0, E // 4) as i:
                for u in range(4):
                    e = i * 4 + u
                    for t in range(TT):
                        ins = nc.vector.tensor_scalar(moe_dg[:, u % 2, t], ident[:], comb[:, t, bass.ds(e, 1)], None, ALU.mult)
                    ins.then_inc(dg_done, 1)
                    dve.wait_ge(moe_h, e + 1)
                    nc.vector.tensor_copy(hid_w, ps[6][:, 0:T]).then_inc(hw_done, 1)
                    dve.wait_ge(hw_done, e + 1)
                    nc.vector.tensor_tensor(hid_p.rearrange("p (f t) -> p f t", f=2), ps[5][:].rearrange(
                        "p (f t) -> p f t", f=2), hid_w.unsqueeze(1).to_broadcast([P, 2, T]), ALU.mult).then_inc(hp_done, 1)
                    dve.wait_ge(hp_done, e + 1)
                    dve.wait_ge(hs_done, e + 1)
                    nc.vector.tensor_tensor(hid[:, u % 2].rearrange("p f t -> p (f t)"), hid_p, hid_s, ALU.mult
                                            ).then_inc(hid_done, 1)
            dve.wait_ge(y_moe, 1)
            for t in range(TT):
                if t:
                    dve.wait_ge(y_evac, t)
                link(nc.vector.tensor_tensor(m_tmp, ps[2 * t][:], gt2b[:, 0:512], ALU.mult))
                link(nc.vector.tensor_tensor(x_sb[:, t, 0:512], x_sb[:, t, 0:512], m_tmp, ALU.add))
                link(nc.vector.tensor_tensor(m_tmp, ps[2 * t + 1][:], gt2b[:, 512:], ALU.mult))
                nc.vector.tensor_tensor(x_sb[:, t, 512:], x_sb[:, t, 512:], m_tmp, ALU.add).then_inc(y_evac, 1)
            dve.wait_ge(x3_sq, TT)
            rstd(st[:, 4:6], D)
            dve.wait_ge(s_fng, 16)
            for t in range(TT):
                nc.vector.scalar_tensor_tensor(x_sb[:, t], x_sb[:, t], st[:, 4 + t:5 + t], fng, ALU.mult,
                                               ALU.mult).then_inc(fin_done, 1)

        @block.tensor
        def _(pe):
            def begin(name):
                bank, b, turn = mix(name)
                if turn:
                    pe.wait_ge(bank_free[b], turn)
                return bank

            def full(name):
                return bank_full[mix(name)[1]]

            def load_wait(i):
                pe.wait_ge(slot_full[i % SLOTS], 16 * (i // SLOTS + 1))
                return ring[:, i % SLOTS]

            def mm(o, l, r, start=True, stop=True):
                return nc.tensor.matmul(o, l, r, start=start, stop=stop)

            def modulation(lo, hi, name):
                bank = begin(name)
                for i in range(lo, hi):
                    n = CHUNK_AT["ada", i]
                    w = load_wait(n)
                    for m in range(4):
                        at = 4 * (i - lo) + m
                        for k in range(KD):
                            ins = mm(bank[:, at:at + 1], w[:, k, m * P:(m + 1) * P], cact[:, k:k + 1], k == 0, k == KD - 1)
                    ins.then_inc(ada_used, 1)
                mm(bank[:, 511:512], ident[:], ones[:, 0:1]).then_inc(full(name), 1)

            def channel_major(u, chunk, src, halves=(0, 1), first=True, last=True):
                w = load_wait(chunk)
                for half in halves:
                    bank, b, turn = unit(u, half)
                    if first and turn:
                        pe.wait_ge(bank_free[b], turn)
                    for a in range(2):
                        m = 2 * half + a
                        for k in range(KD):
                            ins = mm(bank[:, a * T:(a + 1) * T], w[:, k, m * P:(m + 1) * P], src[:, k],
                                     first and k == 0, last and k == KD - 1)
                    if last and half == 0:
                        ins.then_inc(bank_full[b], 1)
                return ins

            def token_major(u, chunk, src):
                w = load_wait(chunk)
                for t in range(TT):
                    bank, b, turn = unit(u, t)
                    if turn:
                        pe.wait_ge(bank_free[b], turn)
                    for k in range(KD):
                        ins = mm(bank[:], src[:, k, t * P:(t + 1) * P], w[:, k], k == 0, k == KD - 1)
                    if t == 0:
                        ins.then_inc(bank_full[b], 1)
                return ins

            def close(u, chunk, ins):
                ins.then_inc(bank_full[unit(u, 1)[1]], 1)

            def project(u, channels):
                n = CHUNK_AT[u]
                close(u, n, (channel_major if channels else token_major)(u, n, hT))

            def transposed(name, pieces, rows=P):
                bank = begin(name)
                at = 0
                for src in pieces:
                    ins = nc.tensor.transpose(bank[:, at:at + P], src, ident[:])
                    at += P
                ins.then_inc(full(name), 1)

            pe.wait_ge(s_stack, 16 * 8)
            pe.wait_ge(s_const, 1)
            bank = begin("cols")
            nc.tensor.transpose(bank[:, 0:P], stackA, ident[:])
            nc.tensor.transpose(bank[:, P:NCOL], stackB[0:NCOL - P, :], ident[0:NCOL - P, 0:NCOL - P]).then_inc(
                full("cols"), 1)
            pe.wait_ge(cact_done, 1)
            modulation(0, 4, "modA")
            pe.wait_ge(xn_done, TT)
            for i in range(4):
                transposed(("xT", i), [xn[:, t, (2 * i + a) * P:(2 * i + a + 1) * P] for a in range(2) for t in range(TT)])
            for i in range(4):
                mix_taken(pe, ("xT", i))
            pe.wait_ge(s_small, 64)
            bank = begin("small")
            for k in range(KD):
                mm(bank[0:RANK, 0:T], wsm[:, k, 0:RANK], hT[:, k], k == 0, k == KD - 1)
            for t in range(TT):
                for k in range(KD):
                    ins = mm(bank[:, T + t * SH:T + (t + 1) * SH], hT[:, k, t * P:(t + 1) * P], wsm[:, k, RANK:], k == 0,
                             k == KD - 1)
            ins.then_inc(full("small"), 1)

            for i in range(8):
                project(("xbc", i), True)
                if 1 <= i <= 6:
                    pe.wait_ge(silu_done, 2 * i)
                    src = xsT[:, (i - 1) % 2] if i <= 4 else BT[:, 4 * (i - 5):4 * (i - 4)]
                    for t in range(TT):
                        transposed(("tr", i - 1, t), [src[:, m, t * P:(t + 1) * P] for m in range(4)])

            project(("k", 0), False)
            pe.wait_ge(dA_done, 1)
            bank = begin("acum")
            for t in range(TT):
                mm(bank[:, t * SH:(t + 1) * SH], upto[:], dA[:, t])
                mm(bank[:, 64 + t * SH:64 + (t + 1) * SH], after[:], dA[:, t])
                for a in range(2):
                    ins = mm(bank[:, 128 + (2 * t + a) * SH:128 + (2 * t + a + 1) * SH], inch[:, a], dA[:, t])
            ins.then_inc(full("acum"), 1)
            for t in range(TT):
                mm(begin(("gklin", t))[:], gkT[:, t * P:(t + 1) * P], wgk2).then_inc(full(("gklin", t)), 1)
            project(("q", 0), True)
            pe.wait_ge(gk_done, TT)
            for t in range(TT):
                mm(begin(("gsuf", t))[:], after[:], gk_ls[:, t]).then_inc(full(("gsuf", t)), 1)
            bank = begin("gdec")
            for h in range(GH):
                for t in range(TT):
                    at = h * NC + 2 * t
                    ins = mm(bank[:, at:at + 2], gk_ls[:, t, h * HK:(h + 1) * HK], inch[:, :, 0])
            ins.then_inc(full("gdec"), 1)

            def rows_of_sums(t):
                pe.wait_ge(rhs_done, t + 1)
                for j in range(4):
                    mm(begin(("arow", t, j))[:], same[:], rhsL[:, 8 * j:8 * j + 8]).then_inc(full(("arow", t, j)), 1)

            project(("v", 0), False)
            rows_of_sums(0)
            project(("v", 1), False)
            rows_of_sums(1)
            pe.wait_ge(silu_done, 16)
            for t in range(TT):
                bank = begin(("cb", t))
                for a in range(2):
                    cs = slice(t * P + a * CH, t * P + (a + 1) * CH)
                    for g in range(SG):
                        ins = mm(bank[a * CH:(a + 1) * CH, g * CH:(g + 1) * CH], BT[:, g, cs], CT[:, g, cs])
                ins.then_inc(full(("cb", t)), 1)

            def gla_updates(c_):
                t, lo = c_ // 2, (c_ % 2) * CH
                for hp in range(2):
                    bank = begin(("gU", c_, hp))
                    for a in range(2):
                        h = 2 * hp + a
                        ins = mm(bank[:, a * HV:(a + 1) * HV], k_tm[lo:lo + CH, t, h * HK:(h + 1) * HK],
                                 v_tm[lo:lo + CH, t, h * HV:(h + 1) * HV])
                    ins.then_inc(full(("gU", c_, hp)), 1)

            def gla_outputs():
                for t in range(TT):
                    for hp in range(2):
                        bank = begin(("gO", t, hp))
                        for a in range(2):
                            c_ = 2 * t + a
                            for b in range(2):
                                h = 2 * hp + b
                                mix_taken(pe, ("gU", c_, hp))
                                ins = mm(bank[a * CH:(a + 1) * CH, b * HV:(b + 1) * HV], qT[:, h, c_ * CH:(c_ + 1) * CH],
                                         gla_st[:, c_, h])
                        ins.then_inc(full(("gO", t, hp)), 1)

            def ssd(j):
                pe.wait_ge(xdd_done, 2 * (j + 1))
                for c_ in range(3):
                    t, lo = c_ // 2, (c_ % 2) * CH
                    bank = begin(("U", j, c_))
                    for a in range(2):
                        g = 2 * j + a
                        ins = mm(bank[:, a * 256:(a + 1) * 256], Btm[lo:lo + CH, t, g * NS:(g + 1) * NS],
                                 xdd[lo:lo + CH, j % 2, t, a * 256:(a + 1) * 256])
                    ins.then_inc(full(("U", j, c_)), 1)
                for t in range(TT):
                    bank = begin(("off", j, t))
                    for b in range(2):
                        c_ = 2 * t + b
                        if c_ == 0:
                            continue
                        mix_taken(pe, ("U", j, c_ - 1))
                        for a in range(2):
                            g = 2 * j + a
                            ins = mm(bank[b * CH:(b + 1) * CH, a * 256:(a + 1) * 256], CT[:, g, c_ * CH:(c_ + 1) * CH],
                                     r_pv[:, c_ - 1, a * 256:(a + 1) * 256])
                    ins.then_inc(full(("off", j, t)), 1)
                for t in range(TT):
                    mix_taken(pe, ("cb", t))
                    bank = begin(("diag", j, t))
                    for b in range(2):
                        part = slice(b * CH, (b + 1) * CH)
                        for h in range(8):
                            ins = mm(bank[part, h * SP_:(h + 1) * SP_], M[part, t, 8 * j + h],
                                     xdt[part, j % 2, t, h * SP_:(h + 1) * SP_])
                    ins.then_inc(full(("diag", j, t)), 1)

            for i in range(2):
                project(("g", i), False)
                if i == 0:
                    pe.wait_ge(kdec_done, TT)
                    for name in (("v", 0), ("v", 1)):
                        for t in range(TT):
                            unit_taken(pe, name, t)
                for c_ in (2 * i, 2 * i + 1):
                    gla_updates(c_)
            for i in range(4):
                project(("z", i), False)
                if i == 0:
                    for h in range(2):
                        unit_taken(pe, ("q", 0), h)
                    gla_outputs()
                else:
                    ssd(i - 1)
            for i in range(4):
                project(("gate", i), True)
                if i == 0:
                    ssd(3)
                if i == 1:
                    for t in range(TT):
                        for hp in range(2):
                            mix_taken(pe, ("gO", t, hp))
                    for m in range(4):
                        transposed(("oaT", m), [g_sb[:, t, (2 * m + a) * P:(2 * m + a + 1) * P] for a in range(2)
                                                for t in range(TT)])
                if i == 3:
                    pe.wait_ge(ob_done, TT)
                    for m in range(8):
                        transposed(("obT", m), [z_tm[:, t, (2 * m + a) * P:(2 * m + a + 1) * P] for a in range(2)
                                                for t in range(TT)])
            modulation(4, 12, "modB")
            for w in range(2):
                for h in range(2):
                    pe.wait_ge(diag_done, 2 * w + h + 1)
                    mm(begin(("gtb", w, h))[:], ones[:], diag[:, h]).then_inc(full(("gtb", w, h)), 1)
            for i in range(4):
                mix_taken(pe, ("oaT", i))
            for i in range(2):
                n = CHUNK_AT["oa", i]
                close(("oa", i), n, channel_major(("oa", i), n, oaT))
            for i in range(8):
                mix_taken(pe, ("obT", i))
            for i in range(2):
                n0, n1 = CHUNK_AT["ob", 2 * i], CHUNK_AT["ob", 2 * i + 1]
                w = [load_wait(n0), load_wait(n1)]
                for half in range(2):
                    bank, b, turn = unit(("ob", i), half)
                    pe.wait_ge(bank_free[b], turn)
                    for a in range(2):
                        m = 2 * half + a
                        for k in range(2 * KD):
                            ins = mm(bank[:, a * T:(a + 1) * T], w[k // KD][:, k % KD, m * P:(m + 1) * P], obT[:, k],
                                     k == 0, k == 2 * KD - 1)
                            if half == 1 and a == 1 and k == KD - 1:
                                ins.then_inc(ob_used, 1)
                    if half == 0:
                        ins.then_inc(bank_full[b], 1)
                close(("ob", i), n1, ins)
            for i in range(2):
                for h in range(2):
                    unit_taken(pe, ("ob", i), h)
            for i in range(2):
                n = CHUNK_AT["out", i]
                close(("out", i), n, token_major(("out", i), n, mT))
            pe.wait_ge(x2n_done, TT)
            for i in range(4):
                transposed(("x2T", i), [x2n[:, t, (2 * i + a) * P:(2 * i + a + 1) * P] for a in range(2) for t in range(TT)])
            for i in range(4):
                mix_taken(pe, ("x2T", i))
            pe.wait_ge(s_wr, 64)
            bank = begin("router")
            for t in range(TT):
                for k in range(KD):
                    ins = mm(bank[:, t * 36:(t + 1) * 36], hT[:, k, t * P:(t + 1) * P], wr[:, k], k == 0, k == KD - 1)
            ins.then_inc(full("router"), 1)
            mix_taken(pe, "router")

            base = len(CHUNKS)

            def up(e, s, k, given, par):
                pe.wait_ge(slot_full[s], k)
                pe.wait_ge(hid_done, given)
                for m in range(4):
                    bank = ps[4 + m // 2]
                    for kk in range(KD):
                        ins = mm(bank[:, (m % 2) * T:(m % 2 + 1) * T], ring[:, s, kk, m * P:(m + 1) * P], hT[:, kk],
                                 kk == 0, kk == KD - 1)
                ins.then_inc(slot_free[s], 1)
                pe.wait_ge(dg_done, e)
                mm(ps[6][:, 0:T], ones[:], moe_dg[:, par].rearrange("p t q -> p (t q)")).then_inc(moe_h, 1)

            def before(s):
                return 16 * len([i for i in range(base) if i % SLOTS == s])

            def down(w2, full_at, hid_at, par, first=False, last=False):
                pe.wait_ge(w2_full[w2], full_at)
                pe.wait_ge(hid_done, hid_at)
                for t in range(TT):
                    for n in range(2):
                        for f in range(2):
                            ins = mm(ps[2 * t + n][:], hid[:, par, f, t * P:(t + 1) * P],
                                     w2_slot[w2][:, f, n * 512:(n + 1) * 512], first and f == 0, last and f == 1)
                ins.then_inc(w2_free[w2], 1)

            for i in range(2):
                for t in range(TT):
                    unit_taken(pe, ("out", i), t)
            def up_static(e):
                s = (base + e) % SLOTS
                up(e + 1, s, before(s) + 32 * (e // 4 + 1), e + 1, e % 2)

            up_static(0)
            up_static(1)
            down(0, 16, 2, 0, first=True)
            with pe.Fori(0, 7) as i:
                for u in range(4):
                    e1 = 2 + u
                    s = (base + e1) % SLOTS
                    up(i * 4 + (e1 + 1), s, i * 32 + (before(s) + 32 * (e1 // 4 + 1)), i * 4 + (e1 + 1), e1 % 2)
                    down((e1 - 1) % 4, i * 16 + 16 * ((e1 - 1) // 4 + 1), i * 4 + (e1 + 1), (e1 - 1) % 2)
            for e in (30, 31):
                up_static(e)
                down((e - 1) % 4, 16 * ((e - 1) // 4 + 1), e + 1, (e - 1) % 2)
            down(3, 16 * 8, E + 1, 1, last=True)
            mm(ps[7][:, 0:1], ident[:], ones[:, 0:1]).then_inc(y_moe, 1)


_INS = ["x", "c", "ada_w", "ada_b", "norm1_g", "w_in", "gla_w_gk2", "gla_b_gk", "gla_norm_g", "conv_w", "conv_b",
        "dt_bias", "a_log", "d_skip", "ssm_norm_g", "w_oa", "w_ob", "w_out", "norm2_g", "router_group_w",
        "router_group_b", "router_expert_w", "router_expert_b", "expert_w1", "expert_w3", "expert_w2", "final_norm_g"]


def kernel(**inputs):
    import concourse.bacc as bacc
    import numpy as np
    from concourse.bass_utils import run_bass_kernel_spmd

    nc = bacc.Bacc("TRN2", target_bir_lowering=False, num_devices=1)
    arrays, args = {}, []
    for name in _INS:
        a = np.ascontiguousarray(inputs[name])
        arrays[f"in_{name}"] = a
        args.append(nc.dram_tensor(f"in_{name}", a.shape, mybir.dt.from_np(a.dtype), kind="ExternalInput").ap())
    out = nc.dram_tensor("out", inputs["x"].shape, F32, kind="ExternalOutput").ap()
    trunk(nc, *args, out)
    r = run_bass_kernel_spmd(nc, [arrays], core_ids=[0])
    return r.results[0]["out"]
```

```python
from contextlib import ExitStack

import concourse.bass as bass
from concourse import mybir

F32, I32 = mybir.dt.float32, mybir.dt.int32
ALU = mybir.AluOpType
ACT = mybir.ActivationFunctionType
AX_X = mybir.AxisListType.X

P = 128
T = 256
TT = T // P
D = 1024
KD = D // P
CH = 64
NC = T // CH
EPS = 1e-6
GH, HK, HV, RANK = 4, 128, 256, 16
SH, SP_, SG, NS = 32, 64, 8, 128
DI = SH * SP_
CONV_CH, TAPS = DI + 2 * SG * NS, 4
E, EG, FF = 32, 8, 256
SLOTS, CW = 4, 512
W = 64
JOBS = 2 * T // W

OFF = {}
_at = 0
for _n, _w in (("q", 512), ("k", 512), ("v", 1024), ("g", 1024), ("gk", RANK), ("z", DI), ("xbc", CONV_CH),
               ("dt", SH), ("gate", 2 * D)):
    OFF[_n] = _at
    _at += _w

COL, _at = {"conv_w": 0}, 128
for _n, _w in (("conv_b", 32), ("ssm_g", 16), ("norm1", 8), ("norm2", 8), ("ada_b", 48), ("c", 8), ("gla_g", 2)):
    COL[_n] = _at
    _at += _w
NCOL = _at

CHUNKS = ([("ada", i) for i in range(4)] + [("xbc", i) for i in range(8)] + [("k", 0), ("q", 0), ("v", 0), ("v", 1)]
          + [("g", i) for i in range(2)] + [("z", i) for i in range(4)] + [("gate", i) for i in range(4)]
          + [("ada", i) for i in range(4, 12)] + [("oa", i) for i in range(2)] + [("ob", i) for i in range(4)]
          + [("out", i) for i in range(2)])
CHUNK_AT = {c: i for i, c in enumerate(CHUNKS)}
UNITS = [c for c in CHUNKS if c[0] not in ("ada", "ob", "oa", "out")] + [("oa", 0), ("oa", 1), ("ob", 0), ("ob", 1),
                                                                        ("out", 0), ("out", 1)]
MIX = ["cols", "modA"] + [("xT", i) for i in range(4)] + ["small"]
for _i in range(1, 7):
    MIX += [("tr", _i - 1, 0), ("tr", _i - 1, 1)]
MIX += ["acum", ("gklin", 0), ("gklin", 1), ("gsuf", 0), ("gsuf", 1), "gdec"]
MIX += [("arow", 0, j) for j in range(4)] + [("arow", 1, j) for j in range(4)] + [("cb", 0), ("cb", 1)]
MIX += [("gU", c, hp) for c in range(NC) for hp in range(2)] + [("gO", t, hp) for t in range(TT) for hp in range(2)]
for _j in range(4):
    MIX += [("U", _j, c) for c in range(3)] + [("off", _j, 0), ("off", _j, 1), ("diag", _j, 0), ("diag", _j, 1)]
MIX += [("oaT", i) for i in range(4)] + [("obT", i) for i in range(8)]
MIX += ["modB"] + [("gtb", w, h) for w in range(4) for h in range(2)]
MIX += [("x2T", i) for i in range(4)] + ["router", "pos"]
MIX_AT = {n: i for i, n in enumerate(MIX)}


def trunk(nc, x, c, ada_w, ada_b, norm1_g, w_in, gla_w_gk2, gla_b_gk, gla_norm_g, conv_w, conv_b, dt_bias, a_log,
          d_skip, ssm_norm_g, w_oa, w_ob, w_out, norm2_g, router_group_w, router_group_b, router_expert_w,
          router_expert_b, expert_w1, expert_w3, expert_w2, final_norm_g, out):
    with ExitStack() as ctx:
        def sb(name, *dims):
            return ctx.enter_context(nc.sbuf_tensor(name, [P, *dims], F32))

        def sem(name):
            return ctx.enter_context(nc.semaphore(name))

        ring = sb("ring", SLOTS, KD, CW)
        x_sb = sb("x_sb", TT, D)
        hT = sb("hT", KD, T)
        r_k = sb("r_k", 1024)
        r_q = sb("r_q", 1024)
        r_v = sb("r_v", 2048)
        g_sb = sb("g_sb", TT, D)
        r_z = sb("r_z", 4096)
        r_xs = sb("r_xs", 4096)
        r_bt = sb("r_bt", 2048)
        r_ct = sb("r_ct", 2048)
        r_btm = sb("r_btm", 2048)
        r_lm = sb("r_lm", 4096)
        r_st = sb("r_st", 4096)
        r_pv = sb("r_pv", 3, 512)

        def view(region, pattern, **kw):
            return region[:].rearrange(pattern, **kw)

        k_tm = view(r_k, "p (t d) -> p t d", t=TT)
        qT = view(r_q, "p (h t) -> p h t", h=GH)
        v_tm = view(r_v, "p (t d) -> p t d", t=TT)
        z_tm = view(r_z, "p (t d) -> p t d", t=TT)
        xn = r_z[:, 0:2048].rearrange("p (t d) -> p t d", t=TT)
        xs = view(r_xs, "p (t d) -> p t d", t=TT)
        BT = view(r_bt, "p (g t) -> p g t", g=SG)
        CT = view(r_ct, "p (g t) -> p g t", g=SG)
        Btm = view(r_btm, "p (t d) -> p t d", t=TT)
        u_cv = r_lm[:, 0:1024].rearrange("p (b a t) -> p b a t", b=2, a=2)
        acc_cv = r_lm[:, 1024:2048].rearrange("p (b a t) -> p b a t", b=2, a=2)
        xsT = r_lm[:, 2048:4096].rearrange("p (b a t) -> p b a t", b=2, a=4)
        M = view(r_lm, "p (t h s) -> p t h s", t=TT, h=SH)
        rhsL = r_st[:, 0:2048].rearrange("p (h s) -> p h s", h=SH)
        gla_st = view(r_st, "p (c h v) -> p c h v", c=NC, h=GH)
        zeros = r_st[:, 2048:2048 + D]
        gateT = view(r_st, "p (m t) -> p m t", m=2 * KD)
        gk_abs = r_pv[:, 0, :]
        gk_sp = r_pv[:, 1, :]
        gsuf_e = r_pv[:, 2, :]
        xdt = view(r_v, "p (b t d) -> p b t d", b=2, t=TT)
        xdd = view(r_bt, "p (b t d) -> p b t d", b=2, t=TT)
        y_tmp = view(r_k, "p (b d) -> p b d", b=2)
        y_off = view(r_q, "p (b d) -> p b d", b=2)
        oaT = view(r_btm, "p (m t) -> p m t", m=KD)
        obT = view(r_lm, "p (m t) -> p m t", m=2 * KD)
        mT = view(r_bt, "p (m t) -> p m t", m=KD)
        gt1b = view(r_k, "p d -> p d")
        gt2b = view(r_q, "p d -> p d")
        s2b, sh2b = r_ct[:, 0:D], r_ct[:, D:2 * D]
        diag = r_pv[:, 0:2, :]
        m_tmp = r_pv[:, 2, :]
        h2 = view(r_v, "p (t d) -> p t d", t=TT)
        w2z = view(r_z, "p (b k d) -> p b k d", b=2, k=2)
        w2x = view(r_xs, "p (b k d) -> p b k d", b=2, k=2)
        w2_slot = [w2z[:, 0], w2z[:, 1], w2x[:, 0], w2x[:, 1]]
        fng = r_k[:, 0:D]
        sq_d = r_bt[:, 0:D]
        pickS = r_bt[:, D:D + 2 * TT * 2 * W].rearrange("p (b t e r) -> p b t e r", b=2, t=TT, e=2)
        hsel = r_lm[:, 0:2 * KD * 2 * W].rearrange("p (b k e r) -> p b k e r", b=2, k=KD, e=2)
        hid_s = r_lm[:, 2048:2048 + 4 * W].rearrange("p (b f) -> p b f", b=2)
        hid = r_lm[:, 2304:2304 + 4 * W].rearrange("p (b f) -> p b f", b=2)
        y_row = r_st[0:W, 0:2 * D].rearrange("p (b d) -> p b d", b=2)
        y_two = view(r_lm, "p (t c d) -> p t c d", t=TT, c=2)
        stackA, stackB = r_z[:, 2048:2176], r_z[:, 2176:2304]
        wsm = r_z[:, 2304:2304 + KD * (RANK + SH)].rearrange("p (k n) -> p k n", k=KD)
        gkT, wgk2 = r_z[0:RANK + 1, 2688:2688 + T], r_z[0:RANK + 1, 2944:2944 + 512]
        gk_ls = g_sb[:, 1]
        gk_ls = gk_ls.rearrange("p (t d) -> p t d", t=TT)
        late = {}
        at = 0
        for name, dims in (("wr", (KD, 36)), ("rb", (36,)), ("lg", (TT, 36)), ("rt", (24, TT, 8)), ("rt4", (TT, 4, EG)),
                           ("mask", (TT, E)), ("rank1", (TT, E)), ("ohG", (2 * TT, E)), ("ohx", (2 * TT, E)),
                           ("cnt", (4, E)), ("jv", (6, JOBS)), ("jp", (TT, JOBS)),
                           ("ix", (8, 2 * TT)), ("ints", (16,))):
            size = 1
            for d in dims:
                size *= d
            late[name] = r_btm[:, at:at + size]
            if len(dims) > 1:
                letters = "abc"[:len(dims)]
                late[name] = late[name].rearrange("p (" + " ".join(letters) + ") -> p " + " ".join(letters),
                                                  **dict(zip(letters, dims)))
            at += size
        wr, rb, lg, rt, rt4, mask, rank1, ohG, ohx, cnt, jv, jp, ix = (late[k] for k in (
            "wr", "rb", "lg", "rt", "rt4", "mask", "rank1", "ohG", "ohx", "cnt", "jv", "jp", "ix"))
        jt = hT[:].rearrange("p k t -> p (k t)")[:, 0:3 * JOBS * E].rearrange("p (a b) -> p a b", b=E)
        jobs_i = late["ints"][:, 0:JOBS + 1].bitcast(I32)
        rows_i = late["ints"][:, 12:16].bitcast(I32)
        sq = sb("sq", 256)
        newton = sb("newton", 3, 16)
        ident = sb("ident", P)
        same = sb("same", P)
        upto = sb("upto", P)
        after = sb("after", P)
        earlier = sb("earlier", P)
        count = sb("count", W + 1)
        count0, count1 = count[:, 0:W], count[:, 1:W + 1]
        upto1 = sb("upto1", CH)
        inch = sb("inch", 2, P)
        ones = sb("ones", P)
        w_down = sb("w_down", 8)
        cols = sb("cols", NCOL)
        rows = sb("rows", 3, SH)
        cact = sb("cact", KD)
        mod = sb("mod", 48)
        st = sb("st", 16)
        dtb = sb("dtb", 5, TT, SH)
        dt, dA, acum, eacum, dend = (dtb[:, i] for i in range(5))
        dt_abs = sb("dt_abs", TT, SH)
        cdec = sb("cdec", NC, SH)
        gdec = sb("gdec", GH, NC)
        gss = sb("gss", 1, TT, GH)
        sss = sb("sss", 1, TT, SG)

        ps = [ctx.enter_context(nc.psum_tensor(f"ps{i}", [P, 512], F32)) for i in range(8)]

        slot_full = [sem(f"slot_full{i}") for i in range(SLOTS)]
        bank_full = [sem(f"bank_full{i}") for i in range(8)]
        bank_free = [sem(f"bank_free{i}") for i in range(8)]
        w2_full, up_full, silu_up, hid_ok, down_full, y_lo, y_hi, y_stored = (
            [sem(f"{n}{i}") for i in range(4)] for n in ("w2_full", "up_full", "silu_up", "hid_ok", "down_full", "y_lo",
                                                         "y_hi", "y_stored"))
        pick_ok, sel_full, sel_taken = ([sem(f"{n}{i}") for i in range(2)] for n in ("pick_ok", "sel_full", "sel_taken"))
        (jobs_ok, x_free, x_loaded, x_pick, x_sel, x_taken, x_up, x_silu, x_hid, x_down, x_lo, x_hi, x_stored, moe_done,
         rows_ok, y_sum, rows_zeroed) = (sem(n) for n in (
            "jobs_ok x_free x_loaded x_pick x_sel x_taken x_up x_silu x_hid x_down x_lo x_hi x_stored moe_done "
            "rows_ok y_sum rows_zeroed").split())
        y_two_ok = [sem(f"y_two_ok{t}") for t in range(TT)]
        s_stack, s_x, s_small, s_rows, s_wr, s_fng = (sem(n) for n in ("s_stack", "s_x", "s_small", "s_rows", "s_wr", "s_fng"))
        s_const = sem("s_const")
        s_pool = sem("s_pool_chain")
        s_dve = sem("s_dve_chain")
        s_act = sem("s_act_chain")
        (x_sq, xn_done, cols_done, cact_done, hT_done, sm_done, a_exp, dt_sp, dA_done, ones_done, conv_step,
         conv_done, silu_done, gk_in, gk_l, gk_done, gsuf_done, kdec_done, gdec_done, ac_done, eac_done,
         rhs_done, seg_unused, L_done, M_done, gO_sq, oa_done, xdt_done, xdd_done, skip_done, y_done, y_sq,
         ob_done, mod_done, diag_done, x2_done, x2_sq, x2n_done, rt_in, rt_e, rt_in2, rt_e2, mask_ok,
         hs_done, hp_done, hw_done, dg_done, hid_done, y_moe, x3_sq, fin_done, out_done, ada_used, moe_h, ob_used,
         y_evac,) = (sem(n) for n in (
            "x_sq xn_done cols_done cact_done hT_done sm_done a_exp dt_sp dA_done ones_done conv_step "
            "conv_done silu_done gk_in gk_l gk_done gsuf_done kdec_done gdec_done ac_done eac_done rhs_done "
            "seg_unused L_done M_done gO_sq oa_done xdt_done xdd_done skip_done y_done y_sq ob_done mod_done "
            "diag_done x2_done x2_sq x2n_done rt_in rt_e rt_in2 rt_e2 mask_ok hs_done hp_done hw_done dg_done "
            "hid_done y_moe x3_sq fin_done out_done ada_used moe_h ob_used y_evac ").split())

        def mix(name):
            n = MIX_AT[name]
            return ps[4 + n % 4], 4 + n % 4, n // 4

        def mix_wait(eng, name):
            bank, b, turn = mix(name)
            eng.wait_ge(bank_full[b], turn + 1)
            return bank

        def mix_used(name):
            return bank_free[mix(name)[1]]

        def mix_taken(eng, name):
            _, b, turn = mix(name)
            eng.wait_ge(bank_free[b], turn + 1)

        def unit(name, half):
            n = 2 * UNITS.index(name) + half
            return ps[n % 4], n % 4, n // 4

        def unit_wait(eng, name, half):
            bank, b, turn = unit(name, half)
            eng.wait_ge(bank_full[b], turn + 1)
            return bank

        def unit_used(name, half):
            return bank_free[unit(name, half)[1]]

        def unit_taken(eng, name, half):
            _, b, turn = unit(name, half)
            eng.wait_ge(bank_free[b], turn + 1)

        def chunk_used(eng, n):
            kind, i = CHUNKS[n]
            if kind == "ada":
                eng.wait_ge(ada_used, i + 1)
            elif kind == "ob" and i % 2 == 0:
                eng.wait_ge(ob_used, i // 2 + 1)
            else:
                unit_wait(eng, (kind, i // 2 if kind == "ob" else i), 1)

        def wait_turn(eng, sems, i, c, per=1):
            v = (i + (c // len(sems) + 1)) * per
            if not isinstance(v, int) or v > 0:
                eng.wait_ge(sems[c % len(sems)], v)

        def col(name, i=0, n=1):
            return cols[:, COL[name] + i:COL[name] + i + n]

        def heads(ap):
            return ap.rearrange("p (h q) -> p h q", q=SP_)

        def over(ap, n):
            return ap.unsqueeze(len(ap.shape)).to_broadcast([*ap.shape, n])

        w_in2, ada2 = w_in[0], ada_w[0]
        y_rows = nc.dram_tensor("y_rows", [(E + JOBS) * W, D], F32, kind="Internal").ap()

        def chunk_src(kind, i):
            w, at = {"ada": (ada2, 0), "oa": (w_oa[0], 0), "out": (w_out[0], 0)}.get(kind, (w_in2, OFF.get(kind, 0)))
            if kind == "ob":
                return w_ob[0, (i % 2) * D:(i % 2 + 1) * D, (i // 2) * CW:(i // 2 + 1) * CW].rearrange(
                    "(k p) n -> p k n", p=P)
            return w[:, at + i * CW:at + (i + 1) * CW].rearrange("(k p) n -> p k n", p=P)

        block = ctx.enter_context(nc.Block())

        @block.sync
        def _(sp):
            rowsA = conv_w[0].rearrange("w (t p) -> (w t) p", p=P)
            sp.dma_start(stackA, rowsA).then_inc(s_stack, 16)
            at = 0
            for v, n in ((conv_b, 32), (ssm_norm_g, 16), (norm1_g, 8), (norm2_g, 8), (ada_b, 48), (c, 8), (gla_norm_g, 2)):
                sp.dma_start(stackB[at:at + n, :], v[0].rearrange("(t p) -> t p", p=P)).then_inc(s_stack, 16)
                at += n
            sp.dma_start(x_sb[:], x[0].rearrange("(t p) d -> p t d", p=P)).then_inc(s_x, 16)
            sp.dma_start(wsm[:, :, 0:RANK], w_in2[:, OFF["gk"]:OFF["gk"] + RANK].rearrange("(k p) n -> p k n", p=P)
                         ).then_inc(s_small, 16)
            sp.dma_start(wsm[:, :, RANK:], w_in2[:, OFF["dt"]:OFF["dt"] + SH].rearrange("(k p) n -> p k n", p=P)
                         ).then_inc(s_small, 16)
            sp.dma_start(wgk2[0:RANK, :], gla_w_gk2[0]).then_inc(s_small, 16)
            sp.dma_start(wgk2[RANK:RANK + 1, :], gla_b_gk).then_inc(s_small, 16)
            for i, v in enumerate((dt_bias, a_log, d_skip)):
                sp.dma_start(rows[:, i, :], v[0].partition_broadcast(P)).then_inc(s_rows, 16)
            for i, (kind, n) in enumerate(CHUNKS):
                s = i % SLOTS
                if i >= SLOTS:
                    chunk_used(sp, i - SLOTS)
                sp.dma_start(ring[:, s], chunk_src(kind, n)).then_inc(slot_full[s], 16)
                if (kind, n) == ("out", 1):
                    for h in range(2):
                        unit_taken(sp, ("oa", 1), h)
                    sp.dma_start(wr[:, :, 0:4], router_group_w[0].rearrange("(k p) n -> p k n", p=P)).then_inc(s_wr, 16)
                    sp.dma_start(wr[:, :, 4:36], router_expert_w[0].rearrange("(k p) n -> p k n", p=P)).then_inc(s_wr, 16)
                    sp.dma_start(rb[:, 0:4], router_group_b[0].partition_broadcast(P)).then_inc(s_wr, 16)
                    sp.dma_start(rb[:, 4:36], router_expert_b[0].partition_broadcast(P)).then_inc(s_wr, 16)
            base = len(CHUNKS)
            w1v = expert_w1[0].rearrange("g e (k p) f -> (g e) p k f", p=P)
            w3v = expert_w3[0].rearrange("g e (k p) f -> (g e) p k f", p=P)
            w2v = expert_w2[0].rearrange("g e (k p) d -> (g e) p k d", p=P)
            for i in range(8):
                mix_taken(sp, ("obT", i))

            def expert(e, u):
                s = (base + u) % SLOTS
                sp.dma_start(ring[:, s, :, 0:FF], w1v[e]).then_inc(slot_full[s], 16)
                sp.dma_start(ring[:, s, :, FF:2 * FF], w3v[e]).then_inc(slot_full[s], 16)
                sp.dma_start(w2_slot[u], w2v[e]).then_inc(w2_full[u], 16)

            for u in range(4):
                chunk_used(sp, base - SLOTS + u)
                expert(u, u)
            with sp.Fori(1, E // 4) as i:
                for u in range(4):
                    wait_turn(sp, up_full, i, u - 4)
                    wait_turn(sp, down_full, i, u - 4)
                    expert(i * 4 + u, u)
            for k in range(4):
                sp.wait_ge(y_stored[k], 16 * (E // 4))
            sp.wait_ge(jobs_ok, 1)
            sp.wait_ge(rows_zeroed, 16 * (JOBS * W // P))
            sp.sem_inc(x_free, 1)
            extra = sp.value_load(jobs_i[0:1, JOBS:JOBS + 1], min_val=0, max_val=JOBS)
            with sp.If(extra > 0):
                with sp.Fori(1, extra + 1) as j:
                    sp.wait_ge(x_free, j)
                    e = sp.value_load(jobs_i[0:1, bass.ds(j - 1, 1)], min_val=0, max_val=E - 1)
                    sp.dma_start(ring[:, 0, :, 0:FF], w1v[e]).then_inc(x_loaded, 16)
                    sp.dma_start(ring[:, 0, :, FF:2 * FF], w3v[e]).then_inc(x_loaded, 16)
                    sp.dma_start(w2_slot[0], w2v[e]).then_inc(x_loaded, 16)
                    sp.wait_ge(x_lo, j)
                    sp.wait_ge(x_hi, j)
                    sp.dma_start(y_rows[bass.ds(j * W + (E - 1) * W, W), :], y_row[:, 0]).then_inc(x_stored, 16)
                    sp.wait_ge(x_stored, j * 16)
                    sp.sem_inc(x_free, 1)
            sp.sem_inc(moe_done, 1)
            for t in range(TT):
                sp.wait_ge(fin_done, t + 1)
                sp.dma_start(out[0, t * P:(t + 1) * P, :], x_sb[:, t]).then_inc(out_done, 16)
            sp.wait_ge(out_done, 16 * TT)

        @block.gpsimd
        def _(pool):
            n = [0]

            def link(ins):
                n[0] += 1
                ins.then_inc(s_pool, 1)
                pool.wait_ge(s_pool, n[0])

            nc.gpsimd.memset(ones[:], 1.0)
            nc.gpsimd.memset(ident[:], 0.0)
            nc.gpsimd.memset(inch[:], 1.0)
            link(nc.gpsimd.memset(same[:], 1.0))
            link(nc.gpsimd.memset(zeros, 0.0))
            for i in range(JOBS * W // P):
                pool.dma_start(y_rows[E * W + i * P:E * W + (i + 1) * P, :], zeros).then_inc(rows_zeroed, 16)
            link(nc.gpsimd.affine_select(out=ident[:], in_=ident[:], compare_op=ALU.not_equal, fill=1.0, base=0,
                                         pattern=[[-1, P]], channel_multiplier=1))
            for m, w in ((same[:].rearrange("p (j t) -> p j t", j=2), CH), (inch[:], P)):
                link(nc.gpsimd.affine_select(out=m, in_=m, compare_op=ALU.is_ge, fill=0.0, base=0,
                                             pattern=[[-CH, 2], [0, w]], channel_multiplier=1))
                link(nc.gpsimd.affine_select(out=m, in_=m, compare_op=ALU.is_ge, fill=0.0, base=CH - 1,
                                             pattern=[[CH, 2], [0, w]], channel_multiplier=-1))
            link(nc.gpsimd.affine_select(out=upto[:], in_=same[:], compare_op=ALU.is_ge, fill=0.0, base=0,
                                         pattern=[[1, P]], channel_multiplier=-1))
            link(nc.gpsimd.affine_select(out=after[:], in_=same[:], compare_op=ALU.is_ge, fill=0.0, base=-1,
                                         pattern=[[-1, P]], channel_multiplier=1))
            link(nc.gpsimd.memset(earlier[:], 1.0))
            link(nc.gpsimd.affine_select(out=earlier[:], in_=earlier[:], compare_op=ALU.is_ge, fill=0.0, base=-1,
                                         pattern=[[1, P]], channel_multiplier=-1))
            link(nc.gpsimd.iota(count[:], pattern=[[1, W + 1]], base=0, channel_multiplier=0,
                                allow_small_or_imprecise_dtypes=True))
            link(nc.gpsimd.iota(w_down[:], pattern=[[-1, 8]], base=8, channel_multiplier=0,
                                allow_small_or_imprecise_dtypes=True))
            nc.gpsimd.tensor_tensor(upto1[:], upto[:, 0:CH], upto[:, CH:P], ALU.add).then_inc(s_const, 1)
            pool.wait_ge(eac_done, 1)
            pool.wait_ge(s_rows, 48)
            for i in range(4):
                for t in range(TT):
                    mix_taken(pool, ("tr", i, t))
            for j in range(4):
                b = j % 2
                if j == 0:
                    for name in [("gU", NC - 1, 0), ("gU", NC - 1, 1), ("cb", 0), ("cb", 1)]:
                        mix_wait(pool, name)
                if j >= 2:
                    for t in range(TT):
                        mix_wait(pool, ("diag", j - 2, t))
                    mix_wait(pool, ("U", j - 2, 2))
                src = xs[:, :, j * 512:(j + 1) * 512]
                for t in range(TT):
                    h = slice(8 * j, 8 * j + 8)
                    link(nc.gpsimd.tensor_tensor(heads(xdt[:, b, t]), heads(src[:, t]), over(dt[:, t, h], SP_), ALU.mult))
                    nc.gpsimd.tensor_tensor(heads(xdd[:, b, t]), heads(xdt[:, b, t]), over(dend[:, t, h], SP_),
                                            ALU.mult).then_inc(xdd_done, 1)
                    nc.gpsimd.tensor_tensor(heads(src[:, t]), heads(src[:, t]), over(rows[:, 2, h], SP_),
                                            ALU.mult).then_inc(skip_done, 1)
            for t in range(TT):
                unit_taken(pool, ("out", 1), t)
            pool.dma_start(fng, final_norm_g.partition_broadcast(P)).then_inc(s_fng, 16)
            pool.wait_ge(rows_ok, 1)
            pool.wait_ge(moe_done, 1)
            for t in range(TT):
                for c_ in range(2):
                    pool.indirect_dma_start(
                        out=y_two[:, t, c_], out_offset=None, in_=y_rows[:, :],
                        in_offset=bass.IndirectOffsetOnAxis(ap=rows_i[:, 2 * t + c_:2 * t + c_ + 1], axis=0)
                    ).then_inc(y_two_ok[t], 16)

        @block.scalar
        def _(act):
            n = [0]

            def link(ins):
                n[0] += 1
                ins.then_inc(s_act, 1)
                act.wait_ge(s_act, n[0])

            act.wait_ge(s_x, 16)
            for t in range(TT):
                ins = nc.scalar.activation(hT[:].rearrange("p k t -> p (k t)")[:, t * D:(t + 1) * D], x_sb[:, t], ACT.Square,
                                           accum_out=st[:, t:t + 1])
                ins.then_inc(x_sq, 1)
            mix_taken(act, "cols")
            nc.scalar.activation(cact[:], col("c", 0, 8), ACT.Silu).then_inc(cact_done, 1)
            act.wait_ge(s_rows, 48)
            nc.scalar.activation(rows[:, 1, :], rows[:, 1, :], ACT.Exp).then_inc(a_exp, 1)
            act.wait_ge(sm_done, 1)
            link(nc.scalar.activation(dt_abs[:], dt_abs[:], ACT.Exp, scale=-1.0))
            nc.scalar.activation(dt_abs[:], dt_abs[:], ACT.Ln, bias=1.0).then_inc(dt_sp, 1)

            def silu_out(g):
                i, a = g // 2, 2 * (g % 2)
                if i < 4:
                    return xsT[:, i % 2, a:a + 2]
                return (BT if i < 6 else CT)[:, 4 * (i % 2) + a:4 * (i % 2) + a + 2]

            def conv_silu(g):
                act.wait_ge(conv_done, g + 1)
                if 4 <= g < 8:
                    mix_wait(act, ("tr", g // 2 - 2, 1))
                nc.scalar.activation(silu_out(g), acc_cv[:, g % 2], ACT.Silu).then_inc(silu_done, 1)

            for i in range(8):
                for half in range(2):
                    g = 2 * i + half
                    bank = unit_wait(act, ("xbc", i), half)
                    if g >= 2:
                        act.wait_ge(conv_done, g - 1)
                    nc.scalar.copy(u_cv[:, g % 2].rearrange("p a t -> p (a t)"), bank[:]).then_inc(
                        unit_used(("xbc", i), half), 1)
                    if g:
                        conv_silu(g - 1)
                if 1 <= i <= 6:
                    for t in range(TT):
                        bank = mix_wait(act, ("tr", i - 1, t))
                        dst = xs[:, t, (i - 1) * 512:i * 512] if i <= 4 else Btm[:, t, (i - 5) * 512:(i - 4) * 512]
                        nc.scalar.copy(dst, bank[:]).then_inc(mix_used(("tr", i - 1, t)), 1)
            conv_silu(15)

            for t in range(TT):
                bank = unit_wait(act, ("k", 0), t)
                nc.scalar.copy(k_tm[:, t], bank[:]).then_inc(unit_used(("k", 0), t), 1)
            for t in range(TT):
                act.wait_ge(gk_in, t + 1)
                link(nc.scalar.activation(gk_abs, gk_abs, ACT.Exp, scale=-1.0))
                nc.scalar.activation(gk_sp, gk_abs, ACT.Ln, bias=1.0).then_inc(gk_l, 1)
            mix_taken(act, "acum")
            nc.scalar.activation(dend, dend, ACT.Exp)
            nc.scalar.activation(eacum, acum, ACT.Exp)
            nc.scalar.activation(cdec[:], cdec[:], ACT.Exp).then_inc(eac_done, 1)
            for t in range(TT):
                bank = mix_wait(act, ("gsuf", t))
                if t:
                    act.wait_ge(kdec_done, t)
                nc.scalar.activation(gsuf_e, bank[:], ACT.Exp, scale=1.0 / 16).then_inc(mix_used(("gsuf", t)), 1)
            bank = mix_wait(act, "gdec")
            nc.scalar.activation(gdec[:].rearrange("p h c -> p (h c)"), bank[:, 0:GH * NC], ACT.Exp,
                                 scale=1.0 / 16).then_inc(mix_used("gdec"), 1)
            for h in range(2):
                bank = unit_wait(act, ("q", 0), h)
                nc.scalar.mul(qT[:, 2 * h:2 * h + 2].rearrange("p h t -> p (h t)"), bank[:], HK ** -0.5).then_inc(
                    unit_used(("q", 0), h), 1)
            for i in range(2):
                for t in range(TT):
                    bank = unit_wait(act, ("v", i), t)
                    nc.scalar.copy(v_tm[:, t, i * CW:(i + 1) * CW], bank[:]).then_inc(unit_used(("v", i), t), 1)
                for j in range(4):
                    mix_taken(act, ("arow", i, j))
                link(nc.scalar.activation(M[:, i], M[:, i], ACT.Abs))
                nc.scalar.activation(M[:, i], M[:, i], ACT.Exp, scale=-1.0).then_inc(L_done, 1)
            for i in range(2):
                for t in range(TT):
                    bank = unit_wait(act, ("g", i), t)
                    nc.scalar.activation(g_sb[:, t, i * CW:(i + 1) * CW], bank[:], ACT.Silu).then_inc(
                        unit_used(("g", i), t), 1)

            def gla_squares():
                for t in range(TT):
                    for hp in range(2):
                        bank = mix_wait(act, ("gO", t, hp))
                        for a in range(2):
                            if t or hp or a:
                                act.wait_ge(gO_sq, 4 * t + 2 * hp + a)
                            nc.scalar.activation(sq[:], bank[:, a * HV:(a + 1) * HV], ACT.Square,
                                                 accum_out=gss[:, 0, t, 2 * hp + a:2 * hp + a + 1]).then_inc(gO_sq, 1)

            def ssd_squares(j):
                for t in range(TT):
                    act.wait_ge(y_done, 2 * j + t + 1)
                    for a in range(2):
                        g, n_sq = 2 * j + a, 4 * j + 2 * t + a
                        if n_sq:
                            act.wait_ge(y_sq, n_sq)
                        else:
                            act.wait_ge(gO_sq, TT * GH)
                        nc.scalar.activation(sq[:], z_tm[:, t, g * 256:(g + 1) * 256], ACT.Square,
                                             accum_out=sss[:, 0, t, g:g + 1]).then_inc(y_sq, 1)

            for i in range(4):
                for t in range(TT):
                    bank = unit_wait(act, ("z", i), t)
                    nc.scalar.activation(z_tm[:, t, i * CW:(i + 1) * CW], bank[:], ACT.Silu).then_inc(
                        unit_used(("z", i), t), 1)
                if i == 0:
                    gla_squares()
                if i >= 2:
                    ssd_squares(i - 2)
            for i in range(4):
                for h in range(2):
                    bank = unit_wait(act, ("gate", i), h)
                    m = 4 * i + 2 * h
                    nc.scalar.activation(gateT[:, m:m + 2].rearrange("p m t -> p (m t)"), bank[:], ACT.Sigmoid).then_inc(
                        unit_used(("gate", i), h), 1)
                if i < 2:
                    ssd_squares(i + 2)
            for i in range(4):
                bank = mix_wait(act, ("oaT", i))
                for a in range(2):
                    m = 2 * i + a
                    ins = nc.scalar.mul(oaT[:, m], bank[:, a * T:(a + 1) * T], col("gla_g", m % 2))
                ins.then_inc(mix_used(("oaT", i)), 1)
            for i in range(8):
                bank = mix_wait(act, ("obT", i))
                for a in range(2):
                    m = 2 * i + a
                    ins = nc.scalar.mul(obT[:, m], bank[:, a * T:(a + 1) * T], col("ssm_g", m))
                ins.then_inc(mix_used(("obT", i)), 1)
            for t in range(TT):
                unit_taken(act, ("out", 1), t)
            for t in range(TT):
                if t:
                    act.wait_ge(x2_sq, t)
                nc.scalar.activation(sq_d, x_sb[:, t], ACT.Square, accum_out=st[:, 2 + t:3 + t]).then_inc(x2_sq, 1)
            for i in range(4):
                bank = mix_wait(act, ("x2T", i))
                nc.scalar.copy(hT[:, 2 * i:2 * i + 2].rearrange("p k t -> p (k t)"), bank[:]).then_inc(
                    mix_used(("x2T", i)), 1)
            act.wait_ge(rt_in, 1)
            nc.scalar.activation(rt[:, 0, :, 0:4], rt[:, 0, :, 0:4], ACT.Exp).then_inc(rt_e, 1)
            act.wait_ge(rt_in2, 1)
            nc.scalar.activation(rt[:, 12, :, 0:1], rt[:, 12, :, 0:1], ACT.Exp).then_inc(rt_e2, 1)

            def take_selected(i, d):
                wait_turn(act, sel_full, i, d)
                for k in range(2):
                    ins = nc.scalar.copy(hsel[:, d % 2, 4 * k:4 * k + 4].rearrange("p k e r -> p (k e r)"), ps[6 + k][:])
                ins.then_inc(sel_taken[d % 2], 1)

            def silu_of(i, c_):
                wait_turn(act, up_full, i, c_)
                wait_turn(act, hid_ok, i, c_ - 2)
                nc.scalar.activation(hid_s[:, c_ % 2], ps[c_ % 2][:, 0:2 * W], ACT.Silu).then_inc(silu_up[c_ % 4], 1)

            def output_low(i, c_, e):
                wait_turn(act, down_full, i, c_)
                wait_turn(act, y_stored, i, c_ - 2, 16)
                nc.scalar.copy(y_row[:, c_ % 2, 0:512], ps[2 + 2 * (c_ % 2)][0:W, :]).then_inc(y_lo[c_ % 4], 1)
                wait_turn(act, y_lo, i, c_)
                wait_turn(act, y_hi, i, c_)
                act.dma_start(y_rows[bass.ds(e * W, W), :], y_row[:, c_ % 2]).then_inc(y_stored[c_ % 4], 16)

            def four_experts(i, last=False):
                for q in range(2):
                    c_ = 2 * q
                    if not (last and q == 1):
                        take_selected(i, q + 1)
                    silu_of(i, c_ + 1)
                    output_low(i, c_, i * 4 + c_)
                    if not (last and q == 1):
                        silu_of(i, c_ + 2)
                    output_low(i, c_ + 1, i * 4 + (c_ + 1))

            take_selected(0, 0)
            silu_of(0, 0)
            four_experts(0)
            with act.Fori(1, E // 4 - 1) as i:
                four_experts(i)
            four_experts(E // 4 - 1, last=True)
            act.wait_ge(jobs_ok, 1)
            extra = act.value_load(jobs_i[0:1, JOBS:JOBS + 1], min_val=0, max_val=JOBS)
            with act.If(extra > 0):
                with act.Fori(1, extra + 1) as j:
                    act.wait_ge(x_sel, j)
                    for k in range(2):
                        ins = nc.scalar.copy(hsel[:, 0, 4 * k:4 * k + 4, 0, :], ps[6 + k][:, 0:4 * W].rearrange(
                            "p (k r) -> p k r", k=4))
                    ins.then_inc(x_taken, 1)
                    act.wait_ge(x_up, j)
                    nc.scalar.activation(hid_s[:, 0], ps[0][:, 0:2 * W], ACT.Silu).then_inc(x_silu, 1)
                    act.wait_ge(x_down, j)
                    nc.scalar.copy(y_row[:, 0, 0:512], ps[2][0:W, :]).then_inc(x_lo, 1)
            for t in range(TT):
                act.wait_ge(y_sum, t + 1)
                if t:
                    act.wait_ge(x3_sq, t)
                nc.scalar.activation(sq_d, x_sb[:, t], ACT.Square, accum_out=st[:, 4 + t:5 + t]).then_inc(x3_sq, 1)

        @block.vector
        def _(dve):
            n = [0]

            def link(ins):
                n[0] += 1
                ins.then_inc(s_dve, 1)
                dve.wait_ge(s_dve, n[0])

            def rstd(ap, width):
                n_el = ap.free_size()
                m, y, s = (newton[:, i, 0:n_el] for i in range(3))
                if len(ap.shape) == 3:
                    m, y, s = (v.rearrange("p (a b) -> p a b", a=ap.shape[1]) for v in (m, y, s))
                link(nc.vector.tensor_scalar(m, ap, 1.0 / width, EPS, ALU.mult, ALU.add))
                link(nc.vector.tensor_scalar(s.bitcast(I32), m.bitcast(I32), 1, None, ALU.logical_shift_right))
                link(nc.vector.tensor_scalar(y.bitcast(I32), s.bitcast(I32), -1.0, float(0x5F3759DF), ALU.mult, ALU.add))
                for step in range(3):
                    link(nc.vector.tensor_tensor(s, y, y, ALU.mult))
                    link(nc.vector.scalar_tensor_tensor(s, s, -0.5, m, ALU.mult, ALU.mult))
                    link(nc.vector.scalar_tensor_tensor(y if step < 2 else ap, s, 1.5, y, ALU.add, ALU.mult))

            nc.vector.memset(gkT, 1.0).then_inc(ones_done, 1)
            nc.vector.memset(st[:, 12:13], 0.0).then_inc(hid_done, 1)
            bank = mix_wait(dve, "cols")
            nc.vector.tensor_copy(cols[:], bank[:, 0:NCOL]).then_inc(mix_used("cols"), 1)
            mix_taken(dve, "cols")
            dve.wait_ge(x_sq, TT)
            rstd(st[:, 0:TT], D)
            for t in range(TT):
                nc.vector.tensor_scalar(xn[:, t], x_sb[:, t], st[:, t:t + 1], None, ALU.mult).then_inc(xn_done, 1)
            bank = mix_wait(dve, "modA")
            link(nc.vector.tensor_tensor(mod[:, 0:16], bank[:, 0:16], col("ada_b", 0, 16), ALU.add))
            ins = nc.vector.scalar_tensor_tensor(mod[:, 8:16], mod[:, 8:16], 1.0, col("norm1", 0, 8), ALU.add, ALU.mult)
            ins.then_inc(mix_used("modA"), 1)
            mix_taken(dve, "modA")
            for i in range(4):
                bank = mix_wait(dve, ("xT", i))
                for a in range(2):
                    k = 2 * i + a
                    ins = nc.vector.tensor_scalar(hT[:, k], bank[:, a * T:(a + 1) * T], mod[:, 8 + k:9 + k],
                                                  mod[:, k:k + 1], ALU.mult, ALU.add)
                ins.then_inc(mix_used(("xT", i)), 1)
            bank = mix_wait(dve, "small")
            dve.wait_ge(ones_done, 1)
            nc.vector.tensor_copy(gkT[0:RANK, :], bank[0:RANK, 0:T])
            dve.wait_ge(s_rows, 48)
            nc.vector.tensor_tensor(dt, bank[:, T:T + TT * SH].rearrange("p (t h) -> p t h", t=TT),
                                    rows[:, 0:1, :].to_broadcast([P, TT, SH]), ALU.add).then_inc(mix_used("small"), 1)
            mix_taken(dve, "small")
            nc.vector.scalar_tensor_tensor(dt_abs[:], dt, -1.0, dt, ALU.mult, ALU.max).then_inc(sm_done, 1)
            dve.wait_ge(dt_sp, 1)
            link(nc.vector.scalar_tensor_tensor(dt, dt, 0.0, dt_abs[:], ALU.max, ALU.add))
            dve.wait_ge(a_exp, 1)
            nc.vector.scalar_tensor_tensor(dA, dt, -1.0, rows[:, 1:2, :].to_broadcast([P, TT, SH]), ALU.mult,
                                           ALU.mult).then_inc(dA_done, 1)
            step = 0
            for g in range(16):
                unit_taken(dve, ("xbc", g // 2), g % 2)
                if g >= 2:
                    dve.wait_ge(silu_done, g - 1)
                u, acc = u_cv[:, g % 2], acc_cv[:, g % 2]
                for tap in range(TAPS):
                    for a in range(2):
                        m = 2 * g + a
                        w = col("conv_w", (TAPS - 1 - tap) * 32 + m)
                        if tap == 0:
                            ins = nc.vector.tensor_scalar(acc[:, a], u[:, a], w, col("conv_b", m), ALU.mult, ALU.add)
                        else:
                            dve.wait_ge(conv_step, step - 1)
                            ins = nc.vector.scalar_tensor_tensor(acc[:, a, tap:], u[:, a, 0:T - tap], w,
                                                                 acc[:, a, tap:], ALU.mult, ALU.add)
                        if tap < TAPS - 1:
                            ins.then_inc(conv_step, 1)
                            step += 1
                        elif a == 0:
                            ins.then_inc(conv_step, 1)
                            step += 1
                        else:
                            ins.then_inc(conv_done, 1)
            bank = mix_wait(dve, "acum")
            nc.vector.tensor_copy(acum, bank[:, 0:64].rearrange("p (t h) -> p t h", t=TT))
            nc.vector.tensor_copy(dend, bank[:, 64:128].rearrange("p (t h) -> p t h", t=TT))
            nc.vector.tensor_copy(cdec[:].rearrange("p c h -> p (c h)"), bank[:, 128:256]).then_inc(mix_used("acum"), 1)
            mix_taken(dve, "acum")
            for t in range(TT):
                bank = mix_wait(dve, ("gklin", t))
                nc.vector.tensor_copy(gk_ls[:, t], bank[:]).then_inc(mix_used(("gklin", t)), 1)
                mix_taken(dve, ("gklin", t))
                nc.vector.scalar_tensor_tensor(gk_abs, gk_ls[:, t], -1.0, gk_ls[:, t], ALU.mult, ALU.max).then_inc(gk_in, 1)
                dve.wait_ge(gk_l, t + 1)
                nc.vector.scalar_tensor_tensor(gk_ls[:, t], gk_ls[:, t], 0.0, gk_sp, ALU.min, ALU.subtract
                                               ).then_inc(gk_done, 1)
            for t in range(TT):
                mix_taken(dve, ("gsuf", t))
                unit_taken(dve, ("k", 0), t)
                nc.vector.tensor_tensor(k_tm[:, t], k_tm[:, t], gsuf_e, ALU.mult).then_inc(kdec_done, 1)
            dve.wait_ge(s_const, 1)
            for t in range(TT):
                if t:
                    for j in range(4):
                        mix_wait(dve, ("arow", t - 1, j))
                nc.vector.tensor_tensor(rhsL, over(dA[:, t], CH), upto1[:].unsqueeze(1).to_broadcast([P, SH, CH]),
                                        ALU.mult).then_inc(rhs_done, 1)
                if t == 0:
                    dve.wait_ge(silu_done, 16)
                    for tt in range(TT):
                        mix_taken(dve, ("tr", 5, tt))
                for j in range(4):
                    bank = mix_wait(dve, ("arow", t, j))
                    ins = nc.vector.tensor_tensor(M[:, t, 8 * j:8 * j + 8], bank[:].rearrange("p (h s) -> p h s", s=CH),
                                                  over(acum[:, t, 8 * j:8 * j + 8], CH), ALU.subtract)
                    ins.then_inc(mix_used(("arow", t, j)), 1)
            for t in range(TT):
                bank = mix_wait(dve, ("cb", t))
                dve.wait_ge(L_done, t + 1)
                Mt = M[:, t].rearrange("p (g r) s -> p g r s", g=SG)
                cb = bank[:].rearrange("p (g s) -> p g s", g=SG).unsqueeze(2).to_broadcast([P, SG, 4, CH])
                nc.vector.tensor_tensor(Mt, Mt, cb, ALU.mult).then_inc(mix_used(("cb", t)), 1)
            dve.wait_ge(rows_zeroed, 16 * (JOBS * W // P))
            mix_taken(dve, "gdec")
            for c_ in range(NC):
                for hp in range(2):
                    bank = mix_wait(dve, ("gU", c_, hp))
                    if c_:
                        mix_taken(dve, ("gU", c_ - 1, hp))
                    for a in range(2):
                        h = 2 * hp + a
                        u = bank[:, a * HV:(a + 1) * HV]
                        if c_ == 0:
                            ins = nc.vector.tensor_copy(gla_st[:, 0, h], u)
                        else:
                            ins = nc.vector.scalar_tensor_tensor(gla_st[:, c_, h], gla_st[:, c_ - 1, h],
                                                                 gdec[:, h, c_:c_ + 1], u, ALU.mult, ALU.add)
                    ins.then_inc(mix_used(("gU", c_, hp)), 1)
            for i in range(2):
                for t in range(TT):
                    unit_taken(dve, ("g", i), t)
            for t in range(TT):
                for hp in range(2):
                    bank = mix_wait(dve, ("gO", t, hp))
                    dve.wait_ge(gO_sq, 4 * t + 2 * hp + 2)
                    rstd(gss[:, 0, t, 2 * hp:2 * hp + 2], HV)
                    for a in range(2):
                        h = 2 * hp + a
                        o = g_sb[:, t, h * HV:(h + 1) * HV]
                        ins = nc.vector.scalar_tensor_tensor(o, bank[:, a * HV:(a + 1) * HV], gss[:, 0, t, h:h + 1], o,
                                                             ALU.mult, ALU.mult)
                    ins.then_inc(mix_used(("gO", t, hp)), 1)
            dve.wait_ge(eac_done, 1)
            for j in range(4):
                hs = slice(8 * j, 8 * j + 8)
                for c_ in range(3):
                    bank = mix_wait(dve, ("U", j, c_))
                    if c_ == 0:
                        ins = nc.vector.tensor_copy(r_pv[:, 0], bank[:])
                    else:
                        link(nc.vector.tensor_tensor(heads(r_pv[:, c_]), heads(r_pv[:, c_ - 1]), over(cdec[:, c_, hs], SP_),
                                                     ALU.mult))
                        ins = nc.vector.tensor_tensor(r_pv[:, c_], r_pv[:, c_], bank[:], ALU.add)
                    ins.then_inc(mix_used(("U", j, c_)), 1)
                    mix_taken(dve, ("U", j, c_))
                dve.wait_ge(skip_done, 2 * j + 2)
                for t in range(TT):
                    lo = CH if t == 0 else 0
                    off = mix_wait(dve, ("off", j, t))
                    nc.vector.tensor_tensor(heads(y_off[lo:, t]), heads(off[lo:, :]), over(eacum[lo:, t, hs], SP_),
                                            ALU.mult).then_inc(mix_used(("off", j, t)), 1)
                for t in range(TT):
                    lo = CH if t == 0 else 0
                    dg = mix_wait(dve, ("diag", j, t))
                    nc.vector.tensor_tensor(y_tmp[:, t], dg[:], xs[:, t, j * 512:(j + 1) * 512], ALU.add).then_inc(
                        mix_used(("diag", j, t)), 1)
                    mix_taken(dve, ("diag", j, t))
                    mix_taken(dve, ("off", j, t))
                    link(nc.vector.tensor_tensor(y_tmp[lo:, t], y_tmp[lo:, t], y_off[lo:, t], ALU.add))
                    unit_taken(dve, ("z", j), t)
                    z = z_tm[:, t, j * 512:(j + 1) * 512]
                    nc.vector.tensor_tensor(z, y_tmp[:, t], z, ALU.mult).then_inc(y_done, 1)
            dve.wait_ge(y_sq, TT * SG)
            rstd(sss[:, 0], 256)
            for t in range(TT):
                for g in range(SG):
                    o = z_tm[:, t, g * 256:(g + 1) * 256]
                    ins = nc.vector.tensor_scalar(o, o, sss[:, 0, t, g:g + 1], None, ALU.mult)
                ins.then_inc(ob_done, 1)
            bank = mix_wait(dve, "modB")
            link(nc.vector.tensor_tensor(mod[:, 16:48], bank[:, 0:32], col("ada_b", 16, 32), ALU.add))
            nc.vector.scalar_tensor_tensor(mod[:, 32:40], mod[:, 32:40], 1.0, col("norm2", 0, 8), ALU.add,
                                           ALU.mult).then_inc(mix_used("modB"), 1)
            mix_taken(dve, "modB")
            for w in range(4):
                for h in range(2):
                    at = (16, 24, 32, 40)[w] + 4 * h
                    nc.vector.tensor_tensor(diag[:, h].rearrange("p (k q) -> p k q", k=4),
                                            ident[:].unsqueeze(1).to_broadcast([P, 4, P]), over(mod[:, at:at + 4], P),
                                            ALU.mult).then_inc(diag_done, 1)
                for h in range(2):
                    bank = mix_wait(dve, ("gtb", w, h))
                    nc.vector.tensor_copy((gt1b, sh2b, s2b, gt2b)[w][:, h * 512:(h + 1) * 512], bank[:]).then_inc(
                        mix_used(("gtb", w, h)), 1)
            for i in range(4):
                for h in range(2):
                    unit_taken(dve, ("gate", i), h)
            for name in ("oa", "ob"):
                for i in range(2):
                    for h in range(2):
                        bank = unit_wait(dve, (name, i), h)
                        m = 4 * i + 2 * h
                        dst = mT[:, m:m + 2].rearrange("p m t -> p (m t)")
                        if name == "oa":
                            ins = nc.vector.tensor_tensor(dst, bank[:], gateT[:, m:m + 2].rearrange("p m t -> p (m t)"),
                                                          ALU.mult)
                        else:
                            link(nc.vector.tensor_tensor(m_tmp, bank[:], gateT[:, KD + m:KD + m + 2].rearrange(
                                "p m t -> p (m t)"), ALU.mult))
                            ins = nc.vector.tensor_tensor(dst, dst, m_tmp, ALU.add)
                        ins.then_inc(unit_used((name, i), h), 1)
                        unit_taken(dve, (name, i), h)
            for i in range(2):
                for t in range(TT):
                    bank = unit_wait(dve, ("out", i), t)
                    xs_ = x_sb[:, t, i * CW:(i + 1) * CW]
                    link(nc.vector.tensor_tensor(m_tmp, bank[:], gt1b[:, i * CW:(i + 1) * CW], ALU.mult))
                    ins = nc.vector.tensor_tensor(xs_, xs_, m_tmp, ALU.add)
                    ins.then_inc(unit_used(("out", i), t), 1)
                    unit_taken(dve, ("out", i), t)
            dve.wait_ge(x2_sq, TT)
            rstd(st[:, 2:4], D)
            for t in range(TT):
                link(nc.vector.scalar_tensor_tensor(h2[:, t], x_sb[:, t], st[:, 2 + t:3 + t], s2b, ALU.mult, ALU.mult))
                nc.vector.tensor_tensor(h2[:, t], h2[:, t], sh2b, ALU.add).then_inc(x2n_done, 1)
            bank = mix_wait(dve, "router")
            dve.wait_ge(s_wr, 64)
            nc.vector.tensor_tensor(lg, bank[:, 0:TT * 36].rearrange("p (t n) -> p t n", t=TT),
                                    rb.unsqueeze(1).to_broadcast([P, TT, 36]), ALU.add).then_inc(mix_used("router"), 1)
            mix_taken(dve, "router")
            R = [rt[:, i] for i in range(24)]

            def pick(dst, vals, top, w, tmp):
                link(nc.vector.tensor_tensor(tmp[:, :, 0:w], vals, top.to_broadcast([P, TT, w]), ALU.is_equal))
                link(nc.vector.tensor_tensor(tmp[:, :, 0:w], tmp[:, :, 0:w],
                                             w_down[:, 0:w].unsqueeze(1).to_broadcast([P, TT, w]), ALU.mult))
                link(nc.vector.reduce_max(R[23][:, :, 0:1], tmp[:, :, 0:w], AX_X))
                link(nc.vector.tensor_tensor(dst, tmp[:, :, 0:w], R[23][:, :, 0:1].to_broadcast([P, TT, w]), ALU.is_equal))

            link(nc.vector.reduce_max(R[1][:, :, 0:1], lg[:, :, 0:4], AX_X))
            pick(R[2][:, :, 0:4], lg[:, :, 0:4], R[1][:, :, 0:1], 4, R[3])
            nc.vector.tensor_tensor(R[0][:, :, 0:4], lg[:, :, 0:4], R[1][:, :, 0:1].to_broadcast([P, TT, 4]),
                                    ALU.subtract).then_inc(rt_in, 1)
            link(nc.vector.tensor_tensor(rt4, lg[:, :, 4:36].rearrange("p t (g e) -> p t g e", g=4),
                                         over(R[2][:, :, 0:4], EG), ALU.mult))
            link(nc.vector.reduce_sum(R[4], rt4.rearrange("p t g e -> p t e g"), AX_X))
            link(nc.vector.reduce_max(R[5][:, :, 0:1], R[4], AX_X))
            link(nc.vector.tensor_tensor(R[6], R[4], R[5][:, :, 0:1].to_broadcast([P, TT, EG]), ALU.subtract))
            link(nc.vector.memset(R[7][:, :, 0:1], 0.0))
            pick(R[8], R[6], R[7][:, :, 0:1], EG, R[9])
            link(nc.vector.scalar_tensor_tensor(R[10], R[8], -1e30, R[6], ALU.mult, ALU.add))
            link(nc.vector.reduce_max(R[11][:, :, 0:1], R[10], AX_X))
            nc.vector.tensor_copy(R[12][:, :, 0:1], R[11][:, :, 0:1]).then_inc(rt_in2, 1)
            pick(R[13], R[10], R[11][:, :, 0:1], EG, R[14])
            dve.wait_ge(rt_e, 1)
            link(nc.vector.reduce_sum(R[15][:, :, 0:1], R[0][:, :, 0:4], AX_X))
            dve.wait_ge(rt_e2, 1)
            link(nc.vector.tensor_scalar(R[16][:, :, 0:1], R[12][:, :, 0:1], 1.0, None, ALU.add))
            link(nc.vector.tensor_tensor(R[16][:, :, 0:1], R[16][:, :, 0:1], R[15][:, :, 0:1], ALU.mult))
            link(nc.vector.reciprocal(R[17][:, :, 0:1], R[16][:, :, 0:1]))
            link(nc.vector.tensor_tensor(R[18][:, :, 0:1], R[17][:, :, 0:1], R[12][:, :, 0:1], ALU.mult))
            link(nc.vector.tensor_tensor(R[19], R[8], R[13], ALU.add))
            nc.vector.tensor_tensor(mask.rearrange("p t (g e) -> p t g e", g=4), over(R[2][:, :, 0:4], EG),
                                    R[19].unsqueeze(2).to_broadcast([P, TT, 4, EG]), ALU.mult).then_inc(mask_ok, 1)
            bank = mix_wait(dve, "pos")
            dve.wait_ge(mask_ok, 1)
            nc.vector.scalar_tensor_tensor(rank1, bank[:, 0:TT * E].rearrange("p (t e) -> p t e", t=TT), 1.0, mask,
                                           ALU.add, ALU.mult)
            link(nc.vector.tensor_copy(cnt[:, 0], bank[:, TT * E:(TT + 1) * E]))

            def pick(i, d, pair):
                wait_turn(dve, sel_full, i, d - 2)
                nc.vector.tensor_tensor(pickS[:, d % 2], over(rank1[:, :, bass.ds(pair * 2, 2)], W),
                                        count1.unsqueeze(1).unsqueeze(1).to_broadcast([P, TT, 2, W]),
                                        ALU.is_equal).then_inc(pick_ok[d % 2], 1)

            pick(0, 0, 0)
            pick(0, 1, 1)
            need, upto_e, before_e = cnt[:, 1], cnt[:, 2], cnt[:, 3]
            link(nc.vector.tensor_scalar(need, cnt[:, 0], W + 0.5, None, ALU.is_ge))
            for n_w in range(2, T // W):
                link(nc.vector.scalar_tensor_tensor(need, cnt[:, 0], n_w * W + 0.5, need, ALU.is_ge, ALU.add))
            link(nc.vector.tensor_tensor_scan(upto_e, need, need, 0.0, ALU.add, ALU.bypass))
            link(nc.vector.tensor_tensor(before_e, upto_e, need, ALU.subtract))
            wide = lambda ap: ap.unsqueeze(1).to_broadcast([P, JOBS, E])
            nth = over(count0[:, 0:JOBS], E)
            of_job, tmp_j, tmp_k = (jt[:, i * JOBS:(i + 1) * JOBS] for i in range(3))
            link(nc.vector.tensor_tensor(of_job, wide(before_e), nth, ALU.is_le))
            link(nc.vector.tensor_tensor(tmp_j, wide(upto_e), nth, ALU.is_gt))
            link(nc.vector.tensor_tensor(of_job, of_job, tmp_j, ALU.mult))
            link(nc.vector.tensor_tensor(tmp_j, of_job, wide(count0[:, 0:E]), ALU.mult))
            link(nc.vector.reduce_sum(jv[:, 0], tmp_j, AX_X))
            link(nc.vector.tensor_tensor(tmp_k, of_job, wide(before_e), ALU.mult))
            link(nc.vector.reduce_sum(jv[:, 1], tmp_k, AX_X))
            link(nc.vector.tensor_tensor(jv[:, 2], count1[:, 0:JOBS], jv[:, 1], ALU.subtract))
            for t in range(TT):
                link(nc.vector.tensor_tensor(tmp_j, of_job, wide(rank1[:, t]), ALU.mult))
                link(nc.vector.reduce_sum(jv[:, 3], tmp_j, AX_X))
                link(nc.vector.scalar_tensor_tensor(jp[:, t], jv[:, 2], -float(W), jv[:, 3], ALU.mult, ALU.add))
            nc.vector.tensor_copy(jobs_i[:, 0:JOBS], jv[:, 0])
            nc.vector.tensor_copy(jobs_i[:, JOBS:JOBS + 1], upto_e[:, E - 1:E]).then_inc(jobs_ok, 1)
            for c_, hot in enumerate((R[8], R[13])):
                for t in range(TT):
                    link(nc.vector.tensor_tensor(ohG[:, 2 * t + c_].rearrange("p (g e) -> p g e", g=4),
                                                 over(R[2][:, t, 0:4], EG),
                                                 hot[:, t].unsqueeze(1).to_broadcast([P, 4, EG]), ALU.mult))
            by_tok = lambda ap: ap.unsqueeze(1).to_broadcast([P, 2 * TT, E])
            ohx4 = ohx.rearrange("p (t c) e -> p t c e", t=TT)
            ohG4 = ohG.rearrange("p (t c) e -> p t c e", t=TT)
            link(nc.vector.tensor_tensor(ohx4, ohG4, rank1.unsqueeze(2).to_broadcast([P, TT, 2, E]), ALU.mult))
            link(nc.vector.reduce_sum(ix[:, 0], ohx, AX_X))
            link(nc.vector.tensor_tensor(ohx, ohG, by_tok(count0[:, 0:E]), ALU.mult))
            link(nc.vector.reduce_sum(ix[:, 1], ohx, AX_X))
            link(nc.vector.tensor_tensor(ohx, ohG, by_tok(before_e), ALU.mult))
            link(nc.vector.reduce_sum(ix[:, 2], ohx, AX_X))
            link(nc.vector.tensor_scalar(ix[:, 3], ix[:, 0], W + 0.5, None, ALU.is_ge))
            link(nc.vector.scalar_tensor_tensor(ix[:, 4], ix[:, 2], float(E - 1), ix[:, 1], ALU.add, ALU.subtract))
            link(nc.vector.tensor_tensor(ix[:, 4], ix[:, 4], ix[:, 3], ALU.mult))
            link(nc.vector.tensor_tensor(ix[:, 4], ix[:, 4], ix[:, 1], ALU.add))
            link(nc.vector.scalar_tensor_tensor(ix[:, 4], ix[:, 4], float(W), ix[:, 0], ALU.mult, ALU.add))
            link(nc.vector.tensor_scalar(ix[:, 4], ix[:, 4], -1.0, None, ALU.add))
            nc.vector.tensor_copy(rows_i, ix[:, 4]).then_inc(rows_ok, 1)

            def hidden(i, c_):
                wait_turn(dve, silu_up, i, c_)
                nc.vector.tensor_tensor(hid[:, c_ % 2], ps[c_ % 2][:, 2 * W:4 * W], hid_s[:, c_ % 2], ALU.mult).then_inc(
                    hid_ok[c_ % 4], 1)

            def output_high(i, c_):
                wait_turn(dve, down_full, i, c_)
                wait_turn(dve, y_stored, i, c_ - 2, 16)
                nc.vector.tensor_copy(y_row[:, c_ % 2, 512:], ps[3 + 2 * (c_ % 2)][0:W, :]).then_inc(y_hi[c_ % 4], 1)

            def four_experts(i, last=False):
                for q in range(2):
                    c_ = 2 * q
                    if not last:
                        pick(i, q + 2, i * 2 + (q + 2))
                    hidden(i, c_ + 1)
                    output_high(i, c_)
                    if not (last and q == 1):
                        hidden(i, c_ + 2)
                    output_high(i, c_ + 1)

            hidden(0, 0)
            four_experts(0)
            with dve.Fori(1, E // 4 - 1) as i:
                four_experts(i)
            four_experts(E // 4 - 1, last=True)
            dve.wait_ge(jobs_ok, 1)
            extra = dve.value_load(jobs_i[0:1, JOBS:JOBS + 1], min_val=0, max_val=JOBS)
            with dve.If(extra > 0):
                with dve.Fori(1, extra + 1) as j:
                    dve.wait_ge(x_free, j)
                    nc.vector.tensor_tensor(pickS[:, 0, :, 0, :], jp[:, :, bass.ds(j - 1, 1)].to_broadcast([P, TT, W]), count1.unsqueeze(1).to_broadcast([P, TT, W]), ALU.is_equal
                        ).then_inc(x_pick, 1)
                    dve.wait_ge(x_silu, j)
                    nc.vector.tensor_tensor(hid[:, 0], ps[0][:, 2 * W:4 * W], hid_s[:, 0], ALU.mult).then_inc(x_hid, 1)
                    dve.wait_ge(x_down, j)
                    nc.vector.tensor_copy(y_row[:, 0, 512:], ps[3][0:W, :]).then_inc(x_hi, 1)
            for t in range(TT):
                dve.wait_ge(y_two_ok[t], 32)
                link(nc.vector.tensor_scalar(y_two[:, t, 0], y_two[:, t, 0], R[17][:, t, 0:1], None, ALU.mult))
                link(nc.vector.scalar_tensor_tensor(y_two[:, t, 0], y_two[:, t, 1], R[18][:, t, 0:1], y_two[:, t, 0],
                                                    ALU.mult, ALU.add))
                link(nc.vector.tensor_tensor(y_two[:, t, 0], y_two[:, t, 0], gt2b, ALU.mult))
                nc.vector.tensor_tensor(x_sb[:, t], x_sb[:, t], y_two[:, t, 0], ALU.add).then_inc(y_sum, 1)
            dve.wait_ge(s_fng, 16)
            for t in range(TT):
                dve.wait_ge(x3_sq, t + 1)
                rstd(st[:, 4 + t:5 + t], D)
                nc.vector.scalar_tensor_tensor(x_sb[:, t], x_sb[:, t], st[:, 4 + t:5 + t], fng, ALU.mult,
                                               ALU.mult).then_inc(fin_done, 1)

        @block.tensor
        def _(pe):
            def begin(name):
                bank, b, turn = mix(name)
                if turn:
                    pe.wait_ge(bank_free[b], turn)
                return bank

            def full(name):
                return bank_full[mix(name)[1]]

            def load_wait(i):
                pe.wait_ge(slot_full[i % SLOTS], 16 * (i // SLOTS + 1))
                return ring[:, i % SLOTS]

            def mm(o, l, r, start=True, stop=True):
                return nc.tensor.matmul(o, l, r, start=start, stop=stop)

            def modulation(lo, hi, name):
                bank = begin(name)
                for i in range(lo, hi):
                    n = CHUNK_AT["ada", i]
                    w = load_wait(n)
                    for m in range(4):
                        at = 4 * (i - lo) + m
                        for k in range(KD):
                            ins = mm(bank[:, at:at + 1], w[:, k, m * P:(m + 1) * P], cact[:, k:k + 1], k == 0, k == KD - 1)
                    ins.then_inc(ada_used, 1)
                mm(bank[:, 511:512], ident[:], ones[:, 0:1]).then_inc(full(name), 1)

            def channel_major(u, chunk, src, halves=(0, 1), first=True, last=True):
                w = load_wait(chunk)
                for half in halves:
                    bank, b, turn = unit(u, half)
                    if first and turn:
                        pe.wait_ge(bank_free[b], turn)
                    for a in range(2):
                        m = 2 * half + a
                        for k in range(KD):
                            ins = mm(bank[:, a * T:(a + 1) * T], w[:, k, m * P:(m + 1) * P], src[:, k],
                                     first and k == 0, last and k == KD - 1)
                    if last and half == 0:
                        ins.then_inc(bank_full[b], 1)
                return ins

            def token_major(u, chunk, src):
                w = load_wait(chunk)
                for t in range(TT):
                    bank, b, turn = unit(u, t)
                    if turn:
                        pe.wait_ge(bank_free[b], turn)
                    for k in range(KD):
                        ins = mm(bank[:], src[:, k, t * P:(t + 1) * P], w[:, k], k == 0, k == KD - 1)
                    if t == 0:
                        ins.then_inc(bank_full[b], 1)
                return ins

            def close(u, chunk, ins):
                ins.then_inc(bank_full[unit(u, 1)[1]], 1)

            def project(u, channels):
                n = CHUNK_AT[u]
                close(u, n, (channel_major if channels else token_major)(u, n, hT))

            def transposed(name, pieces, rows=P):
                bank = begin(name)
                at = 0
                for src in pieces:
                    ins = nc.tensor.transpose(bank[:, at:at + P], src, ident[:])
                    at += P
                ins.then_inc(full(name), 1)

            pe.wait_ge(s_stack, 16 * 8)
            pe.wait_ge(s_const, 1)
            bank = begin("cols")
            nc.tensor.transpose(bank[:, 0:P], stackA, ident[:])
            nc.tensor.transpose(bank[:, P:NCOL], stackB[0:NCOL - P, :], ident[0:NCOL - P, 0:NCOL - P]).then_inc(
                full("cols"), 1)
            pe.wait_ge(cact_done, 1)
            modulation(0, 4, "modA")
            pe.wait_ge(xn_done, TT)
            for i in range(4):
                transposed(("xT", i), [xn[:, t, (2 * i + a) * P:(2 * i + a + 1) * P] for a in range(2) for t in range(TT)])
            for i in range(4):
                mix_taken(pe, ("xT", i))
            pe.wait_ge(s_small, 64)
            bank = begin("small")
            for k in range(KD):
                mm(bank[0:RANK, 0:T], wsm[:, k, 0:RANK], hT[:, k], k == 0, k == KD - 1)
            for t in range(TT):
                for k in range(KD):
                    ins = mm(bank[:, T + t * SH:T + (t + 1) * SH], hT[:, k, t * P:(t + 1) * P], wsm[:, k, RANK:], k == 0,
                             k == KD - 1)
            ins.then_inc(full("small"), 1)

            for i in range(8):
                project(("xbc", i), True)
                if 1 <= i <= 6:
                    pe.wait_ge(silu_done, 2 * i)
                    src = xsT[:, (i - 1) % 2] if i <= 4 else BT[:, 4 * (i - 5):4 * (i - 4)]
                    for t in range(TT):
                        transposed(("tr", i - 1, t), [src[:, m, t * P:(t + 1) * P] for m in range(4)])

            project(("k", 0), False)
            pe.wait_ge(dA_done, 1)
            bank = begin("acum")
            for t in range(TT):
                mm(bank[:, t * SH:(t + 1) * SH], upto[:], dA[:, t])
                mm(bank[:, 64 + t * SH:64 + (t + 1) * SH], after[:], dA[:, t])
                for a in range(2):
                    ins = mm(bank[:, 128 + (2 * t + a) * SH:128 + (2 * t + a + 1) * SH], inch[:, a], dA[:, t])
            ins.then_inc(full("acum"), 1)
            for t in range(TT):
                mm(begin(("gklin", t))[:], gkT[:, t * P:(t + 1) * P], wgk2).then_inc(full(("gklin", t)), 1)
            project(("q", 0), True)
            pe.wait_ge(gk_done, TT)
            for t in range(TT):
                mm(begin(("gsuf", t))[:], after[:], gk_ls[:, t]).then_inc(full(("gsuf", t)), 1)
            bank = begin("gdec")
            for h in range(GH):
                for t in range(TT):
                    at = h * NC + 2 * t
                    ins = mm(bank[:, at:at + 2], gk_ls[:, t, h * HK:(h + 1) * HK], inch[:, :, 0])
            ins.then_inc(full("gdec"), 1)

            def rows_of_sums(t):
                pe.wait_ge(rhs_done, t + 1)
                for j in range(4):
                    mm(begin(("arow", t, j))[:], same[:], rhsL[:, 8 * j:8 * j + 8]).then_inc(full(("arow", t, j)), 1)

            project(("v", 0), False)
            rows_of_sums(0)
            project(("v", 1), False)
            rows_of_sums(1)
            pe.wait_ge(silu_done, 16)
            for t in range(TT):
                bank = begin(("cb", t))
                for a in range(2):
                    cs = slice(t * P + a * CH, t * P + (a + 1) * CH)
                    for g in range(SG):
                        ins = mm(bank[a * CH:(a + 1) * CH, g * CH:(g + 1) * CH], BT[:, g, cs], CT[:, g, cs])
                ins.then_inc(full(("cb", t)), 1)

            def gla_updates(c_):
                t, lo = c_ // 2, (c_ % 2) * CH
                for hp in range(2):
                    bank = begin(("gU", c_, hp))
                    for a in range(2):
                        h = 2 * hp + a
                        ins = mm(bank[:, a * HV:(a + 1) * HV], k_tm[lo:lo + CH, t, h * HK:(h + 1) * HK],
                                 v_tm[lo:lo + CH, t, h * HV:(h + 1) * HV])
                    ins.then_inc(full(("gU", c_, hp)), 1)

            def gla_outputs():
                for t in range(TT):
                    for hp in range(2):
                        bank = begin(("gO", t, hp))
                        for a in range(2):
                            c_ = 2 * t + a
                            for b in range(2):
                                h = 2 * hp + b
                                mix_taken(pe, ("gU", c_, hp))
                                ins = mm(bank[a * CH:(a + 1) * CH, b * HV:(b + 1) * HV], qT[:, h, c_ * CH:(c_ + 1) * CH],
                                         gla_st[:, c_, h])
                        ins.then_inc(full(("gO", t, hp)), 1)

            def ssd(j):
                pe.wait_ge(xdd_done, 2 * (j + 1))
                for c_ in range(3):
                    t, lo = c_ // 2, (c_ % 2) * CH
                    bank = begin(("U", j, c_))
                    for a in range(2):
                        g = 2 * j + a
                        ins = mm(bank[:, a * 256:(a + 1) * 256], Btm[lo:lo + CH, t, g * NS:(g + 1) * NS],
                                 xdd[lo:lo + CH, j % 2, t, a * 256:(a + 1) * 256])
                    ins.then_inc(full(("U", j, c_)), 1)
                for t in range(TT):
                    bank = begin(("off", j, t))
                    for b in range(2):
                        c_ = 2 * t + b
                        if c_ == 0:
                            continue
                        mix_taken(pe, ("U", j, c_ - 1))
                        for a in range(2):
                            g = 2 * j + a
                            ins = mm(bank[b * CH:(b + 1) * CH, a * 256:(a + 1) * 256], CT[:, g, c_ * CH:(c_ + 1) * CH],
                                     r_pv[:, c_ - 1, a * 256:(a + 1) * 256])
                    ins.then_inc(full(("off", j, t)), 1)
                for t in range(TT):
                    mix_taken(pe, ("cb", t))
                    bank = begin(("diag", j, t))
                    for b in range(2):
                        part = slice(b * CH, (b + 1) * CH)
                        for h in range(8):
                            ins = mm(bank[part, h * SP_:(h + 1) * SP_], M[part, t, 8 * j + h],
                                     xdt[part, j % 2, t, h * SP_:(h + 1) * SP_])
                    ins.then_inc(full(("diag", j, t)), 1)

            for i in range(2):
                project(("g", i), False)
                if i == 0:
                    pe.wait_ge(kdec_done, TT)
                    for name in (("v", 0), ("v", 1)):
                        for t in range(TT):
                            unit_taken(pe, name, t)
                for c_ in (2 * i, 2 * i + 1):
                    gla_updates(c_)
            for i in range(4):
                project(("z", i), False)
                if i == 0:
                    for h in range(2):
                        unit_taken(pe, ("q", 0), h)
                    gla_outputs()
                else:
                    ssd(i - 1)
            for i in range(4):
                project(("gate", i), True)
                if i == 0:
                    ssd(3)
                if i == 1:
                    for t in range(TT):
                        for hp in range(2):
                            mix_taken(pe, ("gO", t, hp))
                    for m in range(4):
                        transposed(("oaT", m), [g_sb[:, t, (2 * m + a) * P:(2 * m + a + 1) * P] for a in range(2)
                                                for t in range(TT)])
                if i == 3:
                    pe.wait_ge(ob_done, TT)
                    for m in range(8):
                        transposed(("obT", m), [z_tm[:, t, (2 * m + a) * P:(2 * m + a + 1) * P] for a in range(2)
                                                for t in range(TT)])
            modulation(4, 12, "modB")
            for w in range(4):
                for h in range(2):
                    pe.wait_ge(diag_done, 2 * w + h + 1)
                    mm(begin(("gtb", w, h))[:], ones[:], diag[:, h]).then_inc(full(("gtb", w, h)), 1)
            for i in range(4):
                mix_taken(pe, ("oaT", i))
            for i in range(2):
                n = CHUNK_AT["oa", i]
                close(("oa", i), n, channel_major(("oa", i), n, oaT))
            for i in range(8):
                mix_taken(pe, ("obT", i))
            for i in range(2):
                n0, n1 = CHUNK_AT["ob", 2 * i], CHUNK_AT["ob", 2 * i + 1]
                w = [load_wait(n0), load_wait(n1)]
                for half in range(2):
                    bank, b, turn = unit(("ob", i), half)
                    pe.wait_ge(bank_free[b], turn)
                    for a in range(2):
                        m = 2 * half + a
                        for k in range(2 * KD):
                            ins = mm(bank[:, a * T:(a + 1) * T], w[k // KD][:, k % KD, m * P:(m + 1) * P], obT[:, k],
                                     k == 0, k == 2 * KD - 1)
                            if half == 1 and a == 1 and k == KD - 1:
                                ins.then_inc(ob_used, 1)
                    if half == 0:
                        ins.then_inc(bank_full[b], 1)
                close(("ob", i), n1, ins)
            for i in range(2):
                for h in range(2):
                    unit_taken(pe, ("ob", i), h)
            for i in range(2):
                n = CHUNK_AT["out", i]
                close(("out", i), n, token_major(("out", i), n, mT))
            pe.wait_ge(x2n_done, TT)
            for i in range(4):
                transposed(("x2T", i), [h2[:, t, (2 * i + a) * P:(2 * i + a + 1) * P] for a in range(2) for t in range(TT)])
            for i in range(4):
                mix_taken(pe, ("x2T", i))
            pe.wait_ge(s_wr, 64)
            bank = begin("router")
            for t in range(TT):
                for k in range(KD):
                    ins = mm(bank[:, t * 36:(t + 1) * 36], hT[:, k, t * P:(t + 1) * P], wr[:, k], k == 0, k == KD - 1)
            ins.then_inc(full("router"), 1)
            pe.wait_ge(mask_ok, 1)
            bank = begin("pos")
            mm(bank[:, 0:E], earlier[:], mask[:, 0])
            mm(bank[:, E:2 * E], earlier[:], mask[:, 1], True, False)
            mm(bank[:, E:2 * E], ones[:], mask[:, 0], False, True)
            mm(bank[:, 2 * E:3 * E], ones[:], mask[:, 0], True, False)
            mm(bank[:, 2 * E:3 * E], ones[:], mask[:, 1], False, True).then_inc(full("pos"), 1)
            mix_taken(pe, ("x2T", 3))
            for i in range(2):
                for t in range(TT):
                    unit_taken(pe, ("out", i), t)

            base = len(CHUNKS)

            def gather(onehots, w, sel):
                for k in range(KD):
                    for t in range(TT):
                        ins = mm(ps[6 + k // 4][:, (k % 4) * w:(k % 4 + 1) * w], h2[:, t, k * P:(k + 1) * P],
                                 onehots[:, t], t == 0, t == TT - 1)
                ins.then_inc(sel, 1)

            def up(s, bank, rows_, done):
                for m in range(4):
                    for k in range(KD):
                        ins = mm(bank[:, m * W:(m + 1) * W], ring[:, s, k, m * P:(m + 1) * P], rows_[:, k], k == 0,
                                 k == KD - 1)
                ins.then_inc(done, 1)

            def down(w2, hidden_, banks, done):
                for n in range(2):
                    for f in range(2):
                        ins = mm(banks[n][0:W, :], hidden_[:, f * W:(f + 1) * W], w2[:, f, n * 512:(n + 1) * 512], f == 0,
                                 f == 1)
                ins.then_inc(done, 1)

            def select(i, d):
                wait_turn(pe, pick_ok, i, d)
                wait_turn(pe, sel_taken, i, d - 1)
                gather(pickS[:, d % 2], 2 * W, sel_full[d % 2])

            def up_of(i, c_):
                s = (base + c_) % SLOTS
                before = 16 * len([n for n in range(base) if n % SLOTS == s])
                pe.wait_ge(slot_full[s], i * 32 + (before + 32 * (c_ // 4 + 1)))
                wait_turn(pe, sel_taken, i, c_ // 2)
                wait_turn(pe, hid_ok, i, c_ - 2)
                up(s, ps[c_ % 2], hsel[:, (c_ // 2) % 2, :, c_ % 2], up_full[c_ % 4])

            def down_of(i, c_):
                wait_turn(pe, w2_full, i, c_, 16)
                wait_turn(pe, hid_ok, i, c_)
                wait_turn(pe, y_lo, i, c_ - 2)
                wait_turn(pe, y_hi, i, c_ - 2)
                down(w2_slot[c_ % 4], hid[:, c_ % 2], ps[2 + 2 * (c_ % 2):4 + 2 * (c_ % 2)], down_full[c_ % 4])

            def four_experts(i, last=False):
                for q in range(2):
                    c_ = 2 * q
                    if not (last and q == 1):
                        select(i, q + 1)
                    up_of(i, c_ + 1)
                    down_of(i, c_)
                    if not (last and q == 1):
                        up_of(i, c_ + 2)
                    down_of(i, c_ + 1)

            select(0, 0)
            up_of(0, 0)
            four_experts(0)
            with pe.Fori(1, E // 4 - 1) as i:
                four_experts(i)
            four_experts(E // 4 - 1, last=True)
            pe.wait_ge(jobs_ok, 1)
            extra = pe.value_load(jobs_i[0:1, JOBS:JOBS + 1], min_val=0, max_val=JOBS)
            with pe.If(extra > 0):
                with pe.Fori(1, extra + 1) as j:
                    pe.wait_ge(x_pick, j)
                    gather(pickS[:, 0, :, 0], W, x_sel)
                    pe.wait_ge(x_taken, j)
                    pe.wait_ge(x_loaded, j * 48)
                    up(0, ps[0], hsel[:, 0, :, 0], x_up)
                    pe.wait_ge(x_hid, j)
                    down(w2_slot[0], hid[:, 0], ps[2:4], x_down)


_INS = ["x", "c", "ada_w", "ada_b", "norm1_g", "w_in", "gla_w_gk2", "gla_b_gk", "gla_norm_g", "conv_w", "conv_b",
        "dt_bias", "a_log", "d_skip", "ssm_norm_g", "w_oa", "w_ob", "w_out", "norm2_g", "router_group_w",
        "router_group_b", "router_expert_w", "router_expert_b", "expert_w1", "expert_w3", "expert_w2", "final_norm_g"]


def kernel(**inputs):
    import concourse.bacc as bacc
    import numpy as np
    from concourse.bass_utils import run_bass_kernel_spmd

    nc = bacc.Bacc("TRN2", target_bir_lowering=False, num_devices=1)
    arrays, args = {}, []
    for name in _INS:
        a = np.ascontiguousarray(inputs[name])
        arrays[f"in_{name}"] = a
        args.append(nc.dram_tensor(f"in_{name}", a.shape, mybir.dt.from_np(a.dtype), kind="ExternalInput").ap())
    out = nc.dram_tensor("out", inputs["x"].shape, F32, kind="ExternalOutput").ap()
    trunk(nc, *args, out)
    r = run_bass_kernel_spmd(nc, [arrays], core_ids=[0])
    return r.results[0]["out"]
```

```python
from contextlib import ExitStack

import concourse.bass as bass
from concourse import mybir

F32, F32R, I32 = mybir.dt.float32, mybir.dt.float32r, mybir.dt.int32
ALU = mybir.AluOpType
ACT = mybir.ActivationFunctionType
AX_X = mybir.AxisListType.X

P = 128
T = 256
TT = T // P
D = 1024
KD = D // P
CH = 64
NC = T // CH
EPS = 1e-6
GH, HK, HV, RANK = 4, 128, 256, 16
SH, SP_, SG, NS = 32, 64, 8, 128
DI = SH * SP_
CONV_CH, TAPS = DI + 2 * SG * NS, 4
E, EG, FF = 32, 8, 256
CW, HC = 512, 256
SLOTS, LOADS, HIGHS = 8, 5, 3
AHEAD = 2
W = 64
JOBS = 2 * T // W

OFF = {}
_at = 0
for _n, _w in (("q", 512), ("k", 512), ("v", 1024), ("g", 1024), ("gk", RANK), ("z", DI), ("xbc", CONV_CH),
               ("dt", SH), ("gate", 2 * D)):
    OFF[_n] = _at
    _at += _w

COL, _at = {"conv_w": 0}, 128
for _n, _w in (("conv_b", 32), ("ssm_g", 16), ("norm1", 8), ("norm2", 8), ("ada_b", 48), ("c", 8), ("gla_g", 2)):
    COL[_n] = _at
    _at += _w
NCOL = _at

ADA_LOAD = {("xbc", 0): 4, ("xbc", 2): 5, ("xbc", 4): 6, ("xbc", 6): 7, ("k", 0): 8, ("q", 0): 9, ("v", 0): 10,
            ("v", 1): 11}
ADA_AFTER = {("xbc", 2): 4, ("xbc", 4): 5, ("xbc", 6): 6, ("k", 0): 7, ("q", 0): 8, ("v", 0): 9, ("v", 1): 10,
             ("g", 0): 11}
BLOCKS = [("ada", i) for i in range(4)]
for _b in [("xbc", i) for i in range(8)] + [("k", 0), ("q", 0), ("v", 0), ("v", 1), ("g", 0), ("g", 1)]:
    BLOCKS += [_b] + ([("ada", ADA_LOAD[_b])] if _b in ADA_LOAD else [])
BLOCKS += [(_n, i) for _n in ("z", "gate") for i in range(4)]
BLOCKS += [(_n, i) for _n in ("oa", "ob", "out") for i in range(2)]
PIECES = []
for _n, _i in BLOCKS:
    for _h in range(2):
        PIECES += [(_n, _i, _h, r) for r in range(2 if _n == "ob" else 1)]
PIECE_AT = {p_: i for i, p_ in enumerate(PIECES)}
SPLITS = [p_ for p_ in PIECES if p_[0] != "ada"]
SPLIT_AT = {p_: i for i, p_ in enumerate(SPLITS)}
UNITS = [b_ for b_ in BLOCKS if b_[0] != "ada"]
TOKEN_MAJOR = ("k", "v", "g", "z", "out")
HALVES = [p_ for p_ in SPLITS if p_[0] in TOKEN_MAJOR and p_[2] == 0]
OB_FIRST = [p_ for p_ in SPLITS if p_[0] == "ob" and p_[3] == 0]

PLAN = ["cols"] + [("xT", i) for i in range(4)] + [("ada", i) for i in range(4)]
for _i in range(8):
    PLAN += [("unit", "xbc", _i)] + ["small"] * (_i == 0)
    if 1 <= _i <= 6:
        PLAN += [("tr", _i - 1, 0), ("tr", _i - 1, 1)]
    PLAN += [("ada", ADA_AFTER["xbc", _i])] if ("xbc", _i) in ADA_AFTER else []
PLAN += [("unit", "k", 0), ("ada", 7), "acum", ("gklin", 0), ("gklin", 1)]
PLAN += [("unit", "q", 0), ("ada", 8), ("gsuf", 0), ("gsuf", 1), "gdec"]
for _i in range(2):
    PLAN += [("unit", "v", _i)] + [("ada", 9 + _i)] + [("arow", _i, j) for j in range(4)]
PLAN += [("cb", 0), ("cb", 1)]
for _i in range(2):
    PLAN += [("unit", "g", _i)] + [("ada", 11)] * (_i == 0) + [("gU", c, hp) for c in (2 * _i, 2 * _i + 1) for hp in range(2)]
for _i in range(5):
    PLAN += [("unit", "z", _i) if _i < 4 else ("unit", "gate", 0)]
    if _i == 0:
        PLAN += [("gO", t, hp) for t in range(TT) for hp in range(2)]
    else:
        PLAN += [("U", _i - 1, c) for c in range(3)] + [(n, _i - 1, t) for n in ("off", "diag") for t in range(TT)]
PLAN += [("unit", "gate", 1)] + [("oaT", i) for i in range(4)]
for _i in range(2):
    PLAN += [("unit", "gate", 2 + _i)] + [("gtb", w, h) for w in (2 * _i, 2 * _i + 1) for h in range(2)]
PLAN += [("unit", "oa", 0)] + [("obT", i) for i in range(8)] + [("unit", "oa", 1)]
PLAN += [("unit", n, i) for n in ("ob", "out") for i in range(2)]
PLAN += [("x2T", i) for i in range(4)] + ["router", "pos"]
MIX = [n for n in PLAN if n[0] != "unit"]
MIX_AT = {n: i for i, n in enumerate(MIX)}
PIECES_OF = {}
_at = 0
for _n in PLAN:
    if _n[0] == "unit":
        for _h in range(2):
            _at += 2 if _n[1] == "ob" else 1
            PIECES_OF[_n[1:], _h] = _at
    PIECES_OF[_n] = _at


def trunk(nc, x, c, ada_w, ada_b, norm1_g, w_in, gla_w_gk2, gla_b_gk, gla_norm_g, conv_w, conv_b, dt_bias, a_log,
          d_skip, ssm_norm_g, w_oa, w_ob, w_out, norm2_g, router_group_w, router_group_b, router_expert_w,
          router_expert_b, expert_w1, expert_w3, expert_w2, final_norm_g, out):
    with ExitStack() as ctx:
        def sb(name, *dims):
            return ctx.enter_context(nc.sbuf_tensor(name, [P, *dims], F32))

        rounded = {}

        def sb2(name, *dims):
            with nc.sbuf_tensor(name, [P, *dims], F32) as plain:
                pass
            rounded[name] = ctx.enter_context(nc.sbuf_tensor(name + "_rounded", [P, *dims], F32R))
            return plain

        def sem(name):
            return ctx.enter_context(nc.semaphore(name))

        ring = sb2("ring", SLOTS, KD, HC)
        x_sb = sb2("x_sb", TT, D)
        hT = sb2("hT", KD, T)
        r_k = sb("r_k", 1024)
        r_q = sb("r_q", 1024)
        r_v = sb2("r_v", 2048)
        g_sb = sb2("g_sb", TT, D)
        r_z = sb2("r_z", 4096)
        r_xs = sb2("r_xs", 4096)
        r_bt = sb2("r_bt", 2048)
        r_ct = sb2("r_ct", 2048)
        r_btm = sb2("r_btm", 2048)
        r_lm = sb2("r_lm", 4096)
        r_st = sb2("r_st", 4096)
        r_pv = sb2("r_pv", 3, 512)

        def view(region, pattern, **kw):
            return region[:].rearrange(pattern, **kw)

        k_tm = view(r_k, "p (t d) -> p t d", t=TT)
        qT = view(r_q, "p (h t) -> p h t", h=GH)
        v_tm = view(r_v, "p (t d) -> p t d", t=TT)
        z_tm = view(r_z, "p (t d) -> p t d", t=TT)
        xn = r_z[:, 0:2048].rearrange("p (t d) -> p t d", t=TT)
        xs = view(r_xs, "p (t d) -> p t d", t=TT)
        BT = view(r_bt, "p (g t) -> p g t", g=SG)
        CT = view(r_ct, "p (g t) -> p g t", g=SG)
        Btm = view(r_btm, "p (t d) -> p t d", t=TT)
        u_cv = r_lm[:, 0:1024].rearrange("p (b a t) -> p b a t", b=2, a=2)
        acc_cv = r_lm[:, 1024:2048].rearrange("p (b a t) -> p b a t", b=2, a=2)
        xsT = r_lm[:, 2048:4096].rearrange("p (b a t) -> p b a t", b=2, a=4)
        M = view(r_lm, "p (t h s) -> p t h s", t=TT, h=SH)
        rhsL = r_st[:, 0:2048].rearrange("p (h s) -> p h s", h=SH)
        gla_st = view(r_st, "p (c h v) -> p c h v", c=NC, h=GH)
        zeros = r_st[:, 2048:2048 + D]
        gateT = view(r_st, "p (m t) -> p m t", m=2 * KD)
        gk_abs = r_pv[:, 0, :]
        gk_sp = r_pv[:, 1, :]
        gsuf_e = r_pv[:, 2, :]
        xdt = view(r_v, "p (b t d) -> p b t d", b=2, t=TT)
        xdd = view(r_bt, "p (b t d) -> p b t d", b=2, t=TT)
        y_tmp = view(r_k, "p (b d) -> p b d", b=2)
        y_off = view(r_q, "p (b d) -> p b d", b=2)
        h_f = r_z[:, 0:2048].rearrange("p (k t) -> p k t", k=KD)
        as_k = lambda name: rounded[name][:].rearrange("p t d -> p (t d)").rearrange("p (k t) -> p k t", t=T)
        flat_k = lambda name: rounded[name][:].rearrange("p (k t) -> p k t", t=T)
        h_parts = rounded["hT"][:], as_k("x_sb")
        oa_parts = flat_k("r_btm"), as_k("g_sb")
        ob_parts = flat_k("r_lm"), flat_k("r_xs")
        mT = view(r_bt, "p (m t) -> p m t", m=KD)
        m_parts = rounded["hT"][:], flat_k("r_bt")
        ada_acc = r_st[:, 3072:4096].rearrange("p (b n) -> p b n", b=2)
        gt1b = view(r_k, "p d -> p d")
        gt2b = view(r_q, "p d -> p d")
        s2b, sh2b = r_ct[:, 0:D], r_ct[:, D:2 * D]
        diag = r_pv[:, 0:2, :]
        m_tmp = r_pv[:, 2, :]
        h2 = view(r_v, "p (t d) -> p t d", t=TT)
        h2_parts = rounded["r_ct"][:].rearrange("p (t d) -> p t d", t=TT), rounded["r_v"][:].rearrange(
            "p (t d) -> p t d", t=TT)
        two = lambda ap: ap.rearrange("p (b k d) -> p b k d", b=2, k=2)
        w2_slot, w2_low, w2_high = two(r_z[:]), two(rounded["r_z"][:]), two(rounded["r_xs"][:])
        w13_high = [v.rearrange("p (k f) -> p k f", k=KD) for v in (
            rounded["g_sb"][:].rearrange("p t d -> p (t d)"), rounded["r_bt"][:], rounded["r_st"][:, 2048:],
            rounded["hT"][:].rearrange("p k t -> p (k t)"))]
        fng = r_k[:, 0:D]
        sq_d = g_sb[:, 0]
        pickS = rounded["r_pv"][:, 0, :].rearrange("p (b t e r) -> p b t e r", b=2, t=TT, e=2)
        hsel = rounded["r_lm"][:].rearrange("p (b k e l r) -> p b k e l r", b=2, k=KD, e=2, l=2)
        x_rows = r_lm[:, 0:KD * W].rearrange("p (k r) -> p k r", k=KD)
        up_sb = r_pv[:, 1, :]
        hid_parts = [rounded["r_pv"][:, 2, i * 2 * 2 * W:(i + 1) * 2 * 2 * W].rearrange("p (b f) -> p b f", b=2)
                     for i in range(2)]
        y_row = r_st[0:W, 0:2 * D].rearrange("p (b d) -> p b d", b=2)
        y_two = view(r_lm, "p (t c d) -> p t c d", t=TT, c=2)
        stackA, stackB = r_z[:, 2048:2176], r_z[:, 2176:2304]
        wsm = r_z[:, 2304:2304 + KD * (RANK + SH)].rearrange("p (k n) -> p k n", k=KD)
        gkT, wgk2 = r_z[0:RANK + 1, 2688:2688 + T], r_z[0:RANK + 1, 2944:2944 + 512]
        gk_ls = g_sb[:, 1]
        gk_ls = gk_ls.rearrange("p (t d) -> p t d", t=TT)
        late = {}
        at = 0
        for name, dims in (("wr", (KD, 36)), ("rb", (36,)), ("lg", (TT, 36)), ("rt", (24, TT, 8)), ("rt4", (TT, 4, EG)),
                           ("mask", (TT, E)), ("rank1", (TT, E)), ("ohG", (2 * TT, E)), ("ohx", (2 * TT, E)),
                           ("cnt", (4, E)), ("jv", (6, JOBS)), ("jp", (TT, JOBS)),
                           ("ix", (8, 2 * TT)), ("ints", (16,))):
            size = 1
            for d in dims:
                size *= d
            late[name] = r_btm[:, at:at + size]
            if len(dims) > 1:
                letters = "abc"[:len(dims)]
                late[name] = late[name].rearrange("p (" + " ".join(letters) + ") -> p " + " ".join(letters),
                                                  **dict(zip(letters, dims)))
            at += size
        wr, rb, lg, rt, rt4, mask, rank1, ohG, ohx, cnt, jv, jp, ix = (late[k] for k in (
            "wr", "rb", "lg", "rt", "rt4", "mask", "rank1", "ohG", "ohx", "cnt", "jv", "jp", "ix"))
        jt = r_k[:, 0:3 * JOBS * E].rearrange("p (a b) -> p a b", b=E)
        jobs_i = late["ints"][:, 0:JOBS + 1].bitcast(I32)
        rows_i = late["ints"][:, 12:16].bitcast(I32)
        sq = sb("sq", 256)
        hid_s, hid = sq[:, 0:2 * W], sq[:, 2 * W:4 * W]
        newton = sb("newton", 3, 16)
        ident = sb("ident", P)
        same = sb("same", P)
        upto = sb("upto", P)
        after = sb("after", P)
        earlier = sb("earlier", P)
        count = sb("count", W + 1)
        count0, count1 = count[:, 0:W], count[:, 1:W + 1]
        upto1 = sb("upto1", CH)
        fold = upto1
        inch = sb("inch", 2, P)
        ones = sb("ones", P)
        w_down = sb("w_down", 8)
        cols = sb("cols", NCOL)
        rows = sb("rows", 3, SH)
        cact = sb("cact", KD)
        mod = sb("mod", 48)
        st = sb("st", 16)
        dtb = sb("dtb", 5, TT, SH)
        dt, dA, acum, eacum, dend = (dtb[:, i] for i in range(5))
        dt_abs = sb("dt_abs", TT, SH)
        cdec = sb("cdec", NC, SH)
        gdec = sb("gdec", GH, NC)
        gss = sb("gss", 1, TT, GH)
        sss = sb("sss", 1, TT, SG)

        ps = [ctx.enter_context(nc.psum_tensor(f"ps{i}", [P, 512], F32)) for i in range(8)]

        slot_full = [sem(f"slot_full{i}") for i in range(LOADS)]
        ada_last, pool_step = sem("ada_last"), sem("pool_step")
        w2_hi, w2_lo, w13_hi, w13_lo, up_taken, fold_full, silu_up, hid_ok, fold_ok, sel_hi = (sem(n) for n in (
            "w2_hi w2_lo w13_hi w13_lo up_taken fold_full silu_up hid_ok fold_ok sel_hi").split())
        h2_hi, h2_lo = sem("h2_hi"), sem("h2_lo")
        hid_mul, hid_hi = sem("hid_mul"), sem("hid_hi")
        chain_step = [sem(f"chain_step{h}") for h in range(2)]
        w13_full = [sem(f"w13_full{i}") for i in range(4)]
        hi_ok, lo_ok, half_read, ob_read, ada_early, ada_late, h_full, h_hi, m_full, m_hi, ob_hi, oa_hi, h_lo = (
            sem(n) for n in ("hi_ok lo_ok half_read ob_read ada_early ada_late h_full h_hi m_full m_hi ob_hi oa_hi "
                             "h_lo").split())
        bank_full = [sem(f"bank_full{i}") for i in range(8)]
        bank_free = [sem(f"bank_free{i}") for i in range(8)]
        w2_full, up_full, down_full, y_lo, y_hi, y_stored = (
            [sem(f"{n}{i}") for i in range(4)] for n in ("w2_full", "up_full", "down_full", "y_lo", "y_hi", "y_stored"))
        pick_ok, sel_full, sel_taken = ([sem(f"{n}{i}") for i in range(2)] for n in ("pick_ok", "sel_full", "sel_taken"))
        (jobs_ok, x_free, x_loaded, x_pick, x_sel, x_taken, x_up, x_silu, x_hid, x_down, x_lo, x_hi, x_stored, moe_done,
         rows_ok, y_sum, rows_zeroed) = (sem(n) for n in (
            "jobs_ok x_free x_loaded x_pick x_sel x_taken x_up x_silu x_hid x_down x_lo x_hi x_stored moe_done "
            "rows_ok y_sum rows_zeroed").split())
        y_two_ok = [sem(f"y_two_ok{t}") for t in range(TT)]
        s_stack, s_x, s_small, s_rows, s_wr, s_fng = (sem(n) for n in ("s_stack", "s_x", "s_small", "s_rows", "s_wr", "s_fng"))
        s_const = sem("s_const")
        s_pool = sem("s_pool_chain")
        s_dve = sem("s_dve_chain")
        s_act = sem("s_act_chain")
        (x_sq, xn_done, cact_done, sm_done, a_exp, dt_sp, dA_done, ones_done, conv_step, conv_done,
         silu_done, gk_in, gk_l, gk_done, kdec_done, eac_done, rhs_done, L_done, gO_sq, xdd_done, skip_done,
         y_done, y_sq, ob_done, diag_done, x2_sq, x2n_done, rt_in, rt_e, rt_in2, rt_e2, mask_ok,
         x3_sq, fin_done, out_done) = (
            sem(n) for n in (
                "x_sq xn_done cact_done sm_done a_exp dt_sp dA_done ones_done conv_step conv_done silu_done "
                "gk_in gk_l gk_done kdec_done eac_done rhs_done L_done gO_sq xdd_done skip_done y_done y_sq "
                "ob_done diag_done x2_sq x2n_done rt_in rt_e rt_in2 rt_e2 mask_ok x3_sq fin_done "
                "out_done ").split())

        def mix(name):
            n = MIX_AT[name]
            return ps[4 + n % 4], 4 + n % 4, n // 4

        def mix_wait(eng, name):
            bank, b, turn = mix(name)
            eng.wait_ge(bank_full[b], turn + 1)
            return bank

        def mix_used(name):
            return bank_free[mix(name)[1]]

        def mix_taken(eng, name):
            _, b, turn = mix(name)
            eng.wait_ge(bank_free[b], turn + 1)

        def unit(name, half):
            n = 2 * UNITS.index(name) + half
            return ps[n % 4], n % 4, n // 4

        def unit_wait(eng, name, half):
            bank, b, turn = unit(name, half)
            eng.wait_ge(bank_full[b], turn + 1)
            return bank

        def unit_used(name, half):
            return bank_free[unit(name, half)[1]]

        def unit_taken(eng, name, half):
            _, b, turn = unit(name, half)
            eng.wait_ge(bank_free[b], turn + 1)

        def piece_used(eng, p_):
            kind, i, h, r = p_
            if kind == "ada":
                modulated(eng, i, h)
            elif p_ in HALVES:
                eng.wait_ge(half_read, HALVES.index(p_) + 1)
            elif p_ in OB_FIRST:
                eng.wait_ge(ob_read, OB_FIRST.index(p_) + 1)
            else:
                unit_wait(eng, (kind, i), h)

        def slot_of(p_):
            n = PIECE_AT[p_]
            return ring[:, n % LOADS]

        def low_of(p_):
            return rounded["ring"][:, PIECE_AT[p_] % LOADS]

        def high_of(p_):
            return rounded["ring"][:, LOADS + SPLIT_AT[p_] % HIGHS]

        def loaded(eng, p_):
            n = PIECE_AT[p_]
            eng.wait_ge(slot_full[n % LOADS], 16 * (n // LOADS + 1))

        def wait_turn(eng, sems, i, c, per=1):
            v = (i + (c // len(sems) + 1)) * per
            if not isinstance(v, int) or v > 0:
                eng.wait_ge(sems[c % len(sems)], v)

        def wait_item(eng, one, i, c, n=4):
            v = i * n + (c + 1)
            if not isinstance(v, int) or v > 0:
                eng.wait_ge(one, v)

        def col(name, i=0, n=1):
            return cols[:, COL[name] + i:COL[name] + i + n]

        def heads(ap):
            return ap.rearrange("p (h q) -> p h q", q=SP_)

        def over(ap, n):
            return ap.unsqueeze(len(ap.shape)).to_broadcast([*ap.shape, n])

        w_in2, ada2 = w_in[0], ada_w[0]
        y_rows = nc.dram_tensor("y_rows", [(E + JOBS) * W, D], F32, kind="Internal").ap()

        def piece_src(kind, i, h, r):
            w, at = {"ada": (ada2, 0), "oa": (w_oa[0], 0), "ob": (w_ob[0], 0), "out": (w_out[0], 0)}.get(
                kind, (w_in2, OFF.get(kind, 0)))
            at += i * CW + h * HC
            return w[r * D:(r + 1) * D, at:at + HC].rearrange("(k p) n -> p k n", p=P)

        ADA_SEM = [ada_early, ada_late, ada_early, ada_early] + [ada_late] * 5 + [ada_last] * 3
        ADA_TURN = [0, 0, 1, 2, 1, 2, 3, 4, 5, 0, 1, 2]
        ada_steps, dve_steps = [0], [0, 0]

        def modulated(eng, i, h=1):
            eng.wait_ge(ADA_SEM[i], 2 * ADA_TURN[i] + h + 1)

        def modulate(eng, i):
            if i >= 2:
                mix_wait(eng, ("ada", i - 2))
            pieces = [("ada", i, h, 0) for h in range(2)]
            acc = [ada_acc[:, i % 2, h * HC:(h + 1) * HC] for h in range(2)]
            if eng is nc.gpsimd:
                for h in range(2):
                    loaded(eng, pieces[h])
                    w = slot_of(pieces[h])
                    for dst, a_, b_, op in ((w, w, over(cact[:], HC), ALU.mult), (w[:, 0:4], w[:, 0:4], w[:, 4:8], ALU.add),
                                            (w[:, 0:2], w[:, 0:2], w[:, 2:4], ALU.add)):
                        ada_steps[0] += 1
                        eng.tensor_tensor(dst, a_, b_, op).then_inc(pool_step, 1)
                        eng.wait_ge(pool_step, ada_steps[0])
                    eng.tensor_tensor(acc[h], w[:, 0], w[:, 1], ALU.add).then_inc(ADA_SEM[i], 1)
                return
            for k in range(KD):
                for h in range(2):
                    if k == 0:
                        loaded(eng, pieces[h])
                        ins = eng.tensor_scalar(acc[h], slot_of(pieces[h])[:, k], cact[:, k:k + 1], None, ALU.mult)
                    else:
                        eng.wait_ge(chain_step[h], dve_steps[h])
                        ins = eng.scalar_tensor_tensor(acc[h], slot_of(pieces[h])[:, k], cact[:, k:k + 1], acc[h],
                                                       ALU.mult, ALU.add)
                    if k < KD - 1:
                        ins.then_inc(chain_step[h], 1)
                        dve_steps[h] += 1
                    else:
                        ins.then_inc(ADA_SEM[i], 1)

        block = ctx.enter_context(nc.Block())

        @block.sync
        def _(sp):
            rowsA = conv_w[0].rearrange("w (t p) -> (w t) p", p=P)
            sp.dma_start(stackA, rowsA).then_inc(s_stack, 16)
            at = 0
            for v, n in ((conv_b, 32), (ssm_norm_g, 16), (norm1_g, 8), (norm2_g, 8), (ada_b, 48), (c, 8), (gla_norm_g, 2)):
                sp.dma_start(stackB[at:at + n, :], v[0].rearrange("(t p) -> t p", p=P)).then_inc(s_stack, 16)
                at += n
            for n, p_ in enumerate(PIECES):
                if n >= LOADS:
                    piece_used(sp, PIECES[n - LOADS])
                sp.dma_start(slot_of(p_), piece_src(*p_)).then_inc(slot_full[n % LOADS], 16)
                if p_ == ("ada", 0, 1, 0):
                    sp.dma_start(x_sb[:], x[0].rearrange("(t p) d -> p t d", p=P)).then_inc(s_x, 16)
                if p_ == ("ada", 3, 1, 0):
                    sp.dma_start(wsm[:, :, 0:RANK], w_in2[:, OFF["gk"]:OFF["gk"] + RANK].rearrange("(k p) n -> p k n", p=P)
                                 ).then_inc(s_small, 16)
                    sp.dma_start(wsm[:, :, RANK:], w_in2[:, OFF["dt"]:OFF["dt"] + SH].rearrange("(k p) n -> p k n", p=P)
                                 ).then_inc(s_small, 16)
                    sp.dma_start(wgk2[0:RANK, :], gla_w_gk2[0]).then_inc(s_small, 16)
                    sp.dma_start(wgk2[RANK:RANK + 1, :], gla_b_gk).then_inc(s_small, 16)
                    for i, v in enumerate((dt_bias, a_log, d_skip)):
                        sp.dma_start(rows[:, i, :], v[0].partition_broadcast(P)).then_inc(s_rows, 16)
                if p_ == ("oa", 1, 1, 0):
                    unit_wait(sp, ("gate", 3), 1)
                    sp.dma_start(x_sb[:], x[0].rearrange("(t p) d -> p t d", p=P)).then_inc(s_x, 16)
                if p_ == ("out", 1, 1, 0):
                    for h in range(2):
                        unit_taken(sp, ("oa", 1), h)
                    sp.dma_start(wr[:, :, 0:4], router_group_w[0].rearrange("(k p) n -> p k n", p=P)).then_inc(s_wr, 16)
                    sp.dma_start(wr[:, :, 4:36], router_expert_w[0].rearrange("(k p) n -> p k n", p=P)).then_inc(s_wr, 16)
                    sp.dma_start(rb[:, 0:4], router_group_b[0].partition_broadcast(P)).then_inc(s_wr, 16)
                    sp.dma_start(rb[:, 4:36], router_expert_b[0].partition_broadcast(P)).then_inc(s_wr, 16)
            w1v = expert_w1[0].rearrange("g e (k p) f -> (g e) p k f", p=P)
            w3v = expert_w3[0].rearrange("g e (k p) f -> (g e) p k f", p=P)
            w2v = expert_w2[0].rearrange("g e (k p) d -> (g e) p k d", p=P)
            for h in range(2):
                unit_wait(sp, ("ob", 1), h)

            def load_w13(e, u):
                sp.dma_start(ring[:, 2 * u], w1v[e]).then_inc(w13_full[u], 16)
                sp.dma_start(ring[:, 2 * u + 1], w3v[e]).then_inc(w13_full[u], 16)

            def load_w2(e, u):
                sp.dma_start(w2_slot[:, u % 2], w2v[e]).then_inc(w2_full[u], 16)

            for u in range(4):
                for p_ in PIECES[-LOADS:]:
                    if PIECE_AT[p_] % LOADS in (2 * u, 2 * u + 1):
                        piece_used(sp, p_)
                for p_ in SPLITS[-HIGHS:]:
                    if LOADS + SPLIT_AT[p_] % HIGHS in (2 * u, 2 * u + 1):
                        piece_used(sp, p_)
                load_w13(u, u)
                if u < 2:
                    load_w2(u, u)
            with sp.Fori(1, E // 4) as i:
                for u in range(4):
                    wait_turn(sp, up_full, i, u - 4)
                    load_w13(i * 4 + u, u)
                    wait_turn(sp, down_full, i, u - 4)
                    load_w2(i * 4 + (u - 2), (u - 2) % 4)
            for u in range(2):
                wait_turn(sp, down_full, E // 4 - 1, u)
                load_w2(E - 2 + u, u + 2)
            for k in range(4):
                sp.wait_ge(y_stored[k], 16 * (E // 4))
            sp.wait_ge(jobs_ok, 1)
            sp.wait_ge(rows_zeroed, 16 * (JOBS * W // P))
            sp.sem_inc(x_free, 1)
            extra = sp.value_load(jobs_i[0:1, JOBS:JOBS + 1], min_val=0, max_val=JOBS)
            with sp.If(extra > 0):
                with sp.Fori(1, extra + 1) as j:
                    sp.wait_ge(x_free, j)
                    e = sp.value_load(jobs_i[0:1, bass.ds(j - 1, 1)], min_val=0, max_val=E - 1)
                    sp.dma_start(ring[:, 0], w1v[e]).then_inc(x_loaded, 16)
                    sp.dma_start(ring[:, 1], w3v[e]).then_inc(x_loaded, 16)
                    sp.dma_start(w2_slot[:, 0], w2v[e]).then_inc(x_loaded, 16)
                    sp.wait_ge(x_lo, j)
                    sp.wait_ge(x_hi, j)
                    sp.dma_start(y_rows[bass.ds(j * W + (E - 1) * W, W), :], y_row[:, 0]).then_inc(x_stored, 16)
                    sp.wait_ge(x_stored, j * 16)
                    sp.sem_inc(x_free, 1)
            sp.sem_inc(moe_done, 1)
            for t in range(TT):
                sp.wait_ge(fin_done, t + 1)
                sp.dma_start(out[0, t * P:(t + 1) * P, :], x_sb[:, t]).then_inc(out_done, 16)
            sp.wait_ge(out_done, 16 * TT)

        @block.gpsimd
        def _(pool):
            n = [0]

            def link(ins):
                n[0] += 1
                ins.then_inc(s_pool, 1)
                pool.wait_ge(s_pool, n[0])

            nc.gpsimd.memset(ones[:], 1.0)
            nc.gpsimd.memset(ident[:], 0.0)
            nc.gpsimd.memset(inch[:], 1.0)
            link(nc.gpsimd.memset(same[:], 1.0))
            link(nc.gpsimd.affine_select(out=ident[:], in_=ident[:], compare_op=ALU.not_equal, fill=1.0, base=0,
                                         pattern=[[-1, P]], channel_multiplier=1))
            for m, w in ((same[:].rearrange("p (j t) -> p j t", j=2), CH), (inch[:], P)):
                link(nc.gpsimd.affine_select(out=m, in_=m, compare_op=ALU.is_ge, fill=0.0, base=0,
                                             pattern=[[-CH, 2], [0, w]], channel_multiplier=1))
                link(nc.gpsimd.affine_select(out=m, in_=m, compare_op=ALU.is_ge, fill=0.0, base=CH - 1,
                                             pattern=[[CH, 2], [0, w]], channel_multiplier=-1))
            link(nc.gpsimd.affine_select(out=upto[:], in_=same[:], compare_op=ALU.is_ge, fill=0.0, base=0,
                                         pattern=[[1, P]], channel_multiplier=-1))
            link(nc.gpsimd.affine_select(out=after[:], in_=same[:], compare_op=ALU.is_ge, fill=0.0, base=-1,
                                         pattern=[[-1, P]], channel_multiplier=1))
            link(nc.gpsimd.memset(earlier[:], 1.0))
            link(nc.gpsimd.affine_select(out=earlier[:], in_=earlier[:], compare_op=ALU.is_ge, fill=0.0, base=-1,
                                         pattern=[[1, P]], channel_multiplier=-1))
            link(nc.gpsimd.iota(count[:], pattern=[[1, W + 1]], base=0, channel_multiplier=0,
                                allow_small_or_imprecise_dtypes=True))
            link(nc.gpsimd.iota(w_down[:], pattern=[[-1, 8]], base=8, channel_multiplier=0,
                                allow_small_or_imprecise_dtypes=True))
            nc.gpsimd.tensor_tensor(upto1[:], upto[:, 0:CH], upto[:, CH:P], ALU.add).then_inc(s_const, 1)
            pool.wait_ge(cact_done, 1)
            for i in (1, 4, 5, 6, 7, 8):
                modulate(nc.gpsimd, i)
                if i == 1:
                    link(nc.gpsimd.memset(zeros, 0.0))
                    for i in range(JOBS * W // P):
                        pool.dma_start(y_rows[E * W + i * P:E * W + (i + 1) * P, :], zeros).then_inc(rows_zeroed, 16)
            pool.wait_ge(eac_done, 1)
            pool.wait_ge(s_rows, 48)
            for i in range(4):
                for t in range(TT):
                    mix_taken(pool, ("tr", i, t))
            for j in range(4):
                b = j % 2
                if j == 0:
                    for name in [("gU", NC - 1, 0), ("gU", NC - 1, 1), ("cb", 0), ("cb", 1)]:
                        mix_wait(pool, name)
                if j >= 2:
                    for t in range(TT):
                        mix_wait(pool, ("diag", j - 2, t))
                    mix_wait(pool, ("U", j - 2, 2))
                src = xs[:, :, j * 512:(j + 1) * 512]
                for t in range(TT):
                    h = slice(8 * j, 8 * j + 8)
                    link(nc.gpsimd.tensor_tensor(heads(xdt[:, b, t]), heads(src[:, t]), over(dt[:, t, h], SP_), ALU.mult))
                    nc.gpsimd.tensor_tensor(heads(xdd[:, b, t]), heads(xdt[:, b, t]), over(dend[:, t, h], SP_),
                                            ALU.mult).then_inc(xdd_done, 1)
                    nc.gpsimd.tensor_tensor(heads(src[:, t]), heads(src[:, t]), over(rows[:, 2, h], SP_),
                                            ALU.mult).then_inc(skip_done, 1)
            def w2_low_part(i, c_):
                wait_item(pool, w2_hi, i, c_)
                nc.gpsimd.tensor_tensor(w2_low[:, c_ % 2], w2_slot[:, c_ % 2], w2_high[:, c_ % 2].bitcast(F32), ALU.subtract
                                        ).then_inc(w2_lo, 1)

            with pool.Fori(0, E // 4) as i:
                for c_ in range(4):
                    w2_low_part(i, c_)
            pool.wait_ge(jobs_ok, 1)
            pool.dma_start(fng, final_norm_g.partition_broadcast(P)).then_inc(s_fng, 16)
            pool.wait_ge(rows_ok, 1)
            pool.wait_ge(moe_done, 1)
            for t in range(TT):
                for c_ in range(2):
                    pool.indirect_dma_start(
                        out=y_two[:, t, c_], out_offset=None, in_=y_rows[:, :],
                        in_offset=bass.IndirectOffsetOnAxis(ap=rows_i[:, 2 * t + c_:2 * t + c_ + 1], axis=0)
                    ).then_inc(y_two_ok[t], 16)

        @block.scalar
        def _(act):
            n = [0]

            def link(ins):
                n[0] += 1
                ins.then_inc(s_act, 1)
                act.wait_ge(s_act, n[0])

            split = [0]

            def before(name):
                while split[0] < min(PIECES_OF[name] + AHEAD, len(SPLITS)):
                    p_ = SPLITS[split[0]]
                    split[0] += 1
                    loaded(act, p_)
                    n_split = SPLIT_AT[p_]
                    if n_split >= HIGHS:
                        piece_used(act, SPLITS[n_split - HIGHS])
                    nc.scalar.copy(high_of(p_), slot_of(p_)).then_inc(hi_ok, 1)

            act.wait_ge(s_x, 16)
            for t in range(TT):
                ins = nc.scalar.activation(hT[:].rearrange("p k t -> p (k t)")[:, t * D:(t + 1) * D], x_sb[:, t], ACT.Square,
                                           accum_out=st[:, t:t + 1])
                ins.then_inc(x_sq, 1)
            mix_taken(act, "cols")
            nc.scalar.activation(cact[:], col("c", 0, 8), ACT.Silu).then_inc(cact_done, 1)
            for i in range(4):
                bank = mix_wait(act, ("xT", i))
                nc.scalar.copy(hT[:, 2 * i:2 * i + 2].rearrange("p k t -> p (k t)"), bank[:]).then_inc(
                    mix_used(("xT", i)), 1)
            before("cols")
            for i in range(4):
                act.wait_ge(h_full, 2 * i + 2)
                nc.scalar.copy(h_parts[0][:, 2 * i:2 * i + 2], h_f[:, 2 * i:2 * i + 2]).then_inc(h_hi, 1)
            def silu_out(g):
                i, a = g // 2, 2 * (g % 2)
                if i < 4:
                    return xsT[:, i % 2, a:a + 2]
                return (BT if i < 6 else CT)[:, 4 * (i % 2) + a:4 * (i % 2) + a + 2]

            def conv_silu(g):
                act.wait_ge(conv_done, g + 1)
                if 4 <= g < 8:
                    mix_wait(act, ("tr", g // 2 - 2, 1))
                nc.scalar.activation(silu_out(g), acc_cv[:, g % 2], ACT.Silu).then_inc(silu_done, 1)

            for i in range(8):
                for half in range(2):
                    g = 2 * i + half
                    before((("xbc", i), half))
                    bank = unit_wait(act, ("xbc", i), half)
                    if g >= 2:
                        act.wait_ge(conv_done, g - 1)
                    nc.scalar.copy(u_cv[:, g % 2].rearrange("p a t -> p (a t)"), bank[:]).then_inc(
                        unit_used(("xbc", i), half), 1)
                    if g:
                        conv_silu(g - 1)
                if i == 0:
                    before("small")
                    act.wait_ge(s_rows, 48)
                    nc.scalar.activation(rows[:, 1, :], rows[:, 1, :], ACT.Exp).then_inc(a_exp, 1)
                    act.wait_ge(sm_done, 1)
                    link(nc.scalar.activation(dt_abs[:], dt_abs[:], ACT.Exp, scale=-1.0))
                    nc.scalar.activation(dt_abs[:], dt_abs[:], ACT.Ln, bias=1.0).then_inc(dt_sp, 1)
                if 1 <= i <= 6:
                    for t in range(TT):
                        before(("tr", i - 1, t))
                        bank = mix_wait(act, ("tr", i - 1, t))
                        dst = xs[:, t, (i - 1) * 512:i * 512] if i <= 4 else Btm[:, t, (i - 5) * 512:(i - 4) * 512]
                        nc.scalar.copy(dst, bank[:]).then_inc(mix_used(("tr", i - 1, t)), 1)
            conv_silu(15)

            for t in range(TT):
                before((("k", 0), t))
                bank = unit_wait(act, ("k", 0), t)
                nc.scalar.copy(k_tm[:, t], bank[:]).then_inc(unit_used(("k", 0), t), 1)
            for t in range(TT):
                act.wait_ge(gk_in, t + 1)
                link(nc.scalar.activation(gk_abs, gk_abs, ACT.Exp, scale=-1.0))
                nc.scalar.activation(gk_sp, gk_abs, ACT.Ln, bias=1.0).then_inc(gk_l, 1)
            before("acum")
            mix_taken(act, "acum")
            nc.scalar.activation(dend, dend, ACT.Exp)
            nc.scalar.activation(eacum, acum, ACT.Exp)
            nc.scalar.activation(cdec[:], cdec[:], ACT.Exp).then_inc(eac_done, 1)
            for t in range(TT):
                before(("gsuf", t))
                bank = mix_wait(act, ("gsuf", t))
                if t:
                    act.wait_ge(kdec_done, t)
                nc.scalar.activation(gsuf_e, bank[:], ACT.Exp, scale=1.0 / 16).then_inc(mix_used(("gsuf", t)), 1)
            before("gdec")
            bank = mix_wait(act, "gdec")
            nc.scalar.activation(gdec[:].rearrange("p h c -> p (h c)"), bank[:, 0:GH * NC], ACT.Exp,
                                 scale=1.0 / 16).then_inc(mix_used("gdec"), 1)
            for h in range(2):
                before((("q", 0), h))
                bank = unit_wait(act, ("q", 0), h)
                nc.scalar.mul(qT[:, 2 * h:2 * h + 2].rearrange("p h t -> p (h t)"), bank[:], HK ** -0.5).then_inc(
                    unit_used(("q", 0), h), 1)
            for i in range(2):
                for t in range(TT):
                    before((("v", i), t))
                    bank = unit_wait(act, ("v", i), t)
                    nc.scalar.copy(v_tm[:, t, i * CW:(i + 1) * CW], bank[:]).then_inc(unit_used(("v", i), t), 1)
                for j in range(4):
                    before(("arow", i, j))
                    mix_taken(act, ("arow", i, j))
                link(nc.scalar.activation(M[:, i], M[:, i], ACT.Abs))
                nc.scalar.activation(M[:, i], M[:, i], ACT.Exp, scale=-1.0).then_inc(L_done, 1)
            for i in range(2):
                for t in range(TT):
                    before((("g", i), t))
                    bank = unit_wait(act, ("g", i), t)
                    nc.scalar.activation(g_sb[:, t, i * CW:(i + 1) * CW], bank[:], ACT.Silu).then_inc(
                        unit_used(("g", i), t), 1)

            def gla_squares():
                for t in range(TT):
                    for hp in range(2):
                        before(("gO", t, hp))
                        bank = mix_wait(act, ("gO", t, hp))
                        for a in range(2):
                            if t or hp or a:
                                act.wait_ge(gO_sq, 4 * t + 2 * hp + a)
                            nc.scalar.activation(sq[:], bank[:, a * HV:(a + 1) * HV], ACT.Square,
                                                 accum_out=gss[:, 0, t, 2 * hp + a:2 * hp + a + 1]).then_inc(gO_sq, 1)

            def ssd_squares(j):
                for t in range(TT):
                    act.wait_ge(y_done, 2 * j + t + 1)
                    for a in range(2):
                        g, n_sq = 2 * j + a, 4 * j + 2 * t + a
                        if n_sq:
                            act.wait_ge(y_sq, n_sq)
                        else:
                            act.wait_ge(gO_sq, TT * GH)
                        nc.scalar.activation(sq[:], z_tm[:, t, g * 256:(g + 1) * 256], ACT.Square,
                                             accum_out=sss[:, 0, t, g:g + 1]).then_inc(y_sq, 1)

            for i in range(4):
                for t in range(TT):
                    before((("z", i), t))
                    bank = unit_wait(act, ("z", i), t)
                    nc.scalar.activation(z_tm[:, t, i * CW:(i + 1) * CW], bank[:], ACT.Silu).then_inc(
                        unit_used(("z", i), t), 1)
                if i == 0:
                    gla_squares()
                if i >= 2:
                    ssd_squares(i - 2)
            for i in range(4):
                for h in range(2):
                    before((("gate", i), h))
                    bank = unit_wait(act, ("gate", i), h)
                    m = 4 * i + 2 * h
                    nc.scalar.activation(gateT[:, m:m + 2].rearrange("p m t -> p (m t)"), bank[:], ACT.Sigmoid).then_inc(
                        unit_used(("gate", i), h), 1)
                if i < 2:
                    ssd_squares(i + 2)
                if i == 1:
                    for j in range(4):
                        before(("oaT", j))
                        bank = mix_wait(act, ("oaT", j))
                        for a in range(2):
                            m = 2 * j + a
                            ins = nc.scalar.mul(oa_parts[0][:, m], bank[:, a * T:(a + 1) * T],
                                                col("gla_g", m % 2))
                        ins.then_inc(oa_hi, 1)
            for i in range(8):
                before(("obT", i))
                bank = mix_wait(act, ("obT", i))
                for a in range(2):
                    m = 2 * i + a
                    ins = nc.scalar.mul(ob_parts[0][:, m], bank[:, a * T:(a + 1) * T], col("ssm_g", m))
                ins.then_inc(ob_hi, 1)
            for i in range(4):
                before((("ob", i // 2), i % 2))
                act.wait_ge(m_full, i + 1)
                nc.scalar.copy(m_parts[0][:, 2 * i:2 * i + 2], mT[:, 2 * i:2 * i + 2]).then_inc(m_hi, 1)
            before(PLAN[-1])
            for i in range(2):
                for t in range(TT):
                    unit_taken(act, ("out", i), t)
                    if i or t:
                        act.wait_ge(x2_sq, 2 * i + t)
                    nc.scalar.activation(sq_d[:, 0:CW], x_sb[:, t, i * CW:(i + 1) * CW], ACT.Square,
                                         accum_out=st[:, 2 + 4 * i + t:3 + 4 * i + t]).then_inc(x2_sq, 1)
            for i in range(4):
                before(("x2T", i))
                bank = mix_wait(act, ("x2T", i))
                nc.scalar.copy(hT[:, 4 * (i % 2):4 * (i % 2) + 4, (i // 2) * P:(i // 2 + 1) * P],
                               bank[:].rearrange("p (k t) -> p k t", k=4)).then_inc(mix_used(("x2T", i)), 1)
            for t in range(TT):
                act.wait_ge(x2n_done, t + 1)
                nc.scalar.copy(h2_parts[0][:, t], h2[:, t]).then_inc(h2_hi, 1)
            act.wait_ge(rt_in, 1)
            nc.scalar.activation(rt[:, 0, :, 0:4], rt[:, 0, :, 0:4], ACT.Exp).then_inc(rt_e, 1)
            act.wait_ge(rt_in2, 1)
            nc.scalar.activation(rt[:, 12, :, 0:1], rt[:, 12, :, 0:1], ACT.Exp).then_inc(rt_e2, 1)

            def take_selected(i, d):
                wait_turn(act, sel_full, i, d)
                wait_turn(act, up_full, i, 2 * d - 3)
                for k in range(2):
                    ins = nc.scalar.copy(hsel[:, d % 2, 4 * k:4 * k + 4, :, 0], ps[6 + k][:].rearrange(
                        "p (k e r) -> p k e r", k=4, e=2))
                ins.then_inc(sel_hi, 1)

            def take_up(i, c_):
                wait_turn(act, up_full, i, c_)
                wait_item(act, fold_full, i, c_ - 1)
                nc.scalar.copy(up_sb, ps[0][:]).then_inc(up_taken, 1)

            def silu_of(i, c_):
                wait_item(act, fold_full, i, c_)
                wait_item(act, hid_mul, i, c_ - 1)
                nc.scalar.activation(hid_s, ps[1][:, 0:2 * W], ACT.Silu).then_inc(silu_up, 1)

            def output_low(i, c_, e):
                wait_turn(act, down_full, i, c_)
                wait_turn(act, y_stored, i, c_ - 2, 16)
                nc.scalar.copy(y_row[:, c_ % 2, 0:512], ps[2 + 2 * (c_ % 2)][0:W, :]).then_inc(y_lo[c_ % 4], 1)
                wait_turn(act, y_lo, i, c_)
                wait_turn(act, y_hi, i, c_)
                act.dma_start(y_rows[bass.ds(e * W, W), :], y_row[:, c_ % 2]).then_inc(y_stored[c_ % 4], 16)

            def w13_high_parts(i, c_):
                wait_turn(act, w13_full, i, c_, 32)
                wait_turn(act, up_full, i, c_ - 2)
                for j in range(2):
                    nc.scalar.copy(w13_high[(2 * c_ + j) % 4], ring[:, (2 * c_ + j) % 8]).then_inc(w13_hi, 1)

            def w2_high_part(i, c_):
                wait_turn(act, w2_full, i, c_, 16)
                wait_turn(act, down_full, i, c_ - 2)
                nc.scalar.copy(w2_high[:, c_ % 2], w2_slot[:, c_ % 2]).then_inc(w2_hi, 1)

            def four_experts(i, last=False):
                for c_ in range(4):
                    left = 3 - c_ if last else 4
                    if c_ % 2 == 0 and left >= 2:
                        take_selected(i, c_ // 2 + 1)
                    if left >= 1:
                        take_up(i, c_ + 1)
                    output_low(i, c_, i * 4 + c_)
                    if left >= 1:
                        silu_of(i, c_ + 1)
                    if left >= 3:
                        w13_high_parts(i, c_ + 3)
                    if left >= 2:
                        w2_high_part(i, c_ + 2)

            for h in range(2):
                unit_taken(act, ("ob", 1), h)
            w13_high_parts(0, 0)
            take_selected(0, 0)
            w13_high_parts(0, 1)
            for c_ in range(2):
                w2_high_part(0, c_)
            take_up(0, 0)
            silu_of(0, 0)
            w13_high_parts(0, 2)
            four_experts(0)
            with act.Fori(1, E // 4 - 1) as i:
                four_experts(i)
            four_experts(E // 4 - 1, last=True)
            act.wait_ge(jobs_ok, 1)
            extra = act.value_load(jobs_i[0:1, JOBS:JOBS + 1], min_val=0, max_val=JOBS)
            with act.If(extra > 0):
                with act.Fori(1, extra + 1) as j:
                    act.wait_ge(x_sel, j)
                    for k in range(2):
                        ins = nc.scalar.copy(x_rows[:, 4 * k:4 * k + 4, :], ps[6 + k][:, 0:4 * W].rearrange(
                            "p (k r) -> p k r", k=4))
                    ins.then_inc(x_taken, 1)
                    act.wait_ge(x_up, j)
                    nc.scalar.activation(hid_s, ps[0][:, 0:2 * W], ACT.Silu).then_inc(x_silu, 1)
                    act.wait_ge(x_down, j)
                    nc.scalar.copy(y_row[:, 0, 0:512], ps[2][0:W, :]).then_inc(x_lo, 1)
            for t in range(TT):
                act.wait_ge(y_sum, t + 1)
                if t:
                    act.wait_ge(x3_sq, t)
                nc.scalar.activation(sq_d, x_sb[:, t], ACT.Square, accum_out=st[:, 4 + t:5 + t]).then_inc(x3_sq, 1)

        @block.vector
        def _(dve):
            n = [0]

            def link(ins):
                n[0] += 1
                ins.then_inc(s_dve, 1)
                dve.wait_ge(s_dve, n[0])

            def rstd(ap, width):
                n_el = ap.free_size()
                m, y, s = (newton[:, i, 0:n_el] for i in range(3))
                if len(ap.shape) == 3:
                    m, y, s = (v.rearrange("p (a b) -> p a b", a=ap.shape[1]) for v in (m, y, s))
                link(nc.vector.tensor_scalar(m, ap, 1.0 / width, EPS, ALU.mult, ALU.add))
                link(nc.vector.tensor_scalar(s.bitcast(I32), m.bitcast(I32), 1, None, ALU.logical_shift_right))
                link(nc.vector.tensor_scalar(y.bitcast(I32), s.bitcast(I32), -1.0, float(0x5F3759DF), ALU.mult, ALU.add))
                for step in range(3):
                    link(nc.vector.tensor_tensor(s, y, y, ALU.mult))
                    link(nc.vector.scalar_tensor_tensor(s, s, -0.5, m, ALU.mult, ALU.mult))
                    link(nc.vector.scalar_tensor_tensor(y if step < 2 else ap, s, 1.5, y, ALU.add, ALU.mult))

            split = [0]

            def before(name):
                while split[0] < min(PIECES_OF[name] + AHEAD, len(SPLITS)):
                    p_ = SPLITS[split[0]]
                    split[0] += 1
                    dve.wait_ge(hi_ok, split[0])
                    nc.vector.tensor_tensor(low_of(p_), slot_of(p_), high_of(p_).bitcast(F32), ALU.subtract).then_inc(
                        lo_ok, 1)

            def modulation_out(i):
                before(("ada", i))
                bank = mix_wait(dve, ("ada", i))
                nc.vector.tensor_tensor(mod[:, 4 * i:4 * i + 4], bank[:, 0:4], col("ada_b", 4 * i, 4), ALU.add).then_inc(
                    mix_used(("ada", i)), 1)

            nc.vector.memset(gkT, 1.0).then_inc(ones_done, 1)
            bank = mix_wait(dve, "cols")
            nc.vector.tensor_copy(cols[:], bank[:, 0:NCOL]).then_inc(mix_used("cols"), 1)
            mix_taken(dve, "cols")
            dve.wait_ge(x_sq, TT)
            rstd(st[:, 0:TT], D)
            for t in range(TT):
                nc.vector.tensor_scalar(xn[:, t], x_sb[:, t], st[:, t:t + 1], None, ALU.mult).then_inc(xn_done, 1)
            dve.wait_ge(cact_done, 1)
            for i in (0, 2, 3):
                modulate(nc.vector, i)
            for i in range(4):
                bank = mix_wait(dve, ("ada", i))
                nc.vector.tensor_tensor(mod[:, 4 * i:4 * i + 4], bank[:, 0:4], col("ada_b", 4 * i, 4), ALU.add).then_inc(
                    mix_used(("ada", i)), 1)
                mix_taken(dve, ("ada", i))
            link(nc.vector.scalar_tensor_tensor(mod[:, 8:16], mod[:, 8:16], 1.0, col("norm1", 0, 8), ALU.add, ALU.mult))
            for i in range(4):
                mix_taken(dve, ("xT", i))
            for k in range(KD):
                nc.vector.tensor_scalar(h_f[:, k], hT[:, k], mod[:, 8 + k:9 + k], mod[:, k:k + 1], ALU.mult,
                                        ALU.add).then_inc(h_full, 1)
            for i in range(4):
                dve.wait_ge(h_hi, i + 1)
                ks = slice(2 * i, 2 * i + 2)
                nc.vector.tensor_tensor(h_parts[1][:, ks], h_f[:, ks], h_parts[0][:, ks].bitcast(F32), ALU.subtract
                                        ).then_inc(h_lo, 1)
            def small_out():
                before("small")
                bank = mix_wait(dve, "small")
                dve.wait_ge(ones_done, 1)
                nc.vector.tensor_copy(gkT[0:RANK, :], bank[0:RANK, 0:T])
                dve.wait_ge(s_rows, 48)
                nc.vector.tensor_tensor(dt, bank[:, T:T + TT * SH].rearrange("p (t h) -> p t h", t=TT),
                                        rows[:, 0:1, :].to_broadcast([P, TT, SH]), ALU.add).then_inc(mix_used("small"), 1)
                mix_taken(dve, "small")
                nc.vector.scalar_tensor_tensor(dt_abs[:], dt, -1.0, dt, ALU.mult, ALU.max).then_inc(sm_done, 1)
                dve.wait_ge(dt_sp, 1)
                link(nc.vector.scalar_tensor_tensor(dt, dt, 0.0, dt_abs[:], ALU.max, ALU.add))
                dve.wait_ge(a_exp, 1)
                nc.vector.scalar_tensor_tensor(dA, dt, -1.0, rows[:, 1:2, :].to_broadcast([P, TT, SH]), ALU.mult,
                                               ALU.mult).then_inc(dA_done, 1)

            step = 0
            for g in range(16):
                if g == 2:
                    small_out()
                before((("xbc", g // 2), g % 2))
                unit_taken(dve, ("xbc", g // 2), g % 2)
                if g >= 2:
                    dve.wait_ge(silu_done, g - 1)
                u, acc = u_cv[:, g % 2], acc_cv[:, g % 2]
                for tap in range(TAPS):
                    for a in range(2):
                        m = 2 * g + a
                        w = col("conv_w", (TAPS - 1 - tap) * 32 + m)
                        if tap == 0:
                            ins = nc.vector.tensor_scalar(acc[:, a], u[:, a], w, col("conv_b", m), ALU.mult, ALU.add)
                        else:
                            dve.wait_ge(conv_step, step - 1)
                            ins = nc.vector.scalar_tensor_tensor(acc[:, a, tap:], u[:, a, 0:T - tap], w,
                                                                 acc[:, a, tap:], ALU.mult, ALU.add)
                        if tap < TAPS - 1:
                            ins.then_inc(conv_step, 1)
                            step += 1
                        elif a == 0:
                            ins.then_inc(conv_step, 1)
                            step += 1
                        else:
                            ins.then_inc(conv_done, 1)
                if g % 2 and ("xbc", g // 2 - 1) in ADA_AFTER:
                    modulation_out(ADA_AFTER["xbc", g // 2 - 1])
            modulation_out(7)
            before("acum")
            bank = mix_wait(dve, "acum")
            nc.vector.tensor_copy(acum, bank[:, 0:64].rearrange("p (t h) -> p t h", t=TT))
            nc.vector.tensor_copy(dend, bank[:, 64:128].rearrange("p (t h) -> p t h", t=TT))
            nc.vector.tensor_copy(cdec[:].rearrange("p c h -> p (c h)"), bank[:, 128:256]).then_inc(mix_used("acum"), 1)
            mix_taken(dve, "acum")
            for t in range(TT):
                before(("gklin", t))
                bank = mix_wait(dve, ("gklin", t))
                nc.vector.tensor_copy(gk_ls[:, t], bank[:]).then_inc(mix_used(("gklin", t)), 1)
                mix_taken(dve, ("gklin", t))
                nc.vector.scalar_tensor_tensor(gk_abs, gk_ls[:, t], -1.0, gk_ls[:, t], ALU.mult, ALU.max).then_inc(gk_in, 1)
                dve.wait_ge(gk_l, t + 1)
                nc.vector.scalar_tensor_tensor(gk_ls[:, t], gk_ls[:, t], 0.0, gk_sp, ALU.min, ALU.subtract
                                               ).then_inc(gk_done, 1)
            modulate(nc.vector, 9)
            modulation_out(8)
            for t in range(TT):
                mix_taken(dve, ("gsuf", t))
                before((("k", 0), t))
                unit_taken(dve, ("k", 0), t)
                nc.vector.tensor_tensor(k_tm[:, t], k_tm[:, t], gsuf_e, ALU.mult).then_inc(kdec_done, 1)
            modulate(nc.vector, 10)
            dve.wait_ge(s_const, 1)
            for t in range(TT):
                if t:
                    for j in range(4):
                        mix_wait(dve, ("arow", t - 1, j))
                nc.vector.tensor_tensor(rhsL, over(dA[:, t], CH), upto1[:].unsqueeze(1).to_broadcast([P, SH, CH]),
                                        ALU.mult).then_inc(rhs_done, 1)
                modulation_out(9 + t)
                if t == 0:
                    dve.wait_ge(silu_done, 16)
                    for tt in range(TT):
                        mix_taken(dve, ("tr", 5, tt))
                for j in range(4):
                    before(("arow", t, j))
                    bank = mix_wait(dve, ("arow", t, j))
                    ins = nc.vector.tensor_tensor(M[:, t, 8 * j:8 * j + 8], bank[:].rearrange("p (h s) -> p h s", s=CH),
                                                  over(acum[:, t, 8 * j:8 * j + 8], CH), ALU.subtract)
                    ins.then_inc(mix_used(("arow", t, j)), 1)
            modulate(nc.vector, 11)
            for t in range(TT):
                before(("cb", t))
                bank = mix_wait(dve, ("cb", t))
                dve.wait_ge(L_done, t + 1)
                Mt = M[:, t].rearrange("p (g r) s -> p g r s", g=SG)
                cb = bank[:].rearrange("p (g s) -> p g s", g=SG).unsqueeze(2).to_broadcast([P, SG, 4, CH])
                nc.vector.tensor_tensor(Mt, Mt, cb, ALU.mult).then_inc(mix_used(("cb", t)), 1)
            modulation_out(11)
            dve.wait_ge(rows_zeroed, 16 * (JOBS * W // P))
            mix_taken(dve, "gdec")
            for c_ in range(NC):
                for hp in range(2):
                    before(("gU", c_, hp))
                    bank = mix_wait(dve, ("gU", c_, hp))
                    if c_:
                        mix_taken(dve, ("gU", c_ - 1, hp))
                    for a in range(2):
                        h = 2 * hp + a
                        u = bank[:, a * HV:(a + 1) * HV]
                        if c_ == 0:
                            ins = nc.vector.tensor_copy(gla_st[:, 0, h], u)
                        else:
                            ins = nc.vector.scalar_tensor_tensor(gla_st[:, c_, h], gla_st[:, c_ - 1, h],
                                                                 gdec[:, h, c_:c_ + 1], u, ALU.mult, ALU.add)
                    ins.then_inc(mix_used(("gU", c_, hp)), 1)
            for i in range(2):
                for t in range(TT):
                    before((("g", i), t))
                    unit_taken(dve, ("g", i), t)
            for t in range(TT):
                for hp in range(2):
                    before(("gO", t, hp))
                    bank = mix_wait(dve, ("gO", t, hp))
                    dve.wait_ge(gO_sq, 4 * t + 2 * hp + 2)
                    rstd(gss[:, 0, t, 2 * hp:2 * hp + 2], HV)
                    for a in range(2):
                        h = 2 * hp + a
                        o = g_sb[:, t, h * HV:(h + 1) * HV]
                        ins = nc.vector.scalar_tensor_tensor(o, bank[:, a * HV:(a + 1) * HV], gss[:, 0, t, h:h + 1], o,
                                                             ALU.mult, ALU.mult)
                    ins.then_inc(mix_used(("gO", t, hp)), 1)
            dve.wait_ge(eac_done, 1)
            for j in range(4):
                hs = slice(8 * j, 8 * j + 8)
                for c_ in range(3):
                    before(("U", j, c_))
                    bank = mix_wait(dve, ("U", j, c_))
                    if c_ == 0:
                        ins = nc.vector.tensor_copy(r_pv[:, 0], bank[:])
                    else:
                        link(nc.vector.tensor_tensor(heads(r_pv[:, c_]), heads(r_pv[:, c_ - 1]), over(cdec[:, c_, hs], SP_),
                                                     ALU.mult))
                        ins = nc.vector.tensor_tensor(r_pv[:, c_], r_pv[:, c_], bank[:], ALU.add)
                    ins.then_inc(mix_used(("U", j, c_)), 1)
                    mix_taken(dve, ("U", j, c_))
                dve.wait_ge(skip_done, 2 * j + 2)
                for t in range(TT):
                    lo = CH if t == 0 else 0
                    before(("off", j, t))
                    off = mix_wait(dve, ("off", j, t))
                    nc.vector.tensor_tensor(heads(y_off[lo:, t]), heads(off[lo:, :]), over(eacum[lo:, t, hs], SP_),
                                            ALU.mult).then_inc(mix_used(("off", j, t)), 1)
                for t in range(TT):
                    lo = CH if t == 0 else 0
                    before(("diag", j, t))
                    dg = mix_wait(dve, ("diag", j, t))
                    nc.vector.tensor_tensor(y_tmp[:, t], dg[:], xs[:, t, j * 512:(j + 1) * 512], ALU.add).then_inc(
                        mix_used(("diag", j, t)), 1)
                    mix_taken(dve, ("diag", j, t))
                    mix_taken(dve, ("off", j, t))
                    link(nc.vector.tensor_tensor(y_tmp[lo:, t], y_tmp[lo:, t], y_off[lo:, t], ALU.add))
                    before((("z", j), t))
                    unit_taken(dve, ("z", j), t)
                    z = z_tm[:, t, j * 512:(j + 1) * 512]
                    nc.vector.tensor_tensor(z, y_tmp[:, t], z, ALU.mult).then_inc(y_done, 1)
            for i in range(4):
                before(("oaT", i))
                mix_wait(dve, ("oaT", 3))
                bank, _, _ = mix(("oaT", i))
                dve.wait_ge(oa_hi, i + 1)
                for a in range(2):
                    m = 2 * i + a
                    ins = nc.vector.scalar_tensor_tensor(oa_parts[1][:, m], bank[:, a * T:(a + 1) * T],
                                                         col("gla_g", m % 2), oa_parts[0][:, m].bitcast(F32), ALU.mult, ALU.subtract)
                ins.then_inc(mix_used(("oaT", i)), 1)
            for i in range(4, 12):
                mix_taken(dve, ("ada", i))
            link(nc.vector.scalar_tensor_tensor(mod[:, 32:40], mod[:, 32:40], 1.0, col("norm2", 0, 8), ALU.add, ALU.mult))

            def modulation_rows(w):
                for h in range(2):
                    at = (16, 24, 32, 40)[w] + 4 * h
                    nc.vector.tensor_tensor(diag[:, h].rearrange("p (k q) -> p k q", k=4),
                                            ident[:].unsqueeze(1).to_broadcast([P, 4, P]), over(mod[:, at:at + 4], P),
                                            ALU.mult).then_inc(diag_done, 1)
                for h in range(2):
                    before(("gtb", w, h))
                    bank = mix_wait(dve, ("gtb", w, h))
                    nc.vector.tensor_copy((gt1b, sh2b, s2b, gt2b)[w][:, h * 512:(h + 1) * 512], bank[:]).then_inc(
                        mix_used(("gtb", w, h)), 1)

            modulation_rows(0)
            modulation_rows(1)
            dve.wait_ge(y_sq, TT * SG)
            rstd(sss[:, 0], 256)
            for t in range(TT):
                for g in range(SG):
                    o = z_tm[:, t, g * 256:(g + 1) * 256]
                    ins = nc.vector.tensor_scalar(o, o, sss[:, 0, t, g:g + 1], None, ALU.mult)
                ins.then_inc(ob_done, 1)
            modulation_rows(2)
            modulation_rows(3)
            for i in range(8):
                before(("obT", i))
                bank = mix_wait(dve, ("obT", i))
                dve.wait_ge(ob_hi, i + 1)
                for a in range(2):
                    m = 2 * i + a
                    ins = nc.vector.scalar_tensor_tensor(ob_parts[1][:, m], bank[:, a * T:(a + 1) * T],
                                                         col("ssm_g", m), ob_parts[0][:, m].bitcast(F32), ALU.mult, ALU.subtract)
                ins.then_inc(mix_used(("obT", i)), 1)
            for i in range(4):
                for h in range(2):
                    before((("gate", i), h))
                    unit_taken(dve, ("gate", i), h)
            for name in ("oa", "ob"):
                for i in range(2):
                    for h in range(2):
                        before(((name, i), h))
                        bank = unit_wait(dve, (name, i), h)
                        m = 4 * i + 2 * h
                        dst = mT[:, m:m + 2].rearrange("p m t -> p (m t)")
                        if name == "oa":
                            ins = nc.vector.tensor_tensor(dst, bank[:], gateT[:, m:m + 2].rearrange("p m t -> p (m t)"),
                                                          ALU.mult)
                        else:
                            link(nc.vector.tensor_tensor(m_tmp, bank[:], gateT[:, KD + m:KD + m + 2].rearrange(
                                "p m t -> p (m t)"), ALU.mult))
                            nc.vector.tensor_tensor(dst, dst, m_tmp, ALU.add).then_inc(m_full, 1)
                            dve.wait_ge(m_hi, m // 2 + 1)
                            ins = nc.vector.tensor_tensor(
                                m_parts[1][:, m:m + 2].rearrange("p m t -> p (m t)"), dst,
                                m_parts[0][:, m:m + 2].bitcast(F32).rearrange("p m t -> p (m t)"), ALU.subtract)
                        ins.then_inc(unit_used((name, i), h), 1)
                        unit_taken(dve, (name, i), h)
            dve.wait_ge(s_x, 32)
            for i in range(2):
                for t in range(TT):
                    before((("out", i), t))
                    bank = unit_wait(dve, ("out", i), t)
                    xs_ = x_sb[:, t, i * CW:(i + 1) * CW]
                    link(nc.vector.tensor_tensor(m_tmp, bank[:], gt1b[:, i * CW:(i + 1) * CW], ALU.mult))
                    ins = nc.vector.tensor_tensor(xs_, xs_, m_tmp, ALU.add)
                    ins.then_inc(unit_used(("out", i), t), 1)
                    unit_taken(dve, ("out", i), t)
                    link(nc.vector.tensor_tensor(h2[:, t, i * CW:(i + 1) * CW], xs_, s2b[:, i * CW:(i + 1) * CW], ALU.mult))
            dve.wait_ge(x2_sq, 2 * TT)
            link(nc.vector.tensor_tensor(st[:, 2:4], st[:, 2:4], st[:, 6:8], ALU.add))
            rstd(st[:, 2:4], D)
            for t in range(TT):
                nc.vector.scalar_tensor_tensor(h2[:, t], h2[:, t], st[:, 2 + t:3 + t], sh2b, ALU.mult, ALU.add).then_inc(
                    x2n_done, 1)
            mix_wait(dve, ("x2T", 3))
            for t in range(TT):
                dve.wait_ge(h2_hi, t + 1)
                nc.vector.tensor_tensor(h2_parts[1][:, t], h2[:, t], h2_parts[0][:, t].bitcast(F32), ALU.subtract).then_inc(
                    h2_lo, 1)
            before("router")
            bank = mix_wait(dve, "router")
            dve.wait_ge(s_wr, 64)
            nc.vector.tensor_tensor(lg, bank[:, 0:TT * 36].rearrange("p (t n) -> p t n", t=TT),
                                    rb.unsqueeze(1).to_broadcast([P, TT, 36]), ALU.add).then_inc(mix_used("router"), 1)
            mix_taken(dve, "router")
            R = [rt[:, i] for i in range(24)]

            def pick(dst, vals, top, w, tmp):
                link(nc.vector.tensor_tensor(tmp[:, :, 0:w], vals, top.to_broadcast([P, TT, w]), ALU.is_equal))
                link(nc.vector.tensor_tensor(tmp[:, :, 0:w], tmp[:, :, 0:w],
                                             w_down[:, 0:w].unsqueeze(1).to_broadcast([P, TT, w]), ALU.mult))
                link(nc.vector.reduce_max(R[23][:, :, 0:1], tmp[:, :, 0:w], AX_X))
                link(nc.vector.tensor_tensor(dst, tmp[:, :, 0:w], R[23][:, :, 0:1].to_broadcast([P, TT, w]), ALU.is_equal))

            link(nc.vector.reduce_max(R[1][:, :, 0:1], lg[:, :, 0:4], AX_X))
            pick(R[2][:, :, 0:4], lg[:, :, 0:4], R[1][:, :, 0:1], 4, R[3])
            nc.vector.tensor_tensor(R[0][:, :, 0:4], lg[:, :, 0:4], R[1][:, :, 0:1].to_broadcast([P, TT, 4]),
                                    ALU.subtract).then_inc(rt_in, 1)
            link(nc.vector.tensor_tensor(rt4, lg[:, :, 4:36].rearrange("p t (g e) -> p t g e", g=4),
                                         over(R[2][:, :, 0:4], EG), ALU.mult))
            link(nc.vector.reduce_sum(R[4], rt4.rearrange("p t g e -> p t e g"), AX_X))
            link(nc.vector.reduce_max(R[5][:, :, 0:1], R[4], AX_X))
            link(nc.vector.tensor_tensor(R[6], R[4], R[5][:, :, 0:1].to_broadcast([P, TT, EG]), ALU.subtract))
            link(nc.vector.memset(R[7][:, :, 0:1], 0.0))
            pick(R[8], R[6], R[7][:, :, 0:1], EG, R[9])
            link(nc.vector.scalar_tensor_tensor(R[10], R[8], -1e30, R[6], ALU.mult, ALU.add))
            link(nc.vector.reduce_max(R[11][:, :, 0:1], R[10], AX_X))
            nc.vector.tensor_copy(R[12][:, :, 0:1], R[11][:, :, 0:1]).then_inc(rt_in2, 1)
            pick(R[13], R[10], R[11][:, :, 0:1], EG, R[14])
            dve.wait_ge(rt_e, 1)
            link(nc.vector.reduce_sum(R[15][:, :, 0:1], R[0][:, :, 0:4], AX_X))
            dve.wait_ge(rt_e2, 1)
            link(nc.vector.tensor_scalar(R[16][:, :, 0:1], R[12][:, :, 0:1], 1.0, None, ALU.add))
            link(nc.vector.tensor_tensor(R[16][:, :, 0:1], R[16][:, :, 0:1], R[15][:, :, 0:1], ALU.mult))
            link(nc.vector.reciprocal(R[17][:, :, 0:1], R[16][:, :, 0:1]))
            link(nc.vector.tensor_tensor(R[18][:, :, 0:1], R[17][:, :, 0:1], R[12][:, :, 0:1], ALU.mult))
            link(nc.vector.tensor_tensor(R[19], R[8], R[13], ALU.add))
            nc.vector.tensor_tensor(mask.rearrange("p t (g e) -> p t g e", g=4), over(R[2][:, :, 0:4], EG),
                                    R[19].unsqueeze(2).to_broadcast([P, TT, 4, EG]), ALU.mult).then_inc(mask_ok, 1)
            before("pos")
            bank = mix_wait(dve, "pos")
            dve.wait_ge(mask_ok, 1)
            nc.vector.scalar_tensor_tensor(rank1, bank[:, 0:TT * E].rearrange("p (t e) -> p t e", t=TT), 1.0, mask,
                                           ALU.add, ALU.mult)
            link(nc.vector.tensor_copy(cnt[:, 0], bank[:, TT * E:(TT + 1) * E]))

            def pick(i, d, pair):
                wait_turn(dve, sel_full, i, d - 2)
                nc.vector.tensor_tensor(pickS[:, d % 2], over(rank1[:, :, bass.ds(pair * 2, 2)], W),
                                        count1.unsqueeze(1).unsqueeze(1).to_broadcast([P, TT, 2, W]),
                                        ALU.is_equal).then_inc(pick_ok[d % 2], 1)

            pick(0, 0, 0)
            pick(0, 1, 1)
            nc.vector.tensor_tensor(fold[:], ident[:, 0:CH], ident[:, CH:P], ALU.add).then_inc(fold_ok, 1)
            def w13_low_parts(i, c_):
                for j in range(2):
                    wait_item(dve, w13_hi, i, 2 * c_ + j, 8)
                    nc.vector.tensor_tensor(rounded["ring"][:, (2 * c_ + j) % 8], ring[:, (2 * c_ + j) % 8],
                                            w13_high[(2 * c_ + j) % 4].bitcast(F32), ALU.subtract).then_inc(w13_lo, 1)

            def selected_low(i, d):
                wait_item(dve, sel_hi, i, d, 2)
                for k in range(2):
                    ins = nc.vector.tensor_tensor(hsel[:, d % 2, 4 * k:4 * k + 4, :, 1], ps[6 + k][:].rearrange(
                        "p (k e r) -> p k e r", k=4, e=2), hsel[:, d % 2, 4 * k:4 * k + 4, :, 0].bitcast(F32), ALU.subtract)
                ins.then_inc(sel_taken[d % 2], 1)

            need, upto_e, before_e = cnt[:, 1], cnt[:, 2], cnt[:, 3]
            wide = lambda ap: ap.unsqueeze(1).to_broadcast([P, JOBS, E])
            nth = over(count0[:, 0:JOBS], E)
            of_job, tmp_j, tmp_k = (jt[:, i * JOBS:(i + 1) * JOBS] for i in range(3))

            def extra_windows():
                link(nc.vector.tensor_scalar(need, cnt[:, 0], W + 0.5, None, ALU.is_ge))
                for n_w in range(2, T // W):
                    link(nc.vector.scalar_tensor_tensor(need, cnt[:, 0], n_w * W + 0.5, need, ALU.is_ge, ALU.add))
                link(nc.vector.tensor_tensor_scan(upto_e, need, need, 0.0, ALU.add, ALU.bypass))
                link(nc.vector.tensor_tensor(before_e, upto_e, need, ALU.subtract))
                link(nc.vector.tensor_tensor(of_job, wide(before_e), nth, ALU.is_le))
                link(nc.vector.tensor_tensor(tmp_j, wide(upto_e), nth, ALU.is_gt))
                link(nc.vector.tensor_tensor(of_job, of_job, tmp_j, ALU.mult))
                link(nc.vector.tensor_tensor(tmp_j, of_job, wide(count0[:, 0:E]), ALU.mult))
                link(nc.vector.reduce_sum(jv[:, 0], tmp_j, AX_X))
                link(nc.vector.tensor_tensor(tmp_k, of_job, wide(before_e), ALU.mult))
                link(nc.vector.reduce_sum(jv[:, 1], tmp_k, AX_X))

            def ranks_of_extra_windows():
                link(nc.vector.tensor_tensor(jv[:, 2], count1[:, 0:JOBS], jv[:, 1], ALU.subtract))
                for t in range(TT):
                    link(nc.vector.tensor_tensor(tmp_j, of_job, wide(rank1[:, t]), ALU.mult))
                    link(nc.vector.reduce_sum(jv[:, 3], tmp_j, AX_X))
                    link(nc.vector.scalar_tensor_tensor(jp[:, t], jv[:, 2], -float(W), jv[:, 3], ALU.mult, ALU.add))
                nc.vector.tensor_copy(jobs_i[:, 0:JOBS], jv[:, 0])
                nc.vector.tensor_copy(jobs_i[:, JOBS:JOBS + 1], upto_e[:, E - 1:E]).then_inc(jobs_ok, 1)

            def rows_of_outputs():
                for c_, hot in enumerate((R[8], R[13])):
                    for t in range(TT):
                        link(nc.vector.tensor_tensor(ohG[:, 2 * t + c_].rearrange("p (g e) -> p g e", g=4),
                                                     over(R[2][:, t, 0:4], EG),
                                                     hot[:, t].unsqueeze(1).to_broadcast([P, 4, EG]), ALU.mult))
                by_tok = lambda ap: ap.unsqueeze(1).to_broadcast([P, 2 * TT, E])
                ohx4 = ohx.rearrange("p (t c) e -> p t c e", t=TT)
                ohG4 = ohG.rearrange("p (t c) e -> p t c e", t=TT)
                link(nc.vector.tensor_tensor(ohx4, ohG4, rank1.unsqueeze(2).to_broadcast([P, TT, 2, E]), ALU.mult))
                link(nc.vector.reduce_sum(ix[:, 0], ohx, AX_X))
                link(nc.vector.tensor_tensor(ohx, ohG, by_tok(count0[:, 0:E]), ALU.mult))
                link(nc.vector.reduce_sum(ix[:, 1], ohx, AX_X))
                link(nc.vector.tensor_tensor(ohx, ohG, by_tok(before_e), ALU.mult))
                link(nc.vector.reduce_sum(ix[:, 2], ohx, AX_X))

            def row_numbers():
                link(nc.vector.tensor_scalar(ix[:, 3], ix[:, 0], W + 0.5, None, ALU.is_ge))
                link(nc.vector.scalar_tensor_tensor(ix[:, 4], ix[:, 2], float(E - 1), ix[:, 1], ALU.add, ALU.subtract))
                link(nc.vector.tensor_tensor(ix[:, 4], ix[:, 4], ix[:, 3], ALU.mult))
                link(nc.vector.tensor_tensor(ix[:, 4], ix[:, 4], ix[:, 1], ALU.add))
                link(nc.vector.scalar_tensor_tensor(ix[:, 4], ix[:, 4], float(W), ix[:, 0], ALU.mult, ALU.add))
                link(nc.vector.tensor_scalar(ix[:, 4], ix[:, 4], -1.0, None, ALU.add))
                nc.vector.tensor_copy(rows_i, ix[:, 4]).then_inc(rows_ok, 1)

            def hidden(i, c_):
                hi, lo = (v[:, c_ % 2] for v in hid_parts)
                wait_item(dve, silu_up, i, c_)
                wait_turn(dve, down_full, i, c_ - 2)
                nc.vector.tensor_tensor(hid, ps[1][:, 2 * W:4 * W], hid_s, ALU.mult).then_inc(hid_mul, 1)
                wait_item(dve, hid_mul, i, c_)
                nc.vector.tensor_copy(hi, hid).then_inc(hid_hi, 1)
                wait_item(dve, hid_hi, i, c_)
                nc.vector.tensor_tensor(lo, hid, hi.bitcast(F32), ALU.subtract).then_inc(hid_ok, 1)

            def output_high(i, c_):
                wait_turn(dve, down_full, i, c_)
                wait_turn(dve, y_stored, i, c_ - 2, 16)
                nc.vector.tensor_copy(y_row[:, c_ % 2, 512:], ps[3 + 2 * (c_ % 2)][0:W, :]).then_inc(y_hi[c_ % 4], 1)

            def four_experts(i, last=False, between=()):
                for c_ in range(4):
                    left = 3 - c_ if last else 4
                    if c_ % 2 == 0:
                        if not last:
                            pick(i, c_ // 2 + 2, i * 2 + (c_ // 2 + 2))
                        if left >= 2:
                            selected_low(i, c_ // 2 + 1)
                    output_high(i, c_)
                    if left >= 1:
                        hidden(i, c_ + 1)
                    if left >= 3:
                        w13_low_parts(i, c_ + 3)
                    if c_ < len(between):
                        between[c_]()

            w13_low_parts(0, 0)
            extra_windows()
            selected_low(0, 0)
            w13_low_parts(0, 1)
            ranks_of_extra_windows()
            hidden(0, 0)
            w13_low_parts(0, 2)
            four_experts(0)
            with dve.Fori(1, E // 4 - 1) as i:
                four_experts(i)
            four_experts(E // 4 - 1, last=True, between=(rows_of_outputs, row_numbers))
            dve.wait_ge(jobs_ok, 1)
            extra = dve.value_load(jobs_i[0:1, JOBS:JOBS + 1], min_val=0, max_val=JOBS)
            with dve.If(extra > 0):
                with dve.Fori(1, extra + 1) as j:
                    dve.wait_ge(x_free, j)
                    nc.vector.tensor_tensor(pickS[:, 0, :, 0, :], jp[:, :, bass.ds(j - 1, 1)].to_broadcast([P, TT, W]), count1.unsqueeze(1).to_broadcast([P, TT, W]), ALU.is_equal
                        ).then_inc(x_pick, 1)
                    dve.wait_ge(x_silu, j)
                    nc.vector.tensor_tensor(hid, ps[0][:, 2 * W:4 * W], hid_s, ALU.mult).then_inc(x_hid, 1)
                    dve.wait_ge(x_down, j)
                    nc.vector.tensor_copy(y_row[:, 0, 512:], ps[3][0:W, :]).then_inc(x_hi, 1)
            for t in range(TT):
                dve.wait_ge(y_two_ok[t], 32)
                link(nc.vector.scalar_tensor_tensor(y_two[:, t, 0], y_two[:, t, 1], R[12][:, t, 0:1], y_two[:, t, 0],
                                                    ALU.mult, ALU.add))
                link(nc.vector.scalar_tensor_tensor(y_two[:, t, 0], y_two[:, t, 0], R[17][:, t, 0:1], gt2b, ALU.mult,
                                                    ALU.mult))
                nc.vector.tensor_tensor(x_sb[:, t], x_sb[:, t], y_two[:, t, 0], ALU.add).then_inc(y_sum, 1)
            dve.wait_ge(s_fng, 16)
            dve.wait_ge(x3_sq, TT)
            rstd(st[:, 4:4 + TT], D)
            for t in range(TT):
                nc.vector.scalar_tensor_tensor(x_sb[:, t], x_sb[:, t], st[:, 4 + t:5 + t], fng, ALU.mult,
                                               ALU.mult).then_inc(fin_done, 1)

        @block.tensor
        def _(pe):
            def begin(name):
                bank, b, turn = mix(name)
                if turn:
                    pe.wait_ge(bank_free[b], turn)
                return bank

            def full(name):
                return bank_full[mix(name)[1]]

            def mm(o, l, r, start=True, stop=True):
                return nc.tensor.matmul(o, l, r, start=start, stop=stop)

            def keep_clock(n):
                for _ in range(n):
                    mm(ps[0][:, 0:P], ident[:], ident[:])

            def modulation(i):
                modulated(pe, i)
                bank = begin(("ada", i))
                for m in range(4):
                    ins = mm(bank[:, m:m + 1], ada_acc[:, i % 2, m * P:(m + 1) * P], ones[:, 0:1])
                ins.then_inc(full(("ada", i)), 1)

            def split_product(o, l, r, start, stop):
                for n_, (a_, b_) in enumerate(((0, 0), (0, 1), (1, 0))):
                    ins = mm(o, l[a_], r[b_], start and n_ == 0, stop and n_ == 2)
                return ins

            def parts(p_):
                pe.wait_ge(lo_ok, SPLIT_AT[p_] + 1)
                return high_of(p_), low_of(p_)

            def bank_of(u, half):
                bank, b, turn = unit(u, half)
                if turn:
                    pe.wait_ge(bank_free[b], turn)
                return bank, bank_full[b]

            def channel_major(u, src):
                n_r = 2 if u[0] == "ob" else 1
                for half in range(2):
                    bank, done = bank_of(u, half)
                    for a in range(2):
                        for r in range(n_r):
                            w = parts((*u, half, r))
                            for k in range(KD):
                                ins = split_product(bank[:, a * T:(a + 1) * T], [v[:, k, a * P:(a + 1) * P] for v in w],
                                                    [v[:, r * KD + k] for v in src], r == 0 and k == 0,
                                                    r == n_r - 1 and k == KD - 1)
                            if a == 1:
                                ins.then_inc(done if r == n_r - 1 else ob_read, 1)

            def merged(k):
                unit_taken(pe, ("ob", k // 4), k // 2 % 2)

            def token_major(u, src):
                for half in range(2):
                    w = parts((*u, half, 0))
                    for t in range(TT):
                        bank, done = bank_of(u, t)
                        for k in range(KD):
                            if u == ("out", 0) and half == t == 0 and k % 2 == 0:
                                merged(k)
                            ins = split_product(bank[:, half * HC:(half + 1) * HC], [v[:, k, t * P:(t + 1) * P] for v in src],
                                                [v[:, k] for v in w], k == 0, k == KD - 1)
                        if half:
                            ins.then_inc(done, 1)
                        elif t:
                            ins.then_inc(half_read, 1)

            def project(u, src=h_parts):
                (token_major if u[0] in TOKEN_MAJOR else channel_major)(u, src)

            def transposed(name, pieces, rows=P):
                bank = begin(name)
                at = 0
                for src in pieces:
                    ins = nc.tensor.transpose(bank[:, at:at + P], src, ident[:])
                    at += P
                ins.then_inc(full(name), 1)

            pe.wait_ge(s_stack, 16 * 8)
            pe.wait_ge(s_const, 1)
            bank = begin("cols")
            nc.tensor.transpose(bank[:, 0:P], stackA, ident[:])
            nc.tensor.transpose(bank[:, P:NCOL], stackB[0:NCOL - P, :], ident[0:NCOL - P, 0:NCOL - P]).then_inc(
                full("cols"), 1)
            pe.wait_ge(xn_done, TT)
            for i in range(4):
                transposed(("xT", i), [xn[:, t, (2 * i + a) * P:(2 * i + a + 1) * P] for a in range(2) for t in range(TT)])
            for i in range(4):
                modulation(i)
            keep_clock(10)
            pe.wait_ge(h_full, KD)
            pe.wait_ge(h_lo, 4)
            for i in range(8):
                project(("xbc", i))
                if i == 0:
                    pe.wait_ge(s_small, 64)
                    bank = begin("small")
                    for k in range(KD):
                        mm(bank[0:RANK, 0:T], wsm[:, k, 0:RANK], h_f[:, k], k == 0, k == KD - 1)
                    for t in range(TT):
                        for k in range(KD):
                            ins = mm(bank[:, T + t * SH:T + (t + 1) * SH], h_f[:, k, t * P:(t + 1) * P], wsm[:, k, RANK:], k == 0,
                                     k == KD - 1)
                    ins.then_inc(full("small"), 1)

                if 1 <= i <= 6:
                    pe.wait_ge(silu_done, 2 * i)
                    src = xsT[:, (i - 1) % 2] if i <= 4 else BT[:, 4 * (i - 5):4 * (i - 4)]
                    for t in range(TT):
                        transposed(("tr", i - 1, t), [src[:, m, t * P:(t + 1) * P] for m in range(4)])
                if ("xbc", i) in ADA_AFTER:
                    modulation(ADA_AFTER["xbc", i])

            project(("k", 0))
            modulation(7)
            pe.wait_ge(dA_done, 1)
            bank = begin("acum")
            for t in range(TT):
                mm(bank[:, t * SH:(t + 1) * SH], upto[:], dA[:, t])
                mm(bank[:, 64 + t * SH:64 + (t + 1) * SH], after[:], dA[:, t])
                for a in range(2):
                    ins = mm(bank[:, 128 + (2 * t + a) * SH:128 + (2 * t + a + 1) * SH], inch[:, a], dA[:, t])
            ins.then_inc(full("acum"), 1)
            for t in range(TT):
                mm(begin(("gklin", t))[:], gkT[:, t * P:(t + 1) * P], wgk2).then_inc(full(("gklin", t)), 1)
            project(("q", 0))
            modulation(8)
            pe.wait_ge(gk_done, TT)
            for t in range(TT):
                mm(begin(("gsuf", t))[:], after[:], gk_ls[:, t]).then_inc(full(("gsuf", t)), 1)
            bank = begin("gdec")
            for h in range(GH):
                for t in range(TT):
                    at = h * NC + 2 * t
                    ins = mm(bank[:, at:at + 2], gk_ls[:, t, h * HK:(h + 1) * HK], inch[:, :, 0])
            ins.then_inc(full("gdec"), 1)

            def rows_of_sums(t):
                pe.wait_ge(rhs_done, t + 1)
                for j in range(4):
                    mm(begin(("arow", t, j))[:], same[:], rhsL[:, 8 * j:8 * j + 8]).then_inc(full(("arow", t, j)), 1)

            project(("v", 0))
            modulation(9)
            rows_of_sums(0)
            project(("v", 1))
            modulation(10)
            rows_of_sums(1)
            pe.wait_ge(silu_done, 16)
            for t in range(TT):
                bank = begin(("cb", t))
                for a in range(2):
                    cs = slice(t * P + a * CH, t * P + (a + 1) * CH)
                    for g in range(SG):
                        ins = mm(bank[a * CH:(a + 1) * CH, g * CH:(g + 1) * CH], BT[:, g, cs], CT[:, g, cs])
                ins.then_inc(full(("cb", t)), 1)

            def gla_updates(c_):
                t, lo = c_ // 2, (c_ % 2) * CH
                for hp in range(2):
                    bank = begin(("gU", c_, hp))
                    for a in range(2):
                        h = 2 * hp + a
                        ins = mm(bank[:, a * HV:(a + 1) * HV], k_tm[lo:lo + CH, t, h * HK:(h + 1) * HK],
                                 v_tm[lo:lo + CH, t, h * HV:(h + 1) * HV])
                    ins.then_inc(full(("gU", c_, hp)), 1)

            def gla_outputs():
                for t in range(TT):
                    for hp in range(2):
                        bank = begin(("gO", t, hp))
                        for a in range(2):
                            c_ = 2 * t + a
                            for b in range(2):
                                h = 2 * hp + b
                                mix_taken(pe, ("gU", c_, hp))
                                ins = mm(bank[a * CH:(a + 1) * CH, b * HV:(b + 1) * HV], qT[:, h, c_ * CH:(c_ + 1) * CH],
                                         gla_st[:, c_, h])
                        ins.then_inc(full(("gO", t, hp)), 1)

            def ssd(j):
                pe.wait_ge(xdd_done, 2 * (j + 1))
                for c_ in range(3):
                    t, lo = c_ // 2, (c_ % 2) * CH
                    bank = begin(("U", j, c_))
                    for a in range(2):
                        g = 2 * j + a
                        ins = mm(bank[:, a * 256:(a + 1) * 256], Btm[lo:lo + CH, t, g * NS:(g + 1) * NS],
                                 xdd[lo:lo + CH, j % 2, t, a * 256:(a + 1) * 256])
                    ins.then_inc(full(("U", j, c_)), 1)
                for t in range(TT):
                    bank = begin(("off", j, t))
                    for b in range(2):
                        c_ = 2 * t + b
                        if c_ == 0:
                            continue
                        mix_taken(pe, ("U", j, c_ - 1))
                        for a in range(2):
                            g = 2 * j + a
                            ins = mm(bank[b * CH:(b + 1) * CH, a * 256:(a + 1) * 256], CT[:, g, c_ * CH:(c_ + 1) * CH],
                                     r_pv[:, c_ - 1, a * 256:(a + 1) * 256])
                    ins.then_inc(full(("off", j, t)), 1)
                for t in range(TT):
                    mix_taken(pe, ("cb", t))
                    bank = begin(("diag", j, t))
                    for b in range(2):
                        part = slice(b * CH, (b + 1) * CH)
                        for h in range(8):
                            ins = mm(bank[part, h * SP_:(h + 1) * SP_], M[part, t, 8 * j + h],
                                     xdt[part, j % 2, t, h * SP_:(h + 1) * SP_])
                    ins.then_inc(full(("diag", j, t)), 1)

            for i in range(2):
                project(("g", i))
                if i == 0:
                    modulation(11)
                    pe.wait_ge(kdec_done, TT)
                    for name in (("v", 0), ("v", 1)):
                        for t in range(TT):
                            unit_taken(pe, name, t)
                for c_ in (2 * i, 2 * i + 1):
                    gla_updates(c_)
            for i in range(4):
                project(("z", i))
                if i == 0:
                    for h in range(2):
                        unit_taken(pe, ("q", 0), h)
                    gla_outputs()
                else:
                    ssd(i - 1)
            for i in range(4):
                project(("gate", i))
                if i == 0:
                    ssd(3)
                if i == 1:
                    for t in range(TT):
                        for hp in range(2):
                            mix_taken(pe, ("gO", t, hp))
                    for m in range(4):
                        transposed(("oaT", m), [g_sb[:, t, (2 * m + a) * P:(2 * m + a + 1) * P] for a in range(2)
                                                for t in range(TT)])
                if i >= 2:
                    for w in (2 * i - 4, 2 * i - 3):
                        for h in range(2):
                            pe.wait_ge(diag_done, 2 * w + h + 1)
                            mm(begin(("gtb", w, h))[:], ones[:], diag[:, h]).then_inc(full(("gtb", w, h)), 1)
            for i in range(4):
                mix_taken(pe, ("oaT", i))
            project(("oa", 0), oa_parts)
            pe.wait_ge(ob_done, TT)
            for m in range(8):
                transposed(("obT", m), [z_tm[:, t, (2 * m + a) * P:(2 * m + a + 1) * P] for a in range(2)
                                        for t in range(TT)])
            project(("oa", 1), oa_parts)
            for i in range(8):
                mix_taken(pe, ("obT", i))
            for i in range(2):
                project(("ob", i), ob_parts)
            for i in range(2):
                project(("out", i), m_parts)
            for i in range(2):
                for t in range(TT):
                    unit_taken(pe, ("out", i), t)
            keep_clock(24)
            for i in range(4):
                pe.wait_ge(x2n_done, i // 2 + 1)
                transposed(("x2T", i), [h2[:, i // 2, k * P:(k + 1) * P] for k in range(4 * (i % 2), 4 * (i % 2) + 4)])
            for i in range(4):
                mix_taken(pe, ("x2T", i))
            pe.wait_ge(s_wr, 64)
            bank = begin("router")
            for t in range(TT):
                for k in range(KD):
                    ins = mm(bank[:, t * 36:(t + 1) * 36], hT[:, k, t * P:(t + 1) * P], wr[:, k], k == 0, k == KD - 1)
            ins.then_inc(full("router"), 1)
            keep_clock(24)
            pe.wait_ge(mask_ok, 1)
            bank = begin("pos")
            mm(bank[:, 0:E], earlier[:], mask[:, 0])
            mm(bank[:, E:2 * E], earlier[:], mask[:, 1], True, False)
            mm(bank[:, E:2 * E], ones[:], mask[:, 0], False, True)
            mm(bank[:, 2 * E:3 * E], ones[:], mask[:, 0], True, False)
            mm(bank[:, 2 * E:3 * E], ones[:], mask[:, 1], False, True).then_inc(full("pos"), 1)
            mix_taken(pe, ("x2T", 3))
            for i in range(2):
                for t in range(TT):
                    unit_taken(pe, ("out", i), t)

            def gather(onehots, w, sel):
                for k in range(KD):
                    for t in range(TT):
                        for n_, part in enumerate(h2_parts):
                            ins = mm(ps[6 + k // 4][:, (k % 4) * w:(k % 4 + 1) * w], part[:, t, k * P:(k + 1) * P],
                                     onehots[:, t], t == 0 and n_ == 0, t == TT - 1 and n_ == 1)
                ins.then_inc(sel, 1)

            def up(s, bank, rows_, done):
                for m in range(4):
                    for k in range(KD):
                        ins = mm(bank[:, m * W:(m + 1) * W], ring[:, 2 * s + m // 2, k, (m % 2) * P:(m % 2 + 1) * P], rows_[:, k], k == 0,
                                 k == KD - 1)
                ins.then_inc(done, 1)

            def down(product, w2, hidden_, banks, done):
                for n in range(2):
                    for f in range(2):
                        ins = product(banks[n][0:W, :], [v[:, f * W:(f + 1) * W] for v in hidden_],
                                      [v[:, f, n * 512:(n + 1) * 512] for v in w2], f == 0, f == 1)
                ins.then_inc(done, 1)

            def select(i, d):
                wait_turn(pe, pick_ok, i, d)
                wait_turn(pe, sel_taken, i, d - 1)
                gather(pickS[:, d % 2], 2 * W, sel_full[d % 2])

            def up_of(i, c_):
                rows_ = hsel[:, (c_ // 2) % 2, :, c_ % 2]
                wait_turn(pe, sel_taken, i, c_ // 2)
                wait_item(pe, up_taken, i, c_ - 1)
                for j in range(2):
                    wait_item(pe, w13_lo, i, 2 * c_ + j, 8)
                    hi, lo = w13_high[(2 * c_ + j) % 4], rounded["ring"][:, (2 * c_ + j) % 8]
                    cs = slice(j * HC, (j + 1) * HC)
                    for k in range(KD):
                        if k == KD - 1:
                            mm(ps[0][0:W, cs], rows_[:, k, 0], lo[:, k], False, False)
                        ins = mm(ps[0][:, cs], rows_[:, k].rearrange("p l r -> p (l r)"), hi[:, k], k == 0, k == KD - 1)
                        if k < KD - 1:
                            mm(ps[0][0:W, cs], rows_[:, k, 0], lo[:, k], False, False)
                ins.then_inc(up_full[c_ % 4], 1)

            def fold_of(i, c_):
                wait_item(pe, up_taken, i, c_)
                wait_item(pe, hid_mul, i, c_ - 1)
                for m in range(4):
                    ins = mm(ps[1][:, m * W:(m + 1) * W], up_sb[:, m * P:(m + 1) * P], fold[:])
                ins.then_inc(fold_full, 1)

            def down_of(i, c_):
                wait_item(pe, w2_lo, i, c_)
                wait_item(pe, hid_ok, i, c_)
                wait_turn(pe, y_lo, i, c_ - 2)
                wait_turn(pe, y_hi, i, c_ - 2)
                down(split_product, (w2_high[:, c_ % 2], w2_low[:, c_ % 2]),
                     [v[:, c_ % 2] for v in hid_parts], ps[2 + 2 * (c_ % 2):4 + 2 * (c_ % 2)], down_full[c_ % 4])

            def four_experts(i, last=False):
                for c_ in range(4):
                    left = 3 - c_ if last else 4
                    if c_ % 2 == 0 and left >= 2:
                        select(i, c_ // 2 + 1)
                    if left >= 1:
                        up_of(i, c_ + 1)
                    down_of(i, c_)
                    if left >= 1:
                        fold_of(i, c_ + 1)

            pe.wait_ge(h2_lo, TT)
            select(0, 0)
            pe.wait_ge(fold_ok, 1)
            up_of(0, 0)
            fold_of(0, 0)
            four_experts(0)
            with pe.Fori(1, E // 4 - 1) as i:
                four_experts(i)
            four_experts(E // 4 - 1, last=True)
            pe.wait_ge(jobs_ok, 1)
            extra = pe.value_load(jobs_i[0:1, JOBS:JOBS + 1], min_val=0, max_val=JOBS)
            with pe.If(extra > 0):
                with pe.Fori(1, extra + 1) as j:
                    pe.wait_ge(x_pick, j)
                    gather(pickS[:, 0, :, 0], W, x_sel)
                    pe.wait_ge(x_taken, j)
                    pe.wait_ge(x_loaded, j * 48)
                    up(0, ps[0], x_rows, x_up)
                    pe.wait_ge(x_hid, j)
                    down(lambda o, l, r, start, stop: mm(o, l[0], r[0], start, stop), (w2_slot[:, 0],), (hid,), ps[2:4],
                         x_down)


_INS = ["x", "c", "ada_w", "ada_b", "norm1_g", "w_in", "gla_w_gk2", "gla_b_gk", "gla_norm_g", "conv_w", "conv_b",
        "dt_bias", "a_log", "d_skip", "ssm_norm_g", "w_oa", "w_ob", "w_out", "norm2_g", "router_group_w",
        "router_group_b", "router_expert_w", "router_expert_b", "expert_w1", "expert_w3", "expert_w2", "final_norm_g"]


def kernel(**inputs):
    import concourse.bacc as bacc
    import numpy as np
    from concourse.bass_utils import run_bass_kernel_spmd

    nc = bacc.Bacc("TRN2", target_bir_lowering=False, num_devices=1)
    arrays, args = {}, []
    for name in _INS:
        a = np.ascontiguousarray(inputs[name])
        arrays[f"in_{name}"] = a
        args.append(nc.dram_tensor(f"in_{name}", a.shape, mybir.dt.from_np(a.dtype), kind="ExternalInput").ap())
    out = nc.dram_tensor("out", inputs["x"].shape, F32, kind="ExternalOutput").ap()
    trunk(nc, *args, out)
    r = run_bass_kernel_spmd(nc, [arrays], core_ids=[0])
    return r.results[0]["out"]
```
